# Optimizing a Trainium2 kernel written in Bass

```python
import math
import jax, jax.numpy as jnp
from jax import lax
import numpy as np

D_MODEL = 1024
BATCH = 1
SEQ = 512
DEPTH = 1

HEAD_DIM = 64
N_MIX_HEADS = D_MODEL // HEAD_DIM
FOX_HEADS = N_MIX_HEADS // 2
NSA_HEADS = N_MIX_HEADS - FOX_HEADS
NSA_GQA = 4
NSA_KV_GROUPS = NSA_HEADS // NSA_GQA
Q_BLOCK = 128
SEL_Q_CHUNK = 64
CMP_BLOCK = 32
CMP_STRIDE = 16
CMP_HIDDEN = 256
SEL_BLOCK = 64
N_SEL = 16
WINDOW = 512
N_BUCKETS = 32
MAX_DISTANCE = 128
N_EXPERTS = 64
N_EXPERT_GROUPS = 8
TOPK_GROUPS = 4
TOP_K = 8
D_EXPERT = 256
D_SHARED = 256
ROUTED_SCALE = 2.5
LN_EPS = 1e-5
NEG_BIG = -1e30
FORCE_SCORE = 1e4
DEEPNORM_ALPHA = (2 * DEPTH) ** 0.25
DEEPNORM_BETA = (8 * DEPTH) ** -0.25

FOX_W = FOX_HEADS * HEAD_DIM
NSA_W = NSA_HEADS * HEAD_DIM
KV_W = NSA_KV_GROUPS * HEAD_DIM
IN_WIDTHS = (FOX_W, FOX_W, FOX_W, FOX_HEADS, NSA_W, KV_W, KV_W, KV_W, KV_W, KV_W, KV_W, 3 * NSA_HEADS)
IN_IS_VALUE = (False, False, True, False, False, False, True, False, True, False, True, False)
D_IN_PROJ = sum(IN_WIDTHS)

kernel_name = 'fox_nsa_moe_deepnorm_adaln_hybrid'

def layer_norm(x, g, b):
    xf = x.astype(jnp.float32)
    mu = jnp.mean(xf, axis=-1, keepdims=True)
    var = jnp.mean(jnp.square(xf - mu), axis=-1, keepdims=True)
    y = (xf - mu) * lax.rsqrt(var + LN_EPS)
    return (y * g.astype(jnp.float32) + b.astype(jnp.float32)).astype(x.dtype)

def t5_bucket(dist):
    n = jnp.maximum(dist, 0)
    max_exact = N_BUCKETS // 2
    nf = jnp.maximum(n, 1).astype(jnp.float32)
    large = max_exact + (jnp.log(nf / max_exact) / math.log(MAX_DISTANCE / max_exact)
                         * (N_BUCKETS - max_exact)).astype(jnp.int32)
    large = jnp.minimum(large, N_BUCKETS - 1)
    return jnp.where(n < max_exact, n, large)

def forgetting_attention(q, k, v, log_f):
    B, S, H, Dh = q.shape
    scale = Dh ** -0.5
    cum = jnp.cumsum(log_f, axis=1).transpose(0, 2, 1)
    outs = []
    for i in range(S // Q_BLOCK):
        q0, kend = i * Q_BLOCK, (i + 1) * Q_BLOCK
        logits = jnp.einsum('bqhd,bkhd->bhqk', q[:, q0:kend], k[:, :kend]).astype(jnp.float32) * scale
        decay = cum[:, :, q0:kend, None] - cum[:, :, None, :kend]
        qpos = q0 + jnp.arange(Q_BLOCK)
        mask = jnp.arange(kend)[None, :] <= qpos[:, None]
        logits = jnp.where(mask, logits + decay, -jnp.inf)
        p = jax.nn.softmax(logits, axis=-1)
        outs.append(jnp.einsum('bhqk,bkhd->bqhd', p.astype(v.dtype), v[:, :kend]))
    return jnp.concatenate(outs, axis=1)

def compress_blocks(x, blk_idx, pos, w1, w2):
    B, G = x.shape[0], x.shape[2]
    n_cmp = blk_idx.shape[0]
    xb = x[:, blk_idx] + pos[None, None, :, None, :]
    flat = xb.transpose(0, 1, 3, 2, 4).reshape(B, n_cmp, G, CMP_BLOCK * HEAD_DIM)
    return jax.nn.silu(flat @ w1) @ w2

def nsa_attention(q, k_cmp, v_cmp, k_sel, v_sel, k_win, v_win, gate_logits, rel_bias,
                  cmp_pos_k, cmp_w1_k, cmp_w2_k, cmp_pos_v, cmp_w1_v, cmp_w2_v):
    B, S = q.shape[0], q.shape[1]
    G, R, Dh = NSA_KV_GROUPS, NSA_GQA, HEAD_DIM
    scale = Dh ** -0.5
    qg = q.reshape(B, S, G, R, Dh)
    t = jnp.arange(S)

    n_cmp = (S - CMP_BLOCK) // CMP_STRIDE + 1
    blk_idx = np.arange(n_cmp)[:, None] * CMP_STRIDE + np.arange(CMP_BLOCK)[None, :]
    blk_end = jnp.asarray(blk_idx[:, -1])
    kc = compress_blocks(k_cmp, blk_idx, cmp_pos_k, cmp_w1_k, cmp_w2_k)
    vc = compress_blocks(v_cmp, blk_idx, cmp_pos_v, cmp_w1_v, cmp_w2_v)
    dist_c = t[:, None] - blk_end[None, :]
    bias_c = rel_bias[t5_bucket(dist_c)].reshape(S, n_cmp, G, R).transpose(2, 3, 0, 1)
    valid_c = dist_c >= 0
    logits_c = jnp.einsum('bsgrd,bngd->bgrsn', qg, kc).astype(jnp.float32) * scale
    logits_c = jnp.where(valid_c, logits_c + bias_c, NEG_BIG)
    p_c = jax.nn.softmax(logits_c, axis=-1) * valid_c
    o_c = jnp.einsum('bgrsn,bngd->bsgrd', p_c.astype(vc.dtype), vc)

    n_slc = S // SEL_BLOCK
    n_sel = min(N_SEL, n_slc)
    cs = np.arange(n_cmp)[:, None] * CMP_STRIDE
    sj = np.arange(n_slc)[None, :] * SEL_BLOCK
    overlap = ((cs < sj + SEL_BLOCK) & (cs + CMP_BLOCK > sj)).astype(np.float32)
    imp = jnp.einsum('bgrsn,nj->bgsj', p_c, jnp.asarray(overlap))
    q_blk = t // SEL_BLOCK
    j = jnp.arange(n_slc)
    forced = (j[None, :] == 0) | (j[None, :] == q_blk[:, None]) | (j[None, :] == q_blk[:, None] - 1)
    causal_blk = j[None, :] <= q_blk[:, None]
    sel_score = jnp.where(causal_blk, imp + FORCE_SCORE * forced, -FORCE_SCORE)
    _, sel_idx = lax.top_k(sel_score, n_sel)

    kT = k_sel.transpose(0, 2, 1, 3)
    vT = v_sel.transpose(0, 2, 1, 3)
    tbl = rel_bias.reshape(N_BUCKETS, G, R).transpose(1, 0, 2)
    b_ix = jnp.arange(B)[:, None, None, None]
    g_ix = jnp.arange(G)[None, :, None, None]
    n_chunks = S // SEL_Q_CHUNK
    n_tok = n_sel * SEL_BLOCK

    def sel_chunk(args):
        qc, ic, start = args
        tq = start + jnp.arange(SEL_Q_CHUNK)
        pos = (ic[..., None] * SEL_BLOCK + jnp.arange(SEL_BLOCK)).reshape(B, G, SEL_Q_CHUNK, n_tok)
        kg = kT[b_ix, g_ix, pos]
        vg = vT[b_ix, g_ix, pos]
        dist = tq[None, None, :, None] - pos
        bias = tbl[g_ix, t5_bucket(dist)]
        logits = jnp.einsum('bqgrd,bgqtd->bgrqt', qc, kg).astype(jnp.float32) * scale
        logits = jnp.where((dist >= 0)[:, :, None], logits + jnp.moveaxis(bias, -1, 2), -jnp.inf)
        p = jax.nn.softmax(logits, axis=-1)
        return jnp.einsum('bgrqt,bgqtd->bqgrd', p.astype(vg.dtype), vg)

    q_chunks = jnp.moveaxis(qg.reshape(B, n_chunks, SEL_Q_CHUNK, G, R, Dh), 1, 0)
    i_chunks = jnp.moveaxis(sel_idx.reshape(B, G, n_chunks, SEL_Q_CHUNK, n_sel), 2, 0)
    starts = jnp.arange(n_chunks) * SEL_Q_CHUNK
    o_s = lax.map(sel_chunk, (q_chunks, i_chunks, starts))
    o_s = jnp.moveaxis(o_s, 0, 1).reshape(B, S, G, R, Dh)

    nb = S // Q_BLOCK
    span = WINDOW + Q_BLOCK
    kp = jnp.pad(k_win, ((0, 0), (WINDOW, 0), (0, 0), (0, 0)))
    vp = jnp.pad(v_win, ((0, 0), (WINDOW, 0), (0, 0), (0, 0)))
    widx = np.arange(nb)[:, None] * Q_BLOCK + np.arange(span)[None, :]
    kw = kp[:, widx]
    vw = vp[:, widx]
    qw = qg.reshape(B, nb, Q_BLOCK, G, R, Dh)
    dist_w = np.arange(Q_BLOCK)[:, None] - np.arange(span)[None, :] + WINDOW
    key_pos = widx - WINDOW
    valid_w = ((dist_w >= 0) & (dist_w < WINDOW))[None] & (key_pos >= 0)[:, None, :]
    bias_w = rel_bias[t5_bucket(jnp.asarray(dist_w))].reshape(Q_BLOCK, span, G, R).transpose(2, 3, 0, 1)
    logits_w = jnp.einsum('bnqgrd,bnkgd->bngrqk', qw, kw).astype(jnp.float32) * scale
    logits_w = jnp.where(jnp.asarray(valid_w)[None, :, None, None], logits_w + bias_w, -jnp.inf)
    p_w = jax.nn.softmax(logits_w, axis=-1)
    o_w = jnp.einsum('bngrqk,bnkgd->bnqgrd', p_w.astype(vw.dtype), vw).reshape(B, S, G, R, Dh)

    gates = jax.nn.sigmoid(gate_logits.astype(jnp.float32)).reshape(B, S, G, R, 3).astype(q.dtype)
    o = gates[..., 0:1] * o_c + gates[..., 1:2] * o_s + gates[..., 2:3] * o_w
    return o.reshape(B, S, NSA_HEADS * Dh)

def moe_ffn(h, w_router, e_bias, w_gate, w_up, w_down, ws_gate, ws_up, ws_down):
    B, S, D = h.shape
    scores = jax.nn.sigmoid(jnp.einsum('bsd,de->bse', h, w_router).astype(jnp.float32))
    biased = scores + e_bias.astype(jnp.float32)
    grouped = biased.reshape(B, S, N_EXPERT_GROUPS, N_EXPERTS // N_EXPERT_GROUPS)
    group_score = lax.top_k(grouped, 2)[0].sum(-1)
    _, gidx = lax.top_k(group_score, TOPK_GROUPS)
    gmask = jax.nn.one_hot(gidx, N_EXPERT_GROUPS).sum(-2) > 0
    masked = jnp.where(gmask[..., None], grouped, -jnp.inf).reshape(B, S, N_EXPERTS)
    _, eidx = lax.top_k(masked, TOP_K)
    w = jnp.take_along_axis(scores, eidx, axis=-1)
    w = w / jnp.sum(w, axis=-1, keepdims=True) * ROUTED_SCALE
    gates = jnp.sum(jax.nn.one_hot(eidx, N_EXPERTS, dtype=jnp.float32) * w[..., None], axis=-2)

    def per_seq(args):
        xs, gs = args
        a = jnp.einsum('sd,edf->sef', xs, w_gate)
        u = jnp.einsum('sd,edf->sef', xs, w_up)
        act = jax.nn.silu(a) * u * gs[..., None].astype(xs.dtype)
        return jnp.einsum('sef,efd->sd', act, w_down)

    routed = lax.map(per_seq, (h, gates))
    shared = (jax.nn.silu(h @ ws_gate) * (h @ ws_up)) @ ws_down
    return routed + shared

def setup_inputs(seed: int = 0) -> dict:
    key = jax.random.key(seed)
    ks = jax.random.split(key, 32)
    f32 = jnp.float32

    def nrm(k, shape, scale):
        return jax.random.normal(k, shape, f32) * scale

    D = D_MODEL
    in_keys = jax.random.split(ks[4], len(IN_WIDTHS))
    w_in = jnp.concatenate(
        [nrm(kk, (DEPTH, D, wd), D ** -0.5 * (DEEPNORM_BETA if isv else 1.0))
         for kk, wd, isv in zip(in_keys, IN_WIDTHS, IN_IS_VALUE)], axis=-1)
    return {
        'x': nrm(ks[0], (BATCH, SEQ, D), 1.0),
        'c': nrm(ks[1], (BATCH, D), 1.0),
        'w_ada': nrm(ks[2], (DEPTH, D, 6 * D), D ** -0.5),
        'b_ada': nrm(ks[3], (DEPTH, 6 * D), 0.02),
        'w_in': w_in,
        'b_f': 3.0 + nrm(ks[5], (DEPTH, FOX_HEADS), 0.5),
        'cmp_pos_k': nrm(ks[6], (DEPTH, CMP_BLOCK, HEAD_DIM), 0.1),
        'cmp_w1_k': nrm(ks[7], (DEPTH, CMP_BLOCK * HEAD_DIM, CMP_HIDDEN), (CMP_BLOCK * HEAD_DIM) ** -0.5),
        'cmp_w2_k': nrm(ks[8], (DEPTH, CMP_HIDDEN, HEAD_DIM), CMP_HIDDEN ** -0.5),
        'cmp_pos_v': nrm(ks[9], (DEPTH, CMP_BLOCK, HEAD_DIM), 0.1),
        'cmp_w1_v': nrm(ks[10], (DEPTH, CMP_BLOCK * HEAD_DIM, CMP_HIDDEN), (CMP_BLOCK * HEAD_DIM) ** -0.5),
        'cmp_w2_v': nrm(ks[11], (DEPTH, CMP_HIDDEN, HEAD_DIM), CMP_HIDDEN ** -0.5),
        'rel_bias': nrm(ks[12], (N_BUCKETS, NSA_HEADS), 0.5),
        'w_out': nrm(ks[13], (DEPTH, D, D), D ** -0.5 * DEEPNORM_BETA),
        'ln1_g': 1.0 + nrm(ks[14], (DEPTH, D), 0.05),
        'ln1_b': nrm(ks[15], (DEPTH, D), 0.02),
        'w_router': nrm(ks[16], (DEPTH, D, N_EXPERTS), D ** -0.5),
        'e_bias': nrm(ks[17], (DEPTH, N_EXPERTS), 0.01),
        'w_gate': nrm(ks[18], (DEPTH, N_EXPERTS, D, D_EXPERT), D ** -0.5),
        'w_up': nrm(ks[19], (DEPTH, N_EXPERTS, D, D_EXPERT), D ** -0.5),
        'w_down': nrm(ks[20], (DEPTH, N_EXPERTS, D_EXPERT, D), D_EXPERT ** -0.5 * DEEPNORM_BETA),
        'ws_gate': nrm(ks[21], (DEPTH, D, D_SHARED), D ** -0.5),
        'ws_up': nrm(ks[22], (DEPTH, D, D_SHARED), D ** -0.5),
        'ws_down': nrm(ks[23], (DEPTH, D_SHARED, D), D_SHARED ** -0.5 * DEEPNORM_BETA),
        'ln2_g': 1.0 + nrm(ks[24], (DEPTH, D), 0.05),
        'ln2_b': nrm(ks[25], (DEPTH, D), 0.02),
    }

def reference(x, c, w_ada, b_ada, w_in, b_f, cmp_pos_k, cmp_w1_k, cmp_w2_k, cmp_pos_v, cmp_w1_v,
              cmp_w2_v, rel_bias, w_out, ln1_g, ln1_b, w_router, e_bias, w_gate, w_up, w_down,
              ws_gate, ws_up, ws_down, ln2_g, ln2_b):
    B, S, D = x.shape
    split_pts = [int(v) for v in np.cumsum(IN_WIDTHS)[:-1]]
    kv_shape = (B, S, NSA_KV_GROUPS, HEAD_DIM)
    for l in range(DEPTH):
        mod = jnp.einsum('bd,de->be', jax.nn.silu(c), w_ada[l]) + b_ada[l]
        sh1, sc1, g1, sh2, sc2, g2 = jnp.split(mod[:, None, :], 6, axis=-1)

        h = x * (1.0 + sc1) + sh1
        fq, fk, fv, ff, nq, kc, vc, ksl, vsl, kwn, vwn, ng = jnp.split(h @ w_in[l], split_pts, axis=-1)
        log_f = jax.nn.log_sigmoid(ff.astype(jnp.float32) + b_f[l].astype(jnp.float32))
        o_fox = forgetting_attention(fq.reshape(B, S, FOX_HEADS, HEAD_DIM),
                                     fk.reshape(B, S, FOX_HEADS, HEAD_DIM),
                                     fv.reshape(B, S, FOX_HEADS, HEAD_DIM), log_f)
        o_nsa = nsa_attention(nq.reshape(B, S, NSA_HEADS, HEAD_DIM),
                              kc.reshape(kv_shape), vc.reshape(kv_shape),
                              ksl.reshape(kv_shape), vsl.reshape(kv_shape),
                              kwn.reshape(kv_shape), vwn.reshape(kv_shape), ng, rel_bias,
                              cmp_pos_k[l], cmp_w1_k[l], cmp_w2_k[l],
                              cmp_pos_v[l], cmp_w1_v[l], cmp_w2_v[l])
        mixed = jnp.concatenate([o_fox.reshape(B, S, FOX_W), o_nsa], axis=-1) @ w_out[l]
        x = layer_norm(DEEPNORM_ALPHA * x + g1 * mixed, ln1_g[l], ln1_b[l])

        h = x * (1.0 + sc2) + sh2
        ffn = moe_ffn(h, w_router[l], e_bias[l], w_gate[l], w_up[l], w_down[l],
                      ws_gate[l], ws_up[l], ws_down[l])
        x = layer_norm(DEEPNORM_ALPHA * x + g2 * ffn, ln2_g[l], ln2_b[l])
    return x


_drawn_inputs = setup_inputs


def setup_inputs(seed=0):
    import zlib

    import numpy as np

    out = dict(_drawn_inputs(seed))
    spreads = {}
    factors = {'cmp_pos_k': 27.102, 'ln2_b': 2.811}
    for name, (base, spread) in spreads.items():
        noise = np.random.default_rng([zlib.crc32(name.encode()), seed]).standard_normal(out[name].shape)
        drawn = base * np.exp(spread * noise) if base else spread * noise
        out[name] = __import__('jax').numpy.asarray(drawn.astype(out[name].dtype))
    for name, factor in factors.items():
        out[name] = (out[name] * factor).astype(out[name].dtype)
    return out
```

```python
from contextlib import ExitStack

import concourse.bass as bass
from concourse import mybir

F32 = mybir.dt.float32
BF16 = mybir.dt.bfloat16
I32 = mybir.dt.int32
U32 = mybir.dt.uint32
ALU = mybir.AluOpType
ACT = mybir.ActivationFunctionType
AX = mybir.AxisListType.X

P = 128
S = 512
D = 1024
DH = 64
H = 8
R = 4
G = 2
TT = S // P
KD = D // P
NCMP = (S - 32) // 16 + 1
NB = 32
CMPH = 256
E = 64
EG = 8
F = 256
SCALE = DH ** -0.5
ALPHA = 2.0 ** 0.25
EPS = 1e-5
NEG = -1e30
ROUTED_SCALE = 2.5
TOPK_GROUPS = 4
SLOTS = 128
UNITS = 100
TOP_K = 8
SLOT_BITS = 7
DOWN_BITS = 11
OUT_OF_RANGE = 1024.0
DIST0 = S - 1
NDIST = DIST0 + S - NCMP
CW = 512
WS_SMALL = 288
RING = 4
WS_SLOT = 2
LEAD = 2

CHUNKS = ([("ada", c) for c in range(4)] + [("in", c) for c in range(5)] + [("small", 0)]
          + [("cmp", 0), ("cmp", 1)] + [("ada", c) for c in range(4, 12)]
          + [("out", 0), ("out", 1), ("shared", 0)])
AT = {c: i for i, c in enumerate(CHUNKS)}

TASKS = ([("fox", h, t) for h in range(H) for t in range(TT)]
         + [(kind, h, t) for h in range(H) for t in range(TT) for kind in ("sel", "win")])
NT = len(TASKS)
FIRST_NSA = H * TT


def build(nc, a, out):
    with ExitStack() as ctx:
        def sb(name, shape, dt=F32):
            return ctx.enter_context(nc.sbuf_tensor(name, shape, dt))

        def sem(name):
            return ctx.enter_context(nc.semaphore(name))

        h2_dram = nc.dram_tensor("h2_rows", [S, D], F32, kind="Internal")
        ffn_dram = [nc.dram_tensor(f"ffn_rows{i}", [S, D], F32, kind="Internal") for i in range(2)]

        bank = [ctx.enter_context(nc.psum_tensor(f"bank{i}", [P, 512], F32)) for i in range(8)]

        ring = sb("ring", [P, RING, KD * CW])
        down = sb("down", [P, RING, 2 * D])
        area_a = sb("area_a", [P, KD * S])
        area_c = sb("area_c", [P, TT * D])
        area_d = sb("area_d", [P, TT * D])
        area_e = sb("area_e", [P, 4096])
        area_f = sb("area_f", [P, 3072])
        area_g = sb("area_g", [P, 3072])
        mod_rows = sb("mod_rows", [P, 4, D])

        h1T = area_a[:, :].rearrange("p (k t) -> p k t", k=KD)
        oT = h1T
        h2T = h1T
        fqT = area_d[:, 0:2048].rearrange("p (i t) -> p i t", i=4)
        fkT = area_d[:, 2048:4096].rearrange("p (i t) -> p i t", i=4)
        x_tok = area_d[:, :].rearrange("p (t d) -> p t d", t=TT)
        nqT = area_e[:, 0:2048].rearrange("p (i t) -> p i t", i=4)
        kvT = area_e[:, 2048:4096].rearrange("p (i t) -> p i t", i=4)
        fv = area_f[:, 0:2048].rearrange("p (t d) -> p t d", t=TT)
        vsw = area_f[:, 2048:3072].rearrange("p (t d) -> p t d", t=TT)
        bias_w = area_g[:, 0:2048].rearrange("p (h j) -> p h j", h=H)
        bias_c = area_g[:, 2048:3072].rearrange("p (t h n) -> p t h n", t=TT, h=H)
        o_tok = area_c[:, :].rearrange("p (t d) -> p t d", t=TT)
        h2_tok = o_tok
        ffn_tok = [o_tok, area_a[:, :].rearrange("p (t d) -> p t d", t=TT)]
        silu_c_row = down[:, 2, 0:1024].rearrange("p (k m) -> p k m", k=KD)
        tri = down[:, 2, 1024:1536]
        hid = down[:, 2, 1536:1784]
        hid_e = down[:, 2, 1784:2032]
        pair = [down[:, 0, i * 1024:(i + 1) * 1024].rearrange("p (g t) -> p g t", g=G) for i in range(2)]
        xb = [down[:, 1, i * 1024:i * 1024 + 16 * 62] for i in range(2)]
        fox_parts = area_a[0:3, 0:2048].bitcast(BF16).rearrange("p (h t) -> p h t", h=H)
        vc_diag = area_a[:, 2048:2560].rearrange("p (g d) -> p g d", g=G)
        fox_sum = area_a[0:H, 2560:3072]
        fox_rest = area_a[0:H, 3072:3584]
        fox_split = area_a[0:H, 3584:4096].bitcast(BF16)
        fox_lo = area_a[0:H, 2560:2816].bitcast(BF16)
        p_cmp = down[:, 3, :].rearrange("p (g f) -> p g f", g=4)
        p_buf = [down[:, 3, i * 512:(i + 1) * 512] for i in range(2)]
        pT_buf = [down[:, 3, 1024 + i * 512:1536 + i * 512] for i in range(2)]
        ln_rows = area_e[:, :].rearrange("p (i d) -> p i d", i=4)
        ln_tmp = area_g[:, 2048:3072]
        sh_act = area_f[:, 0:TT * F].rearrange("p (t f) -> p t f", t=TT)
        sh_sil = area_f[:, 1024:1536].rearrange("p (i f) -> p i f", i=2)
        sh_actT = area_f[:, 1536:2048].rearrange("p (i f) -> p i f", i=2)
        sh_y = area_g[:, 0:2048].rearrange("p (i f) -> p i f", i=2)
        r_score = area_c[:, 0:256].rearrange("p (t e) -> p t e", t=TT)
        r_bias = area_c[:, 256:512].rearrange("p (t e) -> p t e", t=TT)
        r_top = area_c[:, 512:768].rearrange("p (t g e) -> p t g e", t=TT, g=EG)
        r_gt = area_c[:, 768:1024].rearrange("p (t g e) -> p t g e", t=TT, g=EG)
        r_eq = area_c[:, 1024:1280].rearrange("p (t g e) -> p t g e", t=TT, g=EG)
        r_group = area_c[:, 1280:1312].rearrange("p (t g) -> p t g", t=TT)
        r_rank = area_c[:, 1312:1344].rearrange("p (t g) -> p t g", t=TT)
        r_gmask = area_c[:, 1344:1376].rearrange("p (t g) -> p t g", t=TT)
        r_masked = area_c[:, 1376:1632].rearrange("p (t e) -> p t e", t=TT)
        r_best = area_c[:, 1632:1664].rearrange("p (t e) -> p t e", t=TT)
        r_sel = area_c[:, 1664:1920].rearrange("p (t e) -> p t e", t=TT)
        r_gate = area_c[:, 1920:2176].rearrange("p (t e) -> p t e", t=TT)
        r_den = area_c[:, 2176:2180]
        r_selb = area_c[:, 2184:2312].bitcast(BF16).rearrange("p (t e) -> p t e", t=TT)
        pos_m = area_c[:, 2312:2568].rearrange("p (t e) -> p t e", t=TT)
        r_kidx = area_c[:, 2568:2824].rearrange("p (t e) -> p t e", t=TT)
        r_pick = [area_c[:, 2824 + 256 * i:3080 + 256 * i].rearrange("p (t e) -> p t e", t=TT) for i in range(2)]
        slot_k = area_c[:, 3336:3368].rearrange("p (t k) -> p t k", t=TT)
        gate_k = area_c[:, 3368:3400].rearrange("p (t k) -> p t k", t=TT)
        slot_ki = area_c[:, 3400:3432].bitcast(I32).rearrange("p (t k) -> p t k", t=TT)
        unit_ki = area_c[:, 3432:3464].bitcast(I32).rearrange("p (t k) -> p t k", t=TT)
        unit_k = area_c[:, 3464:3496].rearrange("p (t k) -> p t k", t=TT)
        gate_parts = area_c[:, 3496:3592].rearrange("p (i t k) -> p i t k", i=3, t=TT)
        slot_hot = area_c[:, 3592:3848].bitcast(BF16).rearrange("p (b s) -> p b s", b=4)
        part_b = area_c[:, 3848:3864].bitcast(BF16).rearrange("p (t k) -> p t k", t=TT)
        n_units = area_c[:, 3864:3928]
        unit_end = area_c[:, 3928:3992]
        zeros_e = area_c[:, 3992:4056]
        expert_u = area_c[:, 4056:4060]

        ident = sb("ident", [P, P])
        ident_b = sb("ident_b", [P, P], BF16)
        ones_b = sb("ones_b", [P, P], BF16)
        causal_b = sb("causal_b", [P, P], BF16)
        before_b = sb("before_b", [P, P], BF16)
        iota_b = sb("iota_b", [P, SLOTS], BF16)
        row_no = sb("row_no", [P, 1])
        table_b = sb("table_b", [P, NDIST + 1], BF16)
        rel_parts = sb("rel_parts", [P, H], BF16)
        c_col = sb("c_col", [P, KD])
        sc_col = sb("sc_col", [P, 3, KD])
        ada_b_col = sb("ada_b_col", [P, 16])
        mod_col = sb("mod_col", [P, 16])
        bf_row = sb("bf_row", [P, H])
        ffng = sb("ffng", [P, TT, 32])
        gates = sb("gates", [P, TT, 24])
        fx = sb("fx", [P, 3, TT, H])
        pos2 = sb("pos2", [P, 2, 16])
        w2 = sb("w2", [P, 2, 2, DH])
        kcT = sb("kcT", [P, 32])
        nmax = sb("nmax", [P, 4])
        rowsum = sb("rowsum", [P, 4])
        early = sb("early", [P, 2])
        coef = sb("coef", [P, 4])
        c_stat = sb("c_stat", [P, 3, 16])
        ln_stats = sb("ln_stats", [P, 12])
        ln_mv = sb("ln_mv", [P, 2])
        ln_r = sb("ln_r", [P, 2])
        e_bias_row = sb("e_bias_row", [P, E])
        slot_idx = mod_rows[:, 1, 0:UNITS].bitcast(U32)
        slot_gate = mod_rows[:, 1, 128:128 + UNITS]
        idx_gather = [sb(f"idx_gather{i}", [P, 1], U32) for i in range(2)]
        idx_scatter = [sb(f"idx_scatter{i}", [P, 1], U32) for i in range(2)]
        unit_at = area_f[0:1, 2944:3072].bitcast(I32)
        unit_expert = area_f[0:1, 2816:2944].bitcast(I32)
        expert_end = mod_rows[0:1, 1, 256:256 + E + 2].bitcast(I32)
        w_router_t = area_f[:, 2048:2560].rearrange("p (k e) -> p k e", k=KD)
        gathered = [area_e[:, i * 1024:(i + 1) * 1024] for i in range(2)]
        gatheredT = [area_f[:, i * 1024:(i + 1) * 1024].rearrange("p (k m) -> p k m", k=KD) for i in range(2)]
        ring_flat = ring[:, :, :].rearrange("p s n -> p (s n)")
        down_flat = down[:, :, :].rearrange("p s n -> p (s n)")
        y_out = [area_g[:, i * 1024:(i + 1) * 1024] for i in range(2)]
        silu_g = area_f[:, 2048:2304]
        e_act = area_f[:, 2304:2560]
        e_actT = area_f[:, 2560:2816].rearrange("p (i f) -> p i f", i=2)
        unit_hot = area_g[:, 2048:3048].bitcast(BF16).rearrange("p (b n) -> p b n", b=4)
        list_sum = area_e[:, 0:5 * UNITS]

        slot_in = [sem(f"slot_in{s}") for s in range(RING)]
        down_in = [sem(f"down_in{s}") for s in range(RING)]
        chunk_used = sem("chunk_used")
        xT_in = sem("xT_in")
        consts_in = sem("consts_in")
        table_in = sem("table_in")
        modb_in = sem("modb_in")
        masks_set = sem("masks_set")
        ident_set = sem("ident_set")
        passed = sem("passed")
        rel_set = sem("rel_set")
        bias_mm = sem("bias_mm")
        bias_out = sem("bias_out")
        c_exp = sem("c_exp")
        c_ready = sem("c_ready")
        c_row_ready = sem("c_row_ready")
        mod_mm = sem("mod_mm")
        mod_ready = sem("mod_ready")
        h1_ready = sem("h1_ready")
        job_mm = sem("job_mm")
        job_act = sem("job_act")
        job_dve = sem("job_dve")
        ffng_act = sem("ffng_act")
        fx_ready = sem("fx_ready")
        cum_mm = sem("cum_mm")
        parts_ready = sem("parts_ready")
        parts_in = sem("parts_in")
        pair_in = [sem("pair_in_k"), sem("pair_in_v")]
        xb_ready = sem("xb_ready")
        hid_mm = sem("hid_mm")
        hid_exp = sem("hid_exp")
        hid_ready = sem("hid_ready")
        kc_mm = sem("kc_mm")
        kc_ready = sem("kc_ready")
        cmp_qk = sem("cmp_qk")
        cmp_max = sem("cmp_max")
        cmp_exp = sem("cmp_exp")
        cmp_p = sem("cmp_p")
        cmp_tr = sem("cmp_tr")
        cmp_pT = sem("cmp_pT")
        cmp_pv = sem("cmp_pv")
        cmp_o = sem("cmp_o")
        qk_done = sem("qk_done")
        max_done = sem("max_done")
        exp_done = sem("exp_done")
        tr_done = sem("tr_done")
        pT_act = sem("pT_act")
        pT_dve = sem("pT_dve")
        pv_done = sem("pv_done")
        o_done = sem("o_done")
        x_in = sem("x_in")
        ln_in = sem("ln_in")
        oT_mm = sem("oT_mm")
        oT_act = sem("oT_act")
        oT_dve = sem("oT_dve")
        mix_mm = sem("mix_mm")
        mix_read = sem("mix_read")
        var_ready = sem("var_ready")
        rstd_ready = sem("rstd_ready")
        x1_ready = sem("x1_ready")
        h2_ready = sem("h2_ready")
        h2_stored = sem("h2_stored")
        h2T_mm = sem("h2T_mm")
        h2T_act = sem("h2T_act")
        router_mm = sem("router_mm")
        router_exp = sem("router_exp")
        router_in = sem("router_in")
        sel_ready = sem("sel_ready")
        pos_mm = sem("pos_mm")
        units_ready = sem("units_ready")
        units_row = sem("units_row")
        hot_ready = sem("hot_ready")
        list_mm = sem("list_mm")
        lists_ready = sem("lists_ready")
        tables_ready = sem("tables_ready")
        weights_ready = sem("weights_ready")
        sh_gu = sem("sh_gu")
        sh_silu = sem("sh_silu")
        sh_act_ready = sem("sh_act_ready")
        sh_tr = sem("sh_tr")
        sh_actT_ready = sem("sh_actT_ready")
        sh_down = sem("sh_down")
        sh_y_ready = sem("sh_y_ready")
        ffn_started = [sem(f"ffn_started{i}") for i in range(2)]
        cleared = sem("cleared")
        idx_set = sem("idx_set")
        idx_out = sem("idx_out")
        gather_in = [sem(f"gather_in{i}") for i in range(2)]
        xe_tr = sem("xe_tr")
        xe_act = sem("xe_act")
        xe_dve = sem("xe_dve")
        gu_done = sem("gu_done")
        silu_done = sem("silu_done")
        act_done = sem("act_done")
        at_tr = sem("at_tr")
        at_ready = sem("at_ready")
        down_done = sem("down_done")
        y_act = sem("y_act")
        y_dve = sem("y_dve")
        scattered = [sem(f"scattered{i}") for i in range(2)]
        ffn_in = [sem(f"ffn_in{t}") for t in range(TT)]
        x2_ready = sem("x2_ready")
        stored = sem("stored")
        dve_step = sem("dve_step")
        act_step = sem("act_step")
        pool_step = sem("pool_step")

        block = ctx.enter_context(nc.Block())

        NJ = 32
        owner = ["act" if j % 2 == 0 and j < 24 else "dve" for j in range(NJ)]

        def copied(j):
            o = owner[j]
            return (job_act if o == "act" else job_dve), sum(owner[i] == o for i in range(j + 1))

        def settle(eng):
            eng.sem_inc(passed, 1)

        def chunks_before(slot):
            return sum(i % RING == slot for i in range(len(CHUNKS)))

        def pT_ready(t):
            if t < FIRST_NSA:
                return pT_dve, t + 1
            return pT_act, t - FIRST_NSA + 1

        @block.sync
        def _(sp):
            def load_chunk(i):
                kind, c = CHUNKS[i]
                if i >= RING:
                    sp.wait_ge(chunk_used, i - RING + 1)
                if kind == "small":
                    sp.dma_start(ring[:, i % RING, 0:KD * WS_SMALL], a["w_small"]).then_inc(slot_in[i % RING], 16)
                else:
                    src = {"ada": a["w_ada"], "in": a["w_in"], "cmp": a["w_cmp1"], "out": a["w_out"],
                           "shared": a["ws_gu"]}[kind]
                    sp.dma_start(ring[:, i % RING, :], src[c]).then_inc(slot_in[i % RING], 16)

            for i in range(len(CHUNKS)):
                load_chunk(i)
            def slot_of(u):
                return (len(CHUNKS) + u) % RING

            def landed(e, i, u):
                s = slot_of(u)
                sp.wait_ge(slot_in[s], 16 * (i + chunks_before(s) + 1))
                settle(sp)
                sp.wait_ge(down_in[s], 16 * (i + (1 if s == WS_SLOT else 0) + 1))
                sp.sem_inc(weights_ready, 1)

            for u in range(RING):
                s = slot_of(u)
                sp.wait_ge(chunk_used, len(CHUNKS) + u - RING + 1)
                sp.dma_start(ring[:, s, :], a["w_gu"][u]).then_inc(slot_in[s], 16)
                if u == 0:
                    sp.wait_ge(o_done, NT)
                    sp.dma_start(down[:, WS_SLOT, :], a["ws_d"]).then_inc(down_in[WS_SLOT], 16)
                if s == WS_SLOT:
                    sp.wait_ge(sh_down, TT)
                sp.dma_start(down[:, s, :], a["w_d"][u]).then_inc(down_in[s], 16)
                if u >= LEAD:
                    landed(u - LEAD, 0, u - LEAD)
            sp.wait_ge(tables_ready, 1)
            with sp.Fori(1, E // RING) as i:
                for u in range(RING):
                    s = slot_of(u)
                    e = i * RING + u
                    units = sp.value_load(expert_end[0:1, bass.ds(e - RING, 1)], min_val=1, max_val=UNITS)
                    sp.wait_ge(gu_done, units)
                    settle(sp)
                    sp.dma_start(ring[:, s, :], a["w_gu"][bass.ds(e, 1)].rearrange("o p n -> p (o n)"))\
                        .then_inc(slot_in[s], 16)
                    sp.wait_ge(down_done, units)
                    settle(sp)
                    sp.dma_start(down[:, s, :], a["w_d"][bass.ds(e, 1)].rearrange("o p n -> p (o n)"))\
                        .then_inc(down_in[s], 16)
                    landed(e - LEAD, i if u >= LEAD else i - 1, (u - LEAD) % RING)
            for u in range(RING - LEAD, RING):
                landed(E - RING + u, E // RING - 1, u)

        @block.scalar
        def _(act):
            steps = [0]

            def link(ins):
                steps[0] += 1
                ins.then_inc(act_step, 1)
                act.wait_ge(act_step, steps[0])

            act.dma_start(c_col[:, :], a["c_col"]).then_inc(consts_in, 16)
            act.dma_start(ada_b_col[:, :], a["ada_b_col"]).then_inc(consts_in, 16)
            act.dma_start(area_a[:, :], a["xT"]).then_inc(xT_in, 16)
            act.dma_start(bf_row[:, :], a["b_f"].to_broadcast([P, H])).then_inc(consts_in, 16)
            act.dma_start(pos2[:, :, :], a["cmp_pos"]).then_inc(consts_in, 16)
            act.dma_start(w2[:, :, :, :], a["w_cmp2"]).then_inc(consts_in, 16)
            act.dma_start(e_bias_row[:, :], a["e_bias"].to_broadcast([P, E])).then_inc(consts_in, 16)
            act.dma_start(mod_rows[:, :, :].rearrange("p i d -> p (i d)"),
                          a["ada_b_row"].to_broadcast([P, 4 * D])).then_inc(modb_in, 16)

            act.wait_ge(consts_in, 96)
            nc.scalar.activation(sc_col[:, 0, :], c_col[:, :], ACT.Exp, scale=-1.0).then_inc(c_exp, 1)

            for j in range(0, 24, 2):
                act.wait_ge(job_mm, j + 1)
                if j < 16:
                    i = j % 4
                    dst = [fqT, fkT, nqT, kvT][j // 4][:, i, :]
                    nc.scalar.activation(dst, bank[j % 4][:, :], ACT.Copy,
                                         scale=SCALE if j // 4 in (0, 2) else 1.0).then_inc(job_act, 1)
                elif j < 20:
                    nc.scalar.activation(fv[:, j - 16, :], bank[j % 4][:, :], ACT.Copy).then_inc(job_act, 1)
                else:
                    t = j - 20
                    nc.scalar.activation(ffng[:, t, :], bank[j % 4][:, 256:288], ACT.Copy).then_inc(ffng_act, 1)
                    nc.scalar.activation(vsw[:, t, :], bank[j % 4][:, 0:256], ACT.Copy).then_inc(job_act, 1)

            act.wait_ge(ffng_act, TT)
            nc.scalar.activation(gates[:, :, :], ffng[:, :, H:32], ACT.Exp, scale=-1.0).then_inc(fx_ready, 1)
            act.wait_ge(fx_ready, 2)
            link(nc.scalar.activation(fx[:, 1, :, :], fx[:, 1, :, :], ACT.Exp, scale=-1.0))
            nc.scalar.activation(fx[:, 1, :, :], fx[:, 1, :, :], ACT.Ln, bias=1.0).then_inc(fx_ready, 1)

            act.wait_ge(hid_mm, 2)
            nc.scalar.activation(hid_e, bank[4][:, 0:248], ACT.Exp, scale=-1.0).then_inc(hid_exp, 1)

            for g in range(G):
                act.wait_ge(cmp_max, g + 1)
                nc.scalar.activation(p_cmp[:, g, :], p_cmp[:, g, :], ACT.Exp).then_inc(cmp_exp, 1)
            for g in range(G):
                act.wait_ge(cmp_tr, g + 1)
                nc.scalar.activation(p_cmp[:, 2 + g, :], bank[6 + g][:, :], ACT.Copy).then_inc(cmp_pT, 1)

            def exp_task(t):
                kind, h, qt = TASKS[t]
                n = P * (qt + 1)
                act.wait_ge(max_done, t + 1)
                if t == 0:
                    act.wait_ge(cmp_pv, 2)
                if t >= 2:
                    act.wait_ge(tr_done, t - 1)
                if t >= 4:
                    act.wait_ge(o_done, t - 3)
                nc.scalar.activation(p_buf[t % 2][:, 0:n], bank[t % 3][:, 0:n], ACT.Exp,
                                     bias=nmax[:, t % 4:t % 4 + 1],
                                     accum_out=rowsum[:, t % 4:t % 4 + 1]).then_inc(exp_done, 1)

            def copy_pT(t):
                n = P * (TASKS[t][2] + 1)
                act.wait_ge(tr_done, t + 1)
                if t >= 2:
                    act.wait_ge(pv_done, t - 1)
                nc.scalar.activation(pT_buf[t % 2][:, 0:n], bank[3 + t % 2][:, 0:n], ACT.Copy).then_inc(pT_act, 1)

            for t in range(NT + 1):
                if t < NT:
                    exp_task(t)
                if t >= 1 and t - 1 >= FIRST_NSA:
                    copy_pT(t - 1)

            act.wait_ge(qk_done, NT)
            act.dma_start(area_d[:, :].rearrange("p (t d) -> p t d", t=TT), a["x_tok"]).then_inc(x_in, 16)
            act.dma_start(ln_rows[:, :, :].rearrange("p i d -> p (i d)"), a["ln_rows"].to_broadcast([P, 4 * D])).then_inc(ln_in, 16)

            act.wait_ge(o_done, NT)
            act.dma_start(w_router_t, a["w_router"]).then_inc(router_in, 16)

            for k in range(0, KD, 2):
                act.wait_ge(oT_mm, k + 1)
                nc.scalar.activation(oT[:, k, :], bank[k % 4][:, :], ACT.Copy).then_inc(oT_act, 1)

            def rstd(n):
                act.wait_ge(var_ready, n)
                link(nc.scalar.activation(ln_r[:, 0:1], ln_r[:, 0:1], ACT.Ln))
                nc.scalar.activation(ln_r[:, 1:2], ln_r[:, 0:1], ACT.Exp, scale=-0.5).then_inc(rstd_ready, 1)

            for t in range(TT):
                rstd(t + 1)
                for half in range(2):
                    act.wait_ge(h2T_mm, 2 * t + half + 1)
                    nc.scalar.activation(h2T[:, 4 * half:4 * half + 4, t * P:(t + 1) * P],
                                         bank[4 + half][:, :].rearrange("p (k m) -> p k m", k=4),
                                         ACT.Copy).then_inc(h2T_act, 1)
            act.wait_ge(router_mm, 1)
            act.wait_ge(h2_stored, 16 * TT)
            nc.scalar.activation(r_score, bank[6][:, 0:256].rearrange("p (t e) -> p t e", t=TT),
                                 ACT.Exp, scale=-1.0).then_inc(router_exp, 1)

            for t in range(TT):
                act.wait_ge(sh_gu, t + 1)
                if t >= 2:
                    act.wait_ge(sh_act_ready, t - 1)
                nc.scalar.activation(sh_sil[:, t % 2, :], bank[t % 2][:, 0:F], ACT.Silu).then_inc(sh_silu, 1)
            for t in range(TT):
                act.wait_ge(sh_tr, t + 1)
                if t >= 1:
                    act.wait_ge(sh_down, t)
                nc.scalar.activation(sh_actT[:, :, 0:P], bank[2][:, 0:F].rearrange("p (i f) -> p i f", i=2),
                                     ACT.Copy).then_inc(sh_actT_ready, 1)
                act.wait_ge(sh_down, t + 1)
                if t >= 2:
                    act.wait_ge(ffn_started[t % 2], 16 * (t // 2))
                nc.scalar.activation(sh_y[:, t % 2, 0:512], bank[4][:, :], ACT.Copy).then_inc(sh_y_ready, 1)
                nc.scalar.activation(sh_y[:, t % 2, 512:1024], bank[5][:, :], ACT.Copy).then_inc(sh_y_ready, 1)
                act.wait_ge(sh_y_ready, 2 * t + 2)
                act.dma_start(ffn_dram[0][t * P:(t + 1) * P, :], sh_y[:, t % 2, :]).then_inc(ffn_started[t % 2], 16)

            def silu(n):
                act.wait_ge(gu_done, n + 1)
                nc.scalar.activation(silu_g, bank[0][:, 0:F], ACT.Silu).then_inc(silu_done, 1)

            def copy_xT(n, u):
                act.wait_ge(xe_tr, n + 1)
                nc.scalar.activation(gatheredT[u % 2][:, 0:4, :], bank[1][:, :].rearrange("p (k m) -> p k m", k=4),
                                     ACT.Copy).then_inc(xe_act, 1)

            def copy_y(n, u, i):
                act.wait_ge(down_done, n + 1)
                if isinstance(i, int) and i == 0:
                    for stored_rows in ffn_started:
                        act.wait_ge(stored_rows, 8 * TT)
                else:
                    act.wait_ge(scattered[u], 16 * (i + u))
                nc.scalar.activation(y_out[u][:, 0:512], bank[4][:, :], ACT.Copy).then_inc(y_act, 1)

            copy_xT(0, 0)
            silu(0)
            copy_xT(1, 1)
            silu(1)
            copy_xT(2, 0)
            copy_y(0, 0, 0)
            act.wait_ge(tables_ready, 1)
            pairs = act.value_load(expert_end[0:1, E:E + 1], min_val=E // 2, max_val=UNITS // 2 - 1)
            with act.Fori(1, pairs) as i:
                silu(2 * i)
                copy_xT(2 * i + 1, 1)
                copy_y(2 * i - 1, 1, i - 1)
                silu(2 * i + 1)
                copy_xT(2 * i + 2, 0)
                copy_y(2 * i, 0, i)
            last = 2 * pairs - 1
            copy_y(last, 1, pairs - 1)

            for t in range(TT):
                rstd(TT + t + 1)

        @block.tensor
        def _(pe):
            pe.wait_ge(table_in, 80)
            pe.wait_ge(rel_set, 1)
            for b in range(4):
                for i in range(64):
                    j = 64 * b + i
                    first = DIST0 + P - j
                    last = nc.tensor.matmul(bank[b][:, 8 * i:8 * i + 8], table_b[0:97, first:first + P],
                                            rel_parts[0:97, :], start=True, stop=True)
                last.then_inc(bias_mm, 1)
            for t in range(TT):
                for n in range(NCMP):
                    first = DIST0 + P * t - 16 * n - 31
                    last = nc.tensor.matmul(bank[4 + t][:, 8 * n:8 * n + 8], table_b[0:97, first:first + P],
                                            rel_parts[0:97, :], start=True, stop=True)
                last.then_inc(bias_mm, 1)

            pe.wait_ge(c_ready, 1)
            pe.wait_ge(bias_out, 1)
            for i in range(4):
                pe.wait_ge(slot_in[i], 16)
                w = ring[:, i, :].rearrange("p (k n) -> p k n", k=KD)
                for m in range(4):
                    for k in range(KD):
                        last = nc.tensor.matmul(bank[0][:, 4 * i + m:4 * i + m + 1], w[:, k, m * P:(m + 1) * P],
                                                sc_col[:, 2, k:k + 1], start=(k == 0), stop=(k == KD - 1))
                last.then_inc(chunk_used, 1)
            pe.wait_ge(mod_ready, 1)
            pe.wait_ge(h1_ready, 1)
            pe.wait_ge(bias_out, 4)

            def arrived(i):
                pe.wait_ge(slot_in[i % RING], 16 * (i // RING + 1))

            def free_bank(j):
                if j >= 4:
                    pe.wait_ge(*copied(j - 4))

            for c in range(4):
                i = AT["in", c]
                arrived(i)
                w = ring[:, i % RING, :].rearrange("p (k n) -> p k n", k=KD)
                for m in range(4):
                    j = 4 * c + m
                    free_bank(j)
                    for k in range(KD):
                        last = nc.tensor.matmul(bank[j % 4][:, :], w[:, k, m * P:(m + 1) * P], h1T[:, k, :],
                                                start=(k == 0), stop=(k == KD - 1))
                    last.then_inc(job_mm, 1)
                pe.wait_ge(job_mm, 4 * c + 4)
                nc.tensor.nop().then_inc(chunk_used, 1)
            for c, width in ((AT["in", 4], CW), (AT["small", 0], WS_SMALL)):
                arrived(c)
                w = ring[:, c % RING, 0:KD * width].rearrange("p (k n) -> p k n", k=KD)
                for t in range(TT):
                    j = (16 if width == CW else 20) + t
                    free_bank(j)
                    for k in range(KD):
                        last = nc.tensor.matmul(bank[j % 4][:, 0:width], h1T[:, k, t * P:(t + 1) * P], w[:, k, :],
                                                start=(k == 0), stop=(k == KD - 1))
                    last.then_inc(job_mm, 1)
                pe.wait_ge(job_mm, j + 1)
                nc.tensor.nop().then_inc(chunk_used, 1)

            for s in range(2):
                i = AT["cmp", s]
                arrived(i)
                pe.wait_ge(xb_ready, s + 1)
                if s == 0:
                    pe.wait_ge(bias_out, 8)
                w = ring[:, i % RING, :].rearrange("p (k n) -> p k n", k=16)
                x = xb[s].rearrange("p (j n) -> p j n", j=16)
                for hh in range(2):
                    for jj in range(16):
                        last = nc.tensor.matmul(bank[4][:, 124 * s + 62 * hh:124 * s + 62 * hh + 62],
                                                w[:, jj, hh * P:(hh + 1) * P], x[:, jj, :],
                                                start=(jj == 0), stop=(jj == 15))
                last.then_inc(hid_mm, 1)
                pe.wait_ge(hid_mm, s + 1)
                nc.tensor.nop().then_inc(chunk_used, 1)

            pe.wait_ge(fx_ready, 4)
            pe.wait_ge(masks_set, 1)
            for kt in range(TT):
                last = nc.tensor.matmul(bank[5][0:H, kt * P:S], fx[:, 2, kt, :], tri[:, 0:S - kt * P],
                                        start=(kt == 0), stop=(kt == TT - 1))
            last.then_inc(cum_mm, 1)

            def ada_row(c):
                i = AT["ada", 4 + c]
                j = 24 + c
                arrived(i)
                free_bank(j)
                w = ring[:, i % RING, :].rearrange("p (k n) -> p k n", k=KD)
                for k in range(KD):
                    last = nc.tensor.matmul(bank[j % 4][:, :], silu_c_row[:, k, :], w[:, k, :],
                                            start=(k == 0), stop=(k == KD - 1))
                last.then_inc(job_mm, 1)
                pe.wait_ge(job_mm, j + 1)
                nc.tensor.nop().then_inc(chunk_used, 1)

            pe.wait_ge(c_row_ready, 1)
            for c in range(2):
                ada_row(c)

            pe.wait_ge(hid_ready, 1)
            hv = hid.rearrange("p (s f g n) -> p s f g n", s=2, f=2, g=G)
            for g in range(G):
                for f in range(2):
                    nc.tensor.matmul(bank[6][g * DH:(g + 1) * DH, 0:NCMP], w2[:, 0, f, :], hv[:, 0, f, g, :],
                                     start=(f == 0), stop=(f == 1))
            for r in range(R):
                for g in range(G):
                    for f in range(2):
                        last = nc.tensor.matmul(bank[7][32 * r:32 * r + NCMP, g * DH:(g + 1) * DH],
                                                hv[:, 1, f, g, :], w2[:, 1, f, :],
                                                start=(f == 0), stop=(f == 1))
            last.then_inc(kc_mm, 1)
            for c in range(2, 4):
                ada_row(c)
            pe.wait_ge(kc_ready, 1)
            for qt in range(TT):
                for r in range(R):
                    for g in range(G):
                        last = nc.tensor.matmul(bank[6 + g][:, (qt * R + r) * 32:(qt * R + r) * 32 + NCMP],
                                                nqT[g * DH:(g + 1) * DH, r, qt * P:(qt + 1) * P],
                                                kcT[g * DH:(g + 1) * DH, 0:NCMP], start=True, stop=True)
            last.then_inc(cmp_qk, 1)
            for c in range(4, 8):
                ada_row(c)
            for g in range(G):
                pe.wait_ge(cmp_p, g + 1)
                if g == 0:
                    pe.wait_ge(ident_set, 2)
                for qt in range(TT):
                    last = nc.tensor.transpose(bank[6 + g][:, qt * P:(qt + 1) * P], p_cmp[:, g, qt * P:(qt + 1) * P],
                                               ident[:, :])
                last.then_inc(cmp_tr, 1)
            for g in range(G):
                pe.wait_ge(cmp_pT, g + 1)
                if g == 0:
                    for j in range(28, 32):
                        pe.wait_ge(*copied(j))
                for qt in range(TT):
                    last = nc.tensor.matmul(bank[2 * g + qt // 2][:, (qt % 2) * 256:(qt % 2) * 256 + 256],
                                            p_cmp[:, 2 + g, qt * P:(qt + 1) * P], vc_diag[:, g, :],
                                            start=True, stop=True)
                last.then_inc(cmp_pv, 1)

            pe.wait_ge(parts_in, 48)

            def qk(t):
                kind, h, qt = TASKS[t]
                n = P * (qt + 1)
                if t >= 3:
                    pe.wait_ge(exp_done, t - 2)
                if t == 0:
                    pe.wait_ge(cmp_o, 2)
                dst = bank[t % 3]
                if kind == "fox":
                    lo = DH * (h % 2)
                    nc.tensor.matmul(dst[:, 0:n], fqT[lo:lo + DH, h // 2, qt * P:(qt + 1) * P],
                                     fkT[lo:lo + DH, h // 2, 0:n], start=True, stop=False)
                    nc.tensor.matmul(dst[:, n - P:n], ident_b[:, :], causal_b[:, :], start=False, stop=False)
                    nc.tensor.matmul(dst[:, 0:n], ones_b[0:3, :], fox_parts[:, h, 0:n],
                                     start=False, stop=True).then_inc(qk_done, 1)
                else:
                    g, r = h // R, h % R
                    lo = DH * g
                    nc.tensor.matmul(dst[:, 0:n], nqT[lo:lo + DH, r, qt * P:(qt + 1) * P],
                                     kvT[lo:lo + DH, 0 if kind == "sel" else 1, 0:n],
                                     start=True, stop=True).then_inc(qk_done, 1)

            def transposes(t):
                qt = TASKS[t][2]
                pe.wait_ge(exp_done, t + 1)
                if t >= 2:
                    pe.wait_ge(*pT_ready(t - 2))
                for kt in range(qt + 1):
                    last = nc.tensor.transpose(bank[3 + t % 2][:, kt * P:(kt + 1) * P],
                                               p_buf[t % 2][:, kt * P:(kt + 1) * P], ident[:, :])
                last.then_inc(tr_done, 1)

            def pv(t):
                kind, h, qt = TASKS[t]
                pe.wait_ge(*pT_ready(t))
                if t >= 2:
                    pe.wait_ge(o_done, t - 1)
                for kt in range(qt + 1):
                    if kind == "fox":
                        v = fv[:, kt, h * DH:(h + 1) * DH]
                    else:
                        at = (0 if kind == "sel" else 128) + DH * (h // R)
                        v = vsw[:, kt, at:at + DH]
                    last = nc.tensor.matmul(bank[5 + t % 2][:, 0:DH], pT_buf[t % 2][:, kt * P:(kt + 1) * P], v,
                                            start=(kt == 0), stop=(kt == qt))
                last.then_inc(pv_done, 1)

            for t in range(NT + 3):
                if t < NT:
                    qk(t)
                if 2 <= t < NT + 2:
                    transposes(t - 2)
                if t >= 3:
                    pv(t - 3)

            pe.wait_ge(o_done, NT)
            for k in range(KD):
                if k >= 4:
                    pe.wait_ge(oT_act if k % 2 == 0 else oT_dve, (k - 4) // 2 + 1)
                for t in range(TT):
                    last = nc.tensor.transpose(bank[k % 4][:, t * P:(t + 1) * P], o_tok[:, t, k * P:(k + 1) * P],
                                               ident[:, :])
                last.then_inc(oT_mm, 1)
            pe.wait_ge(oT_act, KD // 2)
            pe.wait_ge(oT_dve, KD // 2)

            def h2_tile(t):
                pe.wait_ge(h2_ready, t + 1)
                for half in range(2):
                    if t >= 1:
                        pe.wait_ge(h2T_act, 2 * (t - 1) + half + 1)
                    for k in range(4):
                        last = nc.tensor.transpose(bank[4 + half][:, k * P:(k + 1) * P],
                                                   h2_tok[:, t, (4 * half + k) * P:(4 * half + k + 1) * P], ident[:, :])
                    last.then_inc(h2T_mm, 1)

            for t in range(TT):
                for c in range(2):
                    i = AT["out", c]
                    arrived(i)
                    w = ring[:, i % RING, :].rearrange("p (k n) -> p k n", k=KD)
                    if t >= 2:
                        pe.wait_ge(mix_read, 2 * (t - 2) + c + 1)
                    for k in range(KD):
                        last = nc.tensor.matmul(bank[2 * (t % 2) + c][:, :], oT[:, k, t * P:(t + 1) * P], w[:, k, :],
                                                start=(k == 0), stop=(k == KD - 1))
                    last.then_inc(mix_mm, 1)
            pe.wait_ge(mix_mm, 2 * TT)
            nc.tensor.nop().then_inc(chunk_used, 2)
            for t in range(TT):
                h2_tile(t)
            pe.wait_ge(router_in, 16)
            pe.wait_ge(h2T_act, 2 * TT)
            for t in range(TT):
                for k in range(KD):
                    last = nc.tensor.matmul(bank[6][:, t * E:(t + 1) * E], h2T[:, k, t * P:(t + 1) * P],
                                            w_router_t[:, k, :], start=(k == 0), stop=(k == KD - 1))
            last.then_inc(router_mm, 1)

            def positions():
                pe.wait_ge(sel_ready, 1)
                pe.wait_ge(router_exp, 1)
                for t in range(TT):
                    for s in range(t):
                        nc.tensor.matmul(bank[7][:, t * E:(t + 1) * E], ones_b[:, :], r_selb[:, s, :],
                                         start=(s == 0), stop=False)
                    nc.tensor.matmul(bank[7][:, t * E:(t + 1) * E], before_b[:, :], r_selb[:, t, :],
                                     start=(t == 0), stop=True)
                for s in range(TT):
                    last = nc.tensor.matmul(bank[7][:, TT * E:(TT + 1) * E], ones_b[:, :], r_selb[:, s, :],
                                            start=(s == 0), stop=(s == TT - 1))
                last.then_inc(pos_mm, 1)

            i = AT["shared", 0]
            arrived(i)
            pe.wait_ge(mix_read, 2 * TT)
            w = ring[:, i % RING, :].rearrange("p (k n) -> p k n", k=KD)
            for t in range(TT):
                if t == 2:
                    positions()
                if t >= 2:
                    pe.wait_ge(sh_act_ready, t - 1)
                for k in range(KD):
                    last = nc.tensor.matmul(bank[t % 2][:, :], h2T[:, k, t * P:(t + 1) * P], w[:, k, :],
                                            start=(k == 0), stop=(k == KD - 1))
                last.then_inc(sh_gu, 1)
            pe.wait_ge(sh_gu, TT)
            nc.tensor.nop().then_inc(chunk_used, 1)
            pe.wait_ge(down_in[WS_SLOT], 16)
            wd = down[:, WS_SLOT, :].rearrange("p (f n) -> p f n", f=2)
            for t in range(TT):
                pe.wait_ge(sh_act_ready, t + 1)
                if t >= 1:
                    pe.wait_ge(sh_actT_ready, t)
                for f in range(2):
                    last = nc.tensor.transpose(bank[2][:, f * P:(f + 1) * P], sh_act[:, t, f * P:(f + 1) * P], ident[:, :])
                last.then_inc(sh_tr, 1)
                pe.wait_ge(sh_actT_ready, t + 1)
                if t >= 1:
                    pe.wait_ge(sh_y_ready, 2 * t)
                for c in range(2):
                    for f in range(2):
                        last = nc.tensor.matmul(bank[4 + c][:, :], sh_actT[:, f, 0:P], wd[:, f, c * 512:(c + 1) * 512],
                                                start=(f == 0), stop=(f == 1))
                last.then_inc(sh_down, 1)
                if t == 0:
                    pe.wait_ge(units_ready, 1)
                    nc.tensor.matmul(bank[7][0:1, 320:448], expert_u[:, 0:1], ident[:, :],
                                     start=True, stop=True).then_inc(units_row, 1)
                for k in range(TOP_K):
                    j = TOP_K * t + k
                    pe.wait_ge(hot_ready, j + 1)
                    nc.tensor.matmul(bank[6][:, 0:5 * UNITS], slot_hot[:, j % 4, :], unit_hot[:, j % 4, :],
                                     start=(j == 0), stop=(j == TT * TOP_K - 1)).then_inc(list_mm, 1)

            xe_banks = (bank[1], bank[2])

            def tokensT(n, u, i):
                pe.wait_ge(gather_in[u], 16 * (i + 1))
                for half in range(2):
                    for k in range(4):
                        last = nc.tensor.transpose(xe_banks[half][:, k * P:(k + 1) * P],
                                                   gathered[u][:, (4 * half + k) * P:(4 * half + k + 1) * P],
                                                   ident[:, :])
                last.then_inc(xe_tr, 1)

            def gate_up(n, u):
                expert = pe.value_load(unit_expert[0:1, bass.ds(n, 1)], min_val=0, max_val=E - 1)
                at = pe.value_load(unit_at[0:1, bass.ds(n, 1)], min_val=0, max_val=(RING - 1) * 2 * D)
                pe.wait_ge(weights_ready, expert + 1)
                pe.wait_ge(xe_act, n + 1)
                pe.wait_ge(xe_dve, n + 1)
                settle(pe)
                for k in range(KD):
                    last = nc.tensor.matmul(bank[0][:, :], gatheredT[u][:, k, :],
                                            ring_flat[:, bass.ds(at * 2 + k * 2 * F, 2 * F)],
                                            start=(k == 0), stop=(k == KD - 1))
                last.then_inc(gu_done, 1)

            def act_T(n):
                pe.wait_ge(act_done, n + 1)
                for f in range(2):
                    last = nc.tensor.transpose(bank[3][:, f * P:(f + 1) * P], e_act[:, f * P:(f + 1) * P], ident[:, :])
                last.then_inc(at_tr, 1)

            def down_mm(n, used):
                at = pe.value_load(unit_at[0:1, bass.ds(n, 1)], min_val=0, max_val=(RING - 1) * 2 * D)
                pe.wait_ge(at_ready, n + 1)
                if used:
                    pe.wait_ge(y_act, n)
                    pe.wait_ge(y_dve, n)
                settle(pe)
                for c in range(2):
                    for f in range(2):
                        last = nc.tensor.matmul(bank[4 + c][:, :], e_actT[:, f, :],
                                                down_flat[:, bass.ds(at + f * D + c * 512, 512)],
                                                start=(f == 0), stop=(f == 1))
                last.then_inc(down_done, 1)

            pe.wait_ge(tables_ready, 1)
            tokensT(0, 0, 0)
            gate_up(0, 0)
            tokensT(1, 1, 0)
            act_T(0)
            gate_up(1, 1)
            tokensT(2, 0, 1)
            pe.wait_ge(sh_y_ready, 2 * TT)
            down_mm(0, False)
            act_T(1)
            pairs = pe.value_load(expert_end[0:1, E:E + 1], min_val=E // 2, max_val=UNITS // 2 - 1)
            with pe.Fori(1, pairs) as i:
                gate_up(2 * i, 0)
                tokensT(2 * i + 1, 1, i)
                down_mm(2 * i - 1, True)
                act_T(2 * i)
                gate_up(2 * i + 1, 1)
                tokensT(2 * i + 2, 0, i + 1)
                down_mm(2 * i, True)
                act_T(2 * i + 1)
            down_mm(pe.value_load(expert_end[0:1, E + 1:E + 2], min_val=E - 1, max_val=UNITS - 1), True)

        @block.gpsimd
        def _(pool):
            steps = [0]

            def link(ins):
                steps[0] += 1
                ins.then_inc(pool_step, 1)
                pool.wait_ge(pool_step, steps[0])

            pool.dma_start(table_b[0:97, 0:NDIST], a["buckets"]).then_inc(table_in, 16)
            last_row = a["rel_bias"][NB - 1:NB, :]
            for q in range(3):
                pool.dma_start(c_stat[32 * q:32 * q + 32, 0, 0:H], a["rel_bias"]).then_inc(table_in, 16)
            pool.dma_start(c_stat[0:96, 1, 0:H], last_row.to_broadcast([96, H])).then_inc(table_in, 16)

            link(nc.gpsimd.memset(ident[:, :], 0.0))
            nc.gpsimd.affine_select(out=ident[:, :], in_=ident[:, :], compare_op=ALU.not_equal, fill=1.0, base=0,
                                    pattern=[[-1, P]], channel_multiplier=1).then_inc(ident_set, 1)
            link(nc.gpsimd.memset(ident_b[:, :], 0.0))
            nc.gpsimd.affine_select(out=ident_b[:, :], in_=ident_b[:, :], compare_op=ALU.not_equal, fill=1.0,
                                    base=0, pattern=[[-1, P]], channel_multiplier=1).then_inc(ident_set, 1)
            nc.gpsimd.memset(ones_b[:, :], 1.0)
            link(nc.gpsimd.memset(causal_b[:, :], 0.0))
            nc.gpsimd.affine_select(out=causal_b[:, :], in_=causal_b[:, :], compare_op=ALU.is_ge, fill=NEG, base=0,
                                    pattern=[[-1, P]], channel_multiplier=1)
            link(nc.gpsimd.memset(before_b[:, :], 0.0))
            nc.gpsimd.affine_select(out=before_b[:, :], in_=before_b[:, :], compare_op=ALU.is_ge, fill=1.0, base=0,
                                    pattern=[[-1, P]], channel_multiplier=1)
            nc.gpsimd.iota(row_no[:, :], pattern=[[0, 1]], base=0, channel_multiplier=1,
                           allow_small_or_imprecise_dtypes=True)
            nc.gpsimd.iota(iota_b[:, :], pattern=[[1, SLOTS]], base=0, channel_multiplier=0,
                           allow_small_or_imprecise_dtypes=True)
            link(nc.gpsimd.memset(tri, 1.0))
            link(nc.gpsimd.affine_select(out=tri, in_=tri, compare_op=ALU.is_ge, fill=0.0, base=0,
                                         pattern=[[1, S]], channel_multiplier=-1))
            nc.gpsimd.memset(p_cmp[:, 0:2, :], 0.0).then_inc(masks_set, 1)

            for s in range(2):
                j = 14 + s
                pool.wait_ge(*copied(j))
                for half in range(2):
                    for g in range(G):
                        n = S - half
                        pool.dma_start(pair[s][half * DH:(half + 1) * DH, g, 0:n],
                                       kvT[g * DH:(g + 1) * DH, 2 + s, half:S]).then_inc(pair_in[s], 16)

            for i, part in enumerate((fox_split[:, 0:S], fox_split[:, S:2 * S], fox_lo)):
                pool.wait_ge(parts_ready, i + 1)
                pool.dma_start(fox_parts[i:i + 1, :, :], part).then_inc(parts_in, 16)

            for t in range(TT):
                pool.wait_ge(x1_ready, t + 1)
                if t == 0:
                    pool.wait_ge(oT_mm, KD)
                link(nc.gpsimd.tensor_tensor(h2_tok[:, t, :], x_tok[:, t, :], mod_rows[:, 2, :], ALU.mult))
                nc.gpsimd.tensor_tensor(h2_tok[:, t, :], h2_tok[:, t, :], mod_rows[:, 1, :], ALU.add).then_inc(h2_ready, 1)
                pool.wait_ge(h2_ready, t + 1)
                pool.dma_start(h2_dram[t * P:(t + 1) * P, :], h2_tok[:, t, :]).then_inc(h2_stored, 16)

            pool.wait_ge(x1_ready, TT)
            nc.gpsimd.memset(area_e[:, 0:2048], 0.0).then_inc(cleared, 1)
            pool.wait_ge(cleared, 1)
            pool.dma_start(ffn_dram[1].rearrange("(p t) d -> p t d", p=P),
                           area_e[:, 0:1024].rearrange("p (o d) -> p o d", o=1).to_broadcast([P, TT, D]))\
                .then_inc(scattered[1], 16)
            pool.wait_ge(scattered[1], 16)
            pool.wait_ge(h2_stored, 16 * TT)
            last_token = pool.to_reg(S - 1)

            def gather(n, u):
                if not (isinstance(n, int) and n < 2):
                    pool.wait_ge(xe_tr, n - 1)
                    settle(pool)
                nc.gpsimd.tensor_copy(idx_gather[u][:, :], slot_idx[:, bass.ds(n, 1)]).then_inc(idx_set, 1)
                pool.wait_ge(idx_set, n + 1)
                settle(pool)
                pool.indirect_dma_start(gathered[u], None, h2_dram[:, :],
                                        bass.IndirectOffsetOnAxis(ap=idx_gather[u][:, :], axis=0),
                                        bounds_check=last_token, oob_is_err=False).then_inc(gather_in[u], 16)

            def scatter(n, u, i):
                pool.wait_ge(y_act, n + 1)
                pool.wait_ge(y_dve, n + 1)
                if not (isinstance(i, int) and i + u == 0):
                    pool.wait_ge(scattered[u], 16 * (i + u))
                settle(pool)
                nc.gpsimd.tensor_copy(idx_scatter[u][:, :], slot_idx[:, bass.ds(n, 1)]).then_inc(idx_out, 1)
                pool.wait_ge(idx_out, n + 1)
                settle(pool)
                pool.indirect_dma_start(ffn_dram[u][:, :],
                                        bass.IndirectOffsetOnAxis(ap=idx_scatter[u][:, :], axis=0),
                                        y_out[u], None, bounds_check=last_token, oob_is_err=False,
                                        compute_op=ALU.add).then_inc(scattered[u], 16)

            pool.wait_ge(lists_ready, 1)
            gather(0, 0)
            gather(1, 1)
            gather(2, 0)
            gather(3, 1)
            for stored_rows in ffn_started:
                pool.wait_ge(stored_rows, 8 * TT)
            scatter(0, 0, 0)
            pool.wait_ge(tables_ready, 1)
            pairs = pool.value_load(expert_end[0:1, E:E + 1], min_val=E // 2, max_val=UNITS // 2 - 1)
            with pool.Fori(1, pairs) as i:
                gather(2 * i + 2, 0)
                scatter(2 * i - 1, 1, i - 1)
                gather(2 * i + 3, 1)
                scatter(2 * i, 0, i)
            scatter(2 * pairs - 1, 1, pairs - 1)
            pool.wait_ge(gather_in[0], 16 * (pairs + 1))
            pool.wait_ge(gather_in[1], 16 * (pairs + 1))
            pool.wait_ge(scattered[0], 16 * pairs)
            pool.wait_ge(scattered[1], 16 * (pairs + 1))
            settle(pool)
            for t in range(TT):
                for i in range(2):
                    pool.dma_start(ffn_tok[i][:, t, :], ffn_dram[i][t * P:(t + 1) * P, :]).then_inc(ffn_in[t], 16)
            for t in range(TT):
                pool.wait_ge(x2_ready, t + 1)
                pool.dma_start(out[t * P:(t + 1) * P, :], x_tok[:, t, :]).then_inc(stored, 16)
            pool.wait_ge(stored, 16 * TT)

        @block.vector
        def _(dve):
            steps = [0]

            def link(ins):
                steps[0] += 1
                ins.then_inc(dve_step, 1)
                dve.wait_ge(dve_step, steps[0])

            v = nc.vector
            dve.wait_ge(table_in, 80)
            d0 = c_stat[0:96, 0, 0:H]
            d1 = c_stat[0:96, 1, 0:H]
            d2 = c_stat[0:96, 2, 0:H]
            hi = rel_parts[0:96, :]
            link(v.tensor_tensor(d0, d0, d1, ALU.subtract))
            link(v.tensor_copy(hi, d0))
            link(v.tensor_tensor(d1, d0, hi, ALU.subtract))
            link(v.tensor_copy(rel_parts[32:64, :], d1[32:64, :]))
            link(v.tensor_copy(rel_parts[64:96, :], d1[64:96, :]))
            link(v.tensor_tensor(d2[64:96, :], d1[64:96, :], rel_parts[64:96, :], ALU.subtract))
            link(v.tensor_copy(rel_parts[64:96, :], d2[64:96, :]))
            v.memset(rel_parts[96:97, :], NEG).then_inc(rel_set, 1)

            dve.wait_ge(c_exp, 1)
            link(v.tensor_scalar(sc_col[:, 0, :], sc_col[:, 0, :], 1.0, None, ALU.add))
            link(v.reciprocal(sc_col[:, 1, :], sc_col[:, 0, :]))
            v.tensor_tensor(sc_col[:, 2, :], c_col[:, :], sc_col[:, 1, :], ALU.mult).then_inc(c_ready, 1)
            dve.wait_ge(c_ready, 1)
            v.tensor_copy(silu_c_row, sc_col[:, 2, :].rearrange("p (k o) -> p k o", o=1).to_broadcast([P, KD, P]))\
                .then_inc(c_row_ready, 1)
            for b in range(4):
                dve.wait_ge(bias_mm, b + 1)
                v.tensor_copy(bias_w[:, :, 64 * b:64 * b + 64],
                              bank[b][:, :].rearrange("p (j h) -> p h j", h=H)).then_inc(bias_out, 1)
            for t in range(TT):
                dve.wait_ge(bias_mm, 4 + t + 1)
                v.tensor_copy(bias_c[:, t, :, 0:NCMP],
                              bank[4 + t][:, 0:8 * NCMP].rearrange("p (n h) -> p h n", h=H)).then_inc(bias_out, 1)

            dve.wait_ge(chunk_used, 4)
            link(v.tensor_tensor(mod_col[:, :], bank[0][:, 0:16], ada_b_col[:, :], ALU.add))
            v.tensor_scalar(mod_col[:, 8:16], mod_col[:, 8:16], 1.0, None, ALU.add).then_inc(mod_ready, 1)
            dve.wait_ge(mod_ready, 1)
            dve.wait_ge(xT_in, 16)
            for k in range(KD):
                last = v.tensor_scalar(h1T[:, k, :], h1T[:, k, :], mod_col[:, 8 + k:9 + k], mod_col[:, k:k + 1],
                                       ALU.mult, ALU.add)
            last.then_inc(h1_ready, 1)

            for j in range(1, 16, 2):
                dve.wait_ge(job_mm, j + 1)
                dst = [fqT, fkT, nqT, kvT][j // 4][:, j % 4, :]
                v.tensor_scalar(dst, bank[j % 4][:, :], SCALE if j // 4 in (0, 2) else 1.0, None, ALU.mult)\
                    .then_inc(job_dve, 1)

            def build_xb(s):
                dve.wait_ge(pair_in[s], 64)
                dst = xb[s].rearrange("p (j g n) -> p j g n", j=16, g=G)
                for g in range(G):
                    src = pair[s][:, g, :].rearrange("p (n j two) -> p j n two", j=8, two=2)
                    for part in range(2):
                        last = v.tensor_tensor(dst[:, 8 * part:8 * part + 8, g, :], src[:, :, part:part + NCMP, 0],
                                               pos2[:, s, 8 * part:8 * part + 8].rearrange("p (j o) -> p j o", o=1)
                                               .to_broadcast([P, 8, NCMP]), ALU.add)
                last.then_inc(xb_ready, 1)

            for j in range(17, 24, 2):
                dve.wait_ge(job_mm, j + 1)
                if j < 20:
                    v.tensor_copy(fv[:, j - 16, :], bank[j % 4][:, :]).then_inc(job_dve, 1)
                else:
                    v.tensor_copy(ffng[:, j - 20, :], bank[j % 4][:, 256:288]).then_inc(ffng_act, 1)
                    v.tensor_copy(vsw[:, j - 20, :], bank[j % 4][:, 0:256]).then_inc(job_dve, 1)
                if j == 17:
                    build_xb(0)
                if j == 19:
                    build_xb(1)

            dve.wait_ge(ffng_act, TT)
            link(v.tensor_tensor(fx[:, 0, :, :], ffng[:, :, 0:H],
                                 bf_row[:, :].rearrange("p (o h) -> p o h", o=1).to_broadcast([P, TT, H]), ALU.add))
            link(v.tensor_scalar(fx[:, 2, :, :], fx[:, 0, :, :], -1.0, 0.0, ALU.mult, ALU.max))
            v.scalar_tensor_tensor(fx[:, 1, :, :], fx[:, 2, :, :], 2.0, fx[:, 0, :, :], ALU.mult, ALU.add)\
                .then_inc(fx_ready, 1)
            dve.wait_ge(fx_ready, 3)
            v.tensor_tensor(fx[:, 2, :, :], fx[:, 2, :, :], fx[:, 1, :, :], ALU.add).then_inc(fx_ready, 1)
            link(v.tensor_scalar(gates[:, :, :], gates[:, :, :], 1.0, None, ALU.add))
            link(v.reciprocal(gates[:, :, :], gates[:, :, :]))
            g0 = gates[:, 0, :].rearrange("p (h b) -> p h b", b=3)[:, :, 0]
            dve.wait_ge(ident_set, 1)
            link(v.tensor_reduce(coef[:, 1:2], ident[:, 31:P], AX, ALU.add))
            link(v.tensor_scalar(g0, g0, coef[:, 1:2], None, ALU.mult))

            dve.wait_ge(hid_exp, 1)
            link(v.tensor_scalar(hid_e, hid_e, 1.0, None, ALU.add))
            link(v.reciprocal(hid_e, hid_e))
            v.tensor_tensor(hid, bank[4][:, 0:248], hid_e, ALU.mult).then_inc(hid_ready, 1)

            dve.wait_ge(cum_mm, 1)
            link(v.tensor_copy(fox_sum, bank[5][0:H, :]))
            link(v.tensor_copy(fox_split[:, 0:S], fox_sum))
            v.tensor_tensor(fox_rest, fox_sum, fox_split[:, 0:S], ALU.subtract).then_inc(parts_ready, 1)
            dve.wait_ge(parts_ready, 1)
            link(v.tensor_copy(fox_split[:, S:2 * S], fox_rest))
            v.tensor_tensor(fox_rest, fox_rest, fox_split[:, S:2 * S], ALU.subtract).then_inc(parts_ready, 1)
            dve.wait_ge(parts_ready, 2)
            v.tensor_copy(fox_lo, fox_rest).then_inc(parts_ready, 1)

            def ada_rows(c):
                j = 24 + c
                dve.wait_ge(job_mm, j + 1)
                if c == 0:
                    dve.wait_ge(modb_in, 16)
                dst = mod_rows[:, c // 2, (c % 2) * 512:(c % 2) * 512 + 512]
                v.scalar_tensor_tensor(dst, bank[j % 4][:, :], 1.0 if c // 2 == 2 else 0.0, dst,
                                       ALU.add, ALU.add).then_inc(job_dve, 1)

            for c in range(2):
                ada_rows(c)
            v.memset(vc_diag, 0.0)
            dve.wait_ge(kc_mm, 1)
            v.tensor_copy(kcT[:, 0:NCMP], bank[6][:, 0:NCMP]).then_inc(dve_step, 1)
            steps[0] += 1
            dve.wait_ge(dve_step, steps[0])
            for r in range(R):
                last = v.tensor_copy(vc_diag[32 * r:32 * r + NCMP, :, r * DH:(r + 1) * DH],
                                     bank[7][32 * r:32 * r + NCMP, 0:2 * DH].rearrange("p (g d) -> p g d", g=G))
            last.then_inc(kc_ready, 1)
            for c in range(2, 4):
                ada_rows(c)
            dve.wait_ge(cmp_qk, 1)
            for g in range(G):
                pv_ = p_cmp[:, g, :].rearrange("p (t r n) -> p t r n", t=TT, r=R)[:, :, :, 0:NCMP]
                ps_ = bank[6 + g][:, :].rearrange("p (t r n) -> p t r n", t=TT, r=R)[:, :, :, 0:NCMP]
                st = c_stat[:, 0, :].rearrange("p (t r) -> p t r", t=TT)
                link(v.tensor_tensor(pv_, ps_, bias_c[:, :, g * R:(g + 1) * R, 0:NCMP], ALU.add))
                link(v.tensor_reduce(st, pv_, AX, ALU.max))
                v.tensor_tensor(pv_, pv_, st.rearrange("p t (r o) -> p t r o", o=1).to_broadcast([P, TT, R, NCMP]),
                                ALU.subtract).then_inc(cmp_max, 1)
                dve.wait_ge(cmp_max, g + 1)
            for g in range(G):
                pv_ = p_cmp[:, g, :].rearrange("p (t r n) -> p t r n", t=TT, r=R)[:, :, :, 0:NCMP]
                s0 = c_stat[:, 0, :].rearrange("p (t r) -> p t r", t=TT)
                s1 = c_stat[:, 1, :].rearrange("p (t r) -> p t r", t=TT)
                gate = gates[:, :, :].rearrange("p t (h b) -> p t h b", b=3)[:, :, g * R:(g + 1) * R, 0]
                dve.wait_ge(cmp_exp, g + 1)
                link(v.tensor_reduce(s0, pv_, AX, ALU.add))
                link(v.reciprocal(s1, s0))
                link(v.tensor_tensor(s1, s1, gate, ALU.mult))
                v.tensor_tensor(pv_, pv_, s1.rearrange("p t (r o) -> p t r o", o=1).to_broadcast([P, TT, R, NCMP]),
                                ALU.mult).then_inc(cmp_p, 1)
                dve.wait_ge(cmp_p, g + 1)
            for c in range(4, 8):
                ada_rows(c)
            for g in range(G):
                dve.wait_ge(cmp_pv, g + 1)
                at = S + g * R * DH
                for i in range(2):
                    last = v.tensor_copy(o_tok[:, 2 * i:2 * i + 2, at:at + R * DH],
                                         bank[2 * g + i][:, :].rearrange("p (t d) -> p t d", t=2))
                last.then_inc(cmp_o, 1)
            dve.wait_ge(cmp_o, 2)

            def max_task(t):
                kind, h, qt = TASKS[t]
                n = P * (qt + 1)
                b = bank[t % 3]
                dve.wait_ge(qk_done, t + 1)
                nm = nmax[:, t % 4:t % 4 + 1]
                if kind == "fox":
                    v.tensor_reduce(nm, b[:, 0:n], AX, ALU.max, negate=True).then_inc(max_done, 1)
                    return
                near = min(n, 256)
                link(v.tensor_tensor(b[:, n - near:n], b[:, n - near:n], bias_w[:, h, 256 - near:256], ALU.add))
                v.tensor_reduce(nm, b[:, 0:n], AX, ALU.max, negate=True).then_inc(max_done, 1)

            def copy_pT(t):
                n = P * (TASKS[t][2] + 1)
                dve.wait_ge(tr_done, t + 1)
                if t >= 2:
                    dve.wait_ge(pv_done, t - 1)
                v.tensor_copy(pT_buf[t % 2][:, 0:n], bank[3 + t % 2][:, 0:n]).then_inc(pT_dve, 1)

            def output(t):
                kind, h, qt = TASKS[t]
                cf = coef[:, t % 4:t % 4 + 1]
                dve.wait_ge(exp_done, t + 1)
                link(v.reciprocal(cf, rowsum[:, t % 4:t % 4 + 1]))
                o = bank[5 + t % 2][:, 0:DH]
                if kind == "fox":
                    dve.wait_ge(pv_done, t + 1)
                    v.tensor_scalar(o_tok[:, qt, h * DH:(h + 1) * DH], o, cf, None, ALU.mult).then_inc(o_done, 1)
                else:
                    gi = 3 * h + (1 if kind == "sel" else 2)
                    dst = o_tok[:, qt, S + h * DH:S + (h + 1) * DH]
                    link(v.tensor_tensor(cf, cf, gates[:, qt, gi:gi + 1], ALU.mult))
                    dve.wait_ge(pv_done, t + 1)
                    v.scalar_tensor_tensor(dst, o, cf, dst, ALU.mult, ALU.add).then_inc(o_done, 1)
                    dve.wait_ge(o_done, t + 1)

            for t in range(NT + 3):
                if t < NT:
                    max_task(t)
                if 2 <= t < NT + 2 and t - 2 < FIRST_NSA:
                    copy_pT(t - 2)
                if t >= 3:
                    output(t - 3)

            for k in range(1, KD, 2):
                dve.wait_ge(oT_mm, k + 1)
                v.tensor_copy(oT[:, k, :], bank[k % 4][:, :]).then_inc(oT_dve, 1)

            def layer_norm(t, n, g_row, b_row, done):
                x = x_tok[:, t, :]
                for i in range(2):
                    last = v.bn_stats(ln_stats[:, 6 * i:6 * i + 6], x[:, 512 * i:512 * i + 512])
                link(last)
                link(v.bn_aggr(ln_mv[:, :], ln_stats[:, :]))
                v.tensor_scalar(ln_r[:, 0:1], ln_mv[:, 1:2], EPS, None, ALU.add).then_inc(var_ready, 1)
                dve.wait_ge(rstd_ready, n)
                link(v.tensor_scalar(x, x, ln_mv[:, 0:1], ln_r[:, 1:2], ALU.subtract, ALU.mult))
                link(v.tensor_tensor(x, x, ln_rows[:, g_row, :], ALU.mult))
                v.tensor_tensor(x, x, ln_rows[:, b_row, :], ALU.add).then_inc(done, 1)

            dve.wait_ge(x_in, 16)
            dve.wait_ge(ln_in, 16)
            for t in range(TT):
                for c in range(2):
                    dve.wait_ge(mix_mm, 2 * t + c + 1)
                    last = v.tensor_tensor(ln_tmp[:, c * 512:(c + 1) * 512], bank[2 * (t % 2) + c][:, :],
                                           mod_rows[:, 0, c * 512:(c + 1) * 512], ALU.mult)
                    last.then_inc(mix_read, 1)
                dve.wait_ge(mix_read, 2 * t + 2)
                link(v.scalar_tensor_tensor(x_tok[:, t, :], x_tok[:, t, :], ALPHA, ln_tmp, ALU.mult, ALU.add))
                layer_norm(t, t + 1, 0, 1, x1_ready)

            def shared_act(t):
                dve.wait_ge(sh_silu, t + 1)
                v.tensor_tensor(sh_act[:, t, :], sh_sil[:, t % 2, :], bank[t % 2][:, F:2 * F], ALU.mult)\
                    .then_inc(sh_act_ready, 1)

            dve.wait_ge(h2_stored, 16 * TT)
            dve.wait_ge(h2T_mm, 2 * TT)
            dve.wait_ge(router_exp, 1)
            link(v.tensor_scalar(r_score, r_score, 1.0, None, ALU.add))
            link(v.reciprocal(r_score, r_score))
            link(v.tensor_tensor(r_bias, r_score,
                                 e_bias_row[:, :].rearrange("p (o e) -> p o e", o=1).to_broadcast([P, TT, E]), ALU.add))
            for t in range(TT):
                for g in range(EG):
                    last = v.max(r_top[:, t, g, :], r_bias[:, t, 8 * g:8 * g + 8])
            link(last)
            link(v.tensor_tensor(r_group, r_top[:, :, :, 0], r_top[:, :, :, 1], ALU.add))
            mine = r_group.rearrange("p t (g o) -> p t g o", o=1).to_broadcast([P, TT, EG, EG])
            other = r_group.rearrange("p t (o g) -> p t o g", o=1).to_broadcast([P, TT, EG, EG])
            link(v.tensor_tensor(r_gt, other, mine, ALU.is_gt))
            link(v.tensor_tensor(r_eq, other, mine, ALU.is_equal))
            for g in range(1, EG):
                last = v.tensor_tensor(r_gt[:, :, g, 0:g], r_gt[:, :, g, 0:g], r_eq[:, :, g, 0:g], ALU.add)
            link(last)
            link(v.tensor_reduce(r_rank, r_gt, AX, ALU.add))
            link(v.tensor_scalar(r_gmask, r_rank, TOPK_GROUPS - 0.5, None, ALU.is_lt))
            gm = r_gmask.rearrange("p t (g o) -> p t g o", o=1).to_broadcast([P, TT, EG, EG])
            mk = r_masked.rearrange("p t (g e) -> p t g e", g=EG)
            link(v.tensor_tensor(mk, r_bias.rearrange("p t (g e) -> p t g e", g=EG), gm, ALU.mult))
            link(v.tensor_scalar(r_rank, r_gmask, -1.0, -NEG, ALU.add, ALU.mult))
            link(v.tensor_tensor(mk, mk, r_rank.rearrange("p t (g o) -> p t g o", o=1).to_broadcast([P, TT, EG, EG]),
                                 ALU.add))
            for t in range(TT):
                last = v.max(r_best[:, t, :], r_masked[:, t, :])
            link(last)
            for t in range(TT):
                last = v.match_replace(r_sel[:, t, :], r_best[:, t, :], r_masked[:, t, :], 3e38)
            link(last)
            link(v.tensor_scalar(r_sel, r_sel, 2e38, None, ALU.is_gt))
            v.tensor_copy(r_selb, r_sel).then_inc(sel_ready, 1)
            shared_act(0)
            shared_act(1)
            link(v.tensor_tensor(r_gate, r_sel, r_score, ALU.mult))
            link(v.tensor_reduce(r_den, r_gate, AX, ALU.add))
            link(v.reciprocal(r_den, r_den))
            link(v.tensor_scalar(r_den, r_den, ROUTED_SCALE, None, ALU.mult))
            for t in range(TT):
                last = v.tensor_scalar(r_gate[:, t, :], r_gate[:, t, :], r_den[:, t:t + 1], None, ALU.mult)
            link(last)
            link(v.memset(zeros_e, 0.0))
            for t in range(TT):
                last = v.tensor_tensor_scan(r_kidx[:, t, :], r_sel[:, t, :], zeros_e, 0.0, ALU.add, ALU.add)
            link(last)
            link(v.tensor_tensor(r_kidx, r_kidx, r_sel, ALU.mult))
            shared_act(2)
            shared_act(3)
            dve.wait_ge(pos_mm, 1)
            count = bank[7][:, TT * E:(TT + 1) * E]
            link(v.tensor_scalar(n_units, count, SLOTS + 0.5, 1.0, ALU.is_gt, ALU.add))
            for i in range(2, TT):
                link(v.scalar_tensor_tensor(n_units, count, i * SLOTS + 0.5, n_units, ALU.is_gt, ALU.add))
            link(v.tensor_tensor_scan(unit_end, n_units, zeros_e, 0.0, ALU.add, ALU.add))
            link(v.tensor_tensor(n_units, unit_end, n_units, ALU.subtract))
            first = n_units.rearrange("p (o e) -> p o e", o=1).to_broadcast([P, TT, E])
            link(v.scalar_tensor_tensor(pos_m, first, float(SLOTS), bank[7][:, 0:TT * E].rearrange("p (t e) -> p t e", t=TT),
                                        ALU.mult, ALU.add))
            link(v.tensor_scalar(zeros_e, unit_end, row_no[:, :], None, ALU.is_le))
            link(v.tensor_reduce(expert_u[:, 1:2], zeros_e, AX, ALU.add))
            v.tensor_scalar(expert_u[:, 0:1], expert_u[:, 1:2], E - 1.0, None, ALU.min).then_inc(units_ready, 1)
            for k in range(TOP_K):
                v.scalar_tensor_tensor(r_pick[0], r_kidx, k + 1.0, pos_m, ALU.is_equal, ALU.mult)
                link(v.scalar_tensor_tensor(r_pick[1], r_kidx, k + 1.0, r_gate, ALU.is_equal, ALU.mult))
                v.tensor_reduce(slot_k[:, :, k], r_pick[0], AX, ALU.add)
                link(v.tensor_reduce(gate_k[:, :, k], r_pick[1], AX, ALU.add))
            link(v.tensor_copy(slot_ki, slot_k))
            link(v.tensor_scalar(unit_ki, slot_ki, SLOT_BITS, None, ALU.arith_shift_right))
            v.tensor_copy(unit_k, unit_ki)
            link(v.tensor_scalar(slot_ki, slot_ki, SLOTS - 1, None, ALU.bitwise_and))
            v.tensor_copy(slot_k, slot_ki)
            for i in range(2):
                link(v.tensor_copy(part_b, gate_k))
                link(v.tensor_copy(gate_parts[:, i, :, :], part_b))
                link(v.tensor_tensor(gate_k, gate_k, gate_parts[:, i, :, :], ALU.subtract))
            link(v.tensor_copy(gate_parts[:, 2, :, :], gate_k))
            for t in range(TT):
                for k in range(TOP_K):
                    j = TOP_K * t + k
                    b = j % 4
                    if j >= 4:
                        dve.wait_ge(list_mm, j - 3)
                    v.tensor_scalar(slot_hot[:, b, :], iota_b[:, :], slot_k[:, t, k:k + 1], None, ALU.is_equal)
                    values = [row_no[:, :], t * P - OUT_OF_RANGE] + [gate_parts[:, i, t, k:k + 1] for i in range(3)]
                    for c, value in enumerate(values):
                        last = v.tensor_scalar(unit_hot[:, b, c * UNITS:(c + 1) * UNITS], iota_b[:, 0:UNITS],
                                               unit_k[:, t, k:k + 1], value, ALU.is_equal, ALU.mult)
                    last.then_inc(hot_ready, 1)
                if t == 0:
                    dve.wait_ge(units_row, 1)
                    row = bank[7][0:1, 320:448]
                    v.tensor_copy(unit_expert, row)
                    link(v.tensor_scalar(unit_at, row, float(len(CHUNKS)), None, ALU.add))
                    v.tensor_scalar(unit_at, unit_at, RING - 1, DOWN_BITS, ALU.bitwise_and, ALU.logical_shift_left)
                    v.tensor_copy(expert_end[:, 0:E], unit_end[0:1, :])
                    link(v.tensor_scalar(expert_end[:, E:E + 1], unit_end[0:1, E - 1:E], 1.0, None, ALU.add))
                    link(v.tensor_scalar(expert_end[:, E:E + 1], expert_end[:, E:E + 1], 1, None,
                                         ALU.arith_shift_right))
                    v.tensor_scalar(expert_end[:, E + 1:E + 2], expert_end[:, E:E + 1], 2.0, -1.0,
                                    ALU.mult, ALU.add).then_inc(tables_ready, 1)
            dve.wait_ge(list_mm, TT * TOP_K)
            dve.wait_ge(scattered[1], 16)
            link(v.tensor_copy(list_sum, bank[6][:, 0:5 * UNITS]))
            part = [list_sum[:, c * UNITS:(c + 1) * UNITS] for c in range(5)]
            link(v.tensor_tensor(part[2], part[2], part[3], ALU.add))
            v.tensor_tensor(slot_gate[:, :], part[2], part[4], ALU.add)
            v.scalar_tensor_tensor(slot_idx[:, :], part[0], OUT_OF_RANGE, part[1], ALU.add, ALU.add)\
                .then_inc(lists_ready, 1)

            def copy_xT(n, u):
                dve.wait_ge(xe_tr, n + 1)
                v.tensor_copy(gatheredT[u % 2][:, 4:8, :], bank[2][:, :].rearrange("p (k m) -> p k m", k=4))\
                    .then_inc(xe_dve, 1)

            def copy_y(n, u, i):
                dve.wait_ge(down_done, n + 1)
                if isinstance(i, int) and i == 0:
                    for stored_rows in ffn_started:
                        dve.wait_ge(stored_rows, 8 * TT)
                else:
                    dve.wait_ge(scattered[u], 16 * (i + u))
                v.tensor_copy(y_out[u][:, 512:1024], bank[5][:, :]).then_inc(y_dve, 1)

            def activation(n):
                dve.wait_ge(silu_done, n + 1)
                settle(dve)
                v.scalar_tensor_tensor(e_act, bank[0][:, F:2 * F], slot_gate[:, bass.ds(n, 1)], silu_g,
                                       ALU.mult, ALU.mult).then_inc(act_done, 1)

            def copy_aT(n):
                dve.wait_ge(at_tr, n + 1)
                v.tensor_copy(e_actT, bank[3][:, 0:F].rearrange("p (i f) -> p i f", i=2)).then_inc(at_ready, 1)

            copy_xT(0, 0)
            activation(0)
            copy_xT(1, 1)
            copy_aT(0)
            activation(1)
            copy_xT(2, 0)
            copy_y(0, 0, 0)
            copy_aT(1)
            dve.wait_ge(tables_ready, 1)
            pairs = dve.value_load(expert_end[0:1, E:E + 1], min_val=E // 2, max_val=UNITS // 2 - 1)
            with dve.Fori(1, pairs) as i:
                activation(2 * i)
                copy_xT(2 * i + 1, 1)
                copy_y(2 * i - 1, 1, i - 1)
                copy_aT(2 * i)
                activation(2 * i + 1)
                copy_xT(2 * i + 2, 0)
                copy_y(2 * i, 0, i)
                copy_aT(2 * i + 1)
            copy_y(2 * pairs - 1, 1, pairs - 1)

            for t in range(TT):
                dve.wait_ge(ffn_in[t], 32)
                y = ffn_tok[0][:, t, :]
                link(v.tensor_tensor(y, y, ffn_tok[1][:, t, :], ALU.add))
                link(v.tensor_tensor(y, y, mod_rows[:, 3, :], ALU.mult))
                link(v.scalar_tensor_tensor(x_tok[:, t, :], x_tok[:, t, :], ALPHA, y, ALU.mult, ALU.add))
                layer_norm(t, TT + t + 1, 2, 3, x2_ready)


def bucket_table(np):
    dist = np.arange(NDIST) - DIST0
    n = np.maximum(dist, 0)
    exact = NB // 2
    nf = np.maximum(n, 1).astype(np.float32)
    large = exact + (np.log(nf / np.float32(exact)) / np.float32(np.log(128 / exact)) * (NB - exact)).astype(np.int32)
    bucket = np.where(n < exact, n, np.minimum(large, NB - 1))
    table = np.zeros((97, NDIST), np.float32)
    for part in range(3):
        table[NB * part + bucket[dist >= 0], np.nonzero(dist >= 0)[0]] = 1.0
    table[96, dist < 0] = 1.0
    return table


def kernel(x, c, w_ada, b_ada, w_in, b_f, cmp_pos_k, cmp_w1_k, cmp_w2_k, cmp_pos_v, cmp_w1_v, cmp_w2_v,
           rel_bias, w_out, ln1_g, ln1_b, w_router, e_bias, w_gate, w_up, w_down,
           ws_gate, ws_up, ws_down, ln2_g, ln2_b):
    import numpy as np
    import concourse.bacc as bacc
    from concourse.bass_utils import run_bass_kernel_spmd

    def rows(w):
        w = np.asarray(w)
        return np.ascontiguousarray(w.reshape(w.shape[0] // P, P, w.shape[1]).transpose(1, 0, 2))

    def chunks(w):
        w = np.asarray(w)
        n = w.shape[1] // CW
        return np.ascontiguousarray(w.reshape(KD, P, n, CW).transpose(2, 1, 0, 3)).reshape(n, P, KD * CW)

    xs = np.asarray(x)[0]
    widths = (512, 512, 512, 8, 512, 128, 128, 128, 128, 128, 128, 24)
    at = np.cumsum((0,) + widths)
    fq, fk, fv, ff, nq, kc, vc, ksl, vsl, kwn, vwn, ng = (np.asarray(w_in)[0][:, at[i]:at[i + 1]] for i in range(12))
    nq = nq.reshape(D, G, R, DH).transpose(0, 2, 1, 3).reshape(D, 512)
    wg, wu, wd = np.asarray(w_gate)[0], np.asarray(w_up)[0], np.asarray(w_down)[0]
    gu = np.empty((E, P, KD, 2, F), np.float32)
    gu[:, :, :, 0] = wg.reshape(E, KD, P, F).transpose(0, 2, 1, 3)
    gu[:, :, :, 1] = wu.reshape(E, KD, P, F).transpose(0, 2, 1, 3)
    ba = np.asarray(b_ada)[0]
    pos = np.stack([np.asarray(p)[0].reshape(16, P).T for p in (cmp_pos_k, cmp_pos_v)], axis=1)
    arrays = {
        "xT": rows(xs.T).reshape(P, KD * S),
        "x_tok": np.ascontiguousarray(xs.reshape(TT, P, D).transpose(1, 0, 2)),
        "c_col": np.ascontiguousarray(np.asarray(c)[0].reshape(KD, P).T),
        "w_ada": chunks(np.asarray(w_ada)[0]),
        "ada_b_col": np.ascontiguousarray(ba[0:2 * D].reshape(16, P).T),
        "ada_b_row": np.ascontiguousarray(ba[2 * D:].reshape(1, 4 * D)),
        "w_in": chunks(np.concatenate([fq, fk, nq, ksl, kwn, kc, vc, fv], axis=1)),
        "w_small": rows(np.concatenate([vsl, vwn, ff, ng], axis=1)).reshape(P, KD * WS_SMALL),
        "b_f": np.asarray(b_f).reshape(1, H),
        "w_cmp1": np.stack([rows(np.asarray(w)[0]).reshape(P, 16 * CMPH) for w in (cmp_w1_k, cmp_w1_v)]),
        "w_cmp2": np.stack([rows(np.asarray(w)[0]) for w in (cmp_w2_k, cmp_w2_v)], axis=1),
        "cmp_pos": np.ascontiguousarray(pos),
        "rel_bias": np.asarray(rel_bias),
        "buckets": bucket_table(np),
        "w_out": chunks(np.asarray(w_out)[0]),
        "ln_rows": np.concatenate([np.asarray(r)[0] for r in (ln1_g, ln1_b, ln2_g, ln2_b)]).reshape(1, 4 * D),
        "w_router": rows(np.asarray(w_router)[0]),
        "e_bias": np.asarray(e_bias).reshape(1, E),
        "w_gu": gu.reshape(E, P, KD * 2 * F),
        "w_d": np.ascontiguousarray(wd.reshape(E, 2, P, D).transpose(0, 2, 1, 3)).reshape(E, P, 2 * D),
        "ws_gu": chunks(np.concatenate([np.asarray(ws_gate)[0], np.asarray(ws_up)[0]], axis=1)),
        "ws_d": rows(np.asarray(ws_down)[0]).reshape(P, 2 * D),
    }
    nc = bacc.Bacc("TRN2", target_bir_lowering=False, num_devices=1)
    ins = {n: nc.dram_tensor(f"in_{n}", v.shape, F32, kind="ExternalInput").ap() for n, v in arrays.items()}
    out = nc.dram_tensor("out_x", (S, D), F32, kind="ExternalOutput").ap()
    build(nc, ins, out)
    r = run_bass_kernel_spmd(nc, [{f"in_{n}": v for n, v in arrays.items()}], core_ids=[0])
    return r.results[0]["out_x"].reshape(1, S, D)
```

```python
from contextlib import ExitStack

import concourse.bass as bass
from concourse import mybir

F32 = mybir.dt.float32
BF16 = mybir.dt.bfloat16
I32 = mybir.dt.int32
U32 = mybir.dt.uint32
ALU = mybir.AluOpType
ACT = mybir.ActivationFunctionType
AX = mybir.AxisListType.X

P = 128
S = 512
D = 1024
DH = 64
H = 8
R = 4
G = 2
TT = S // P
KD = D // P
NCMP = (S - 32) // 16 + 1
NB = 32
CMPH = 256
E = 64
EG = 8
F = 256
SCALE = DH ** -0.5
ALPHA = 2.0 ** 0.25
EPS = 1e-5
NEG = -1e30
ROUTED_SCALE = 2.5
TOPK_GROUPS = 4
SLOTS = 128
UNITS = 100
TOP_K = 8
SLOT_BITS = 7
DOWN_BITS = 11
OUT_OF_RANGE = 1024.0
DIST0 = S - 1
NDIST = DIST0 + S - NCMP
CW = 512
WS_SMALL = 288
RING = 4
WS_SLOT = 2
LEAD = 2

CHUNKS = ([("ada", c) for c in range(4)]
          + [("in", 0), ("in", 1), ("ada", 4), ("in", 2), ("ada", 5), ("ada", 6), ("in", 3), ("ada", 7), ("ada", 8),
             ("in", 4), ("ada", 9), ("ada", 10), ("small", 0), ("ada", 11), ("cmp", 0), ("cmp", 1),
             ("out", 0), ("out", 1), ("shared", 0)])
AT = {c: i for i, c in enumerate(CHUNKS)}

Q_ORDER = (0, 3, 1, 2)
TASKS = ([("fox", 2 * u + i, t) for u in range(H // 2) for t in Q_ORDER for i in range(2)]
         + [(kind, 2 * u + i, t) for u in range(H // 2) for t in Q_ORDER for kind in ("sel", "win") for i in range(2)])
NT = len(TASKS)
FIRST_NSA = H * TT
LAST_PAIR = [TT * u + TT - 1 for u in range(H // 2)] + [FIRST_NSA // 2 + 2 * TT * (u + 1) - 1 for u in range(H // 2)]


def build(nc, a, out):
    with ExitStack() as ctx:
        def sb(name, shape, dt=F32):
            return ctx.enter_context(nc.sbuf_tensor(name, shape, dt))

        def sem(name):
            return ctx.enter_context(nc.semaphore(name))

        h2_dram = nc.dram_tensor("h2_rows", [S, D], F32, kind="Internal")
        ffn_dram = [nc.dram_tensor(f"ffn_rows{i}", [S, D], F32, kind="Internal") for i in range(2)]

        bank = [ctx.enter_context(nc.psum_tensor(f"bank{i}", [P, 512], F32)) for i in range(8)]

        ring = sb("ring", [P, RING, KD * CW])
        down = sb("down", [P, RING, 2 * D])
        area_a = sb("area_a", [P, KD * S])
        area_c = sb("area_c", [P, TT * D])
        area_d = sb("area_d", [P, TT * D])
        area_e = sb("area_e", [P, 4096])
        area_f = sb("area_f", [P, 3072])
        area_g = sb("area_g", [P, 3072])
        mod_rows = sb("mod_rows", [P, 4, D])

        h1T = area_a[:, :].rearrange("p (k t) -> p k t", k=KD)
        h2T = h1T
        fqT = area_d[:, 0:2048].rearrange("p (i t) -> p i t", i=4)
        fkT = area_d[:, 2048:4096].rearrange("p (i t) -> p i t", i=4)
        x_tok = area_d[:, :].rearrange("p (t d) -> p t d", t=TT)
        nqT = area_e[:, 0:2048].rearrange("p (i t) -> p i t", i=4)
        kvT = area_e[:, 2048:4096].rearrange("p (i t) -> p i t", i=4)
        fv = area_f[:, 0:2048].rearrange("p (t d) -> p t d", t=TT)
        vsw = area_f[:, 2048:3072].rearrange("p (t d) -> p t d", t=TT)
        bias_w = area_g[:, 0:2048].rearrange("p (h j) -> p h j", h=H)
        bias_c = area_g[:, 2048:3072].rearrange("p (t h n) -> p t h n", t=TT, h=H)
        oT = area_c[:, :].rearrange("p (k t) -> p k t", k=KD)
        h2_tok = [area_f[:, 0:1024], area_f[:, 1024:2048], area_g[:, 0:1024], area_g[:, 1024:2048]]
        ffn_tok = [area_c[:, :].rearrange("p (t d) -> p t d", t=TT), area_a[:, :].rearrange("p (t d) -> p t d", t=TT)]
        ada_sum = [down[:, 2, 512 * i:512 * i + 512] for i in range(2)]
        tri = down[:, 2, 1024:1536]
        ones_f = down[:, 2, 1024 + P:1024 + 2 * P]
        hid = down[:, 2, 1536:1792]
        hid_e = down[:, 2, 1792:2048]
        hidT = hid_e.rearrange("p (f m) -> p f m", f=2)
        pair = [down[:, 0, i * 1024:(i + 1) * 1024].rearrange("p (g t) -> p g t", g=G) for i in range(2)]
        xb = [down[:, 1, i * 1024:(i + 1) * 1024] for i in range(2)]
        fox_parts = area_a[0:3, 0:2048].bitcast(BF16).rearrange("p (h t) -> p h t", h=H)
        vc_diag = area_a[:, 2048:2560].rearrange("p (g d) -> p g d", g=G)
        fox_sum = area_a[0:H, 2560:3072]
        fox_rest = area_a[0:H, 3072:3584]
        fox_split = area_a[0:H, 3584:4096].bitcast(BF16)
        fox_lo = area_a[0:H, 2560:2816].bitcast(BF16)
        p_cmp = down[:, 3, 0:1024].rearrange("p (i f) -> p i f", i=2)
        p_cmpT = down[:, 3, 1024:2048].rearrange("p (g f) -> p g f", g=G)
        diag = down[:, 3, 0:512].rearrange("p (i q) -> p i q", i=4)
        pT_buf = [down[:, 1, i * 512:(i + 1) * 512] for i in range(4)]
        p_buf = [down[:, 2, i * 512:(i + 1) * 512] for i in range(4)]
        fk_odd = down[:, 0, :].rearrange("p (i t) -> p i t", i=4)
        ln_rows = area_e[:, :].rearrange("p (i d) -> p i d", i=4)
        ln_tmp = area_g[:, 2048:3072]
        sh_act = area_f[:, 0:TT * F].rearrange("p (t f) -> p t f", t=TT)
        sh_sil = area_f[:, 1024:1536].rearrange("p (i f) -> p i f", i=2)
        sh_actT = area_f[:, 1536:2048].rearrange("p (i f) -> p i f", i=2)
        sh_y = area_g[:, 0:2048].rearrange("p (i f) -> p i f", i=2)
        r_score = area_c[:, 0:256].rearrange("p (t e) -> p t e", t=TT)
        r_bias = area_c[:, 256:512].rearrange("p (t e) -> p t e", t=TT)
        r_top = area_c[:, 512:768].rearrange("p (t g e) -> p t g e", t=TT, g=EG)
        r_gt = area_c[:, 768:1024].rearrange("p (t g e) -> p t g e", t=TT, g=EG)
        r_eq = area_c[:, 1024:1280].rearrange("p (t g e) -> p t g e", t=TT, g=EG)
        r_group = area_c[:, 1280:1312].rearrange("p (t g) -> p t g", t=TT)
        r_rank = area_c[:, 1312:1344].rearrange("p (t g) -> p t g", t=TT)
        r_gmask = area_c[:, 1344:1376].rearrange("p (t g) -> p t g", t=TT)
        r_masked = area_c[:, 1376:1632].rearrange("p (t e) -> p t e", t=TT)
        r_best = area_c[:, 1632:1664].rearrange("p (t e) -> p t e", t=TT)
        r_sel = area_c[:, 1664:1920].rearrange("p (t e) -> p t e", t=TT)
        r_gate = area_c[:, 1920:2176].rearrange("p (t e) -> p t e", t=TT)
        r_den = area_c[:, 2176:2180]
        r_selb = area_c[:, 2184:2312].bitcast(BF16).rearrange("p (t e) -> p t e", t=TT)
        pos_m = area_c[:, 2312:2568].rearrange("p (t e) -> p t e", t=TT)
        r_kidx = area_c[:, 2568:2824].rearrange("p (t e) -> p t e", t=TT)
        r_pick = [area_c[:, 2824 + 256 * i:3080 + 256 * i].rearrange("p (t e) -> p t e", t=TT) for i in range(2)]
        slot_k = area_c[:, 3336:3368].rearrange("p (t k) -> p t k", t=TT)
        gate_k = area_c[:, 3368:3400].rearrange("p (t k) -> p t k", t=TT)
        slot_ki = area_c[:, 3400:3432].bitcast(I32).rearrange("p (t k) -> p t k", t=TT)
        unit_ki = area_c[:, 3432:3464].bitcast(I32).rearrange("p (t k) -> p t k", t=TT)
        unit_k = area_c[:, 3464:3496].rearrange("p (t k) -> p t k", t=TT)
        gate_parts = area_c[:, 3496:3592].rearrange("p (i t k) -> p i t k", i=3, t=TT)
        slot_hot = area_c[:, 3592:3848].bitcast(BF16).rearrange("p (b s) -> p b s", b=4)
        part_b = area_c[:, 3848:3864].bitcast(BF16).rearrange("p (t k) -> p t k", t=TT)
        n_units = area_c[:, 3864:3928]
        unit_end = area_c[:, 3928:3992]
        zeros_e = area_c[:, 3992:4056]
        expert_u = area_c[:, 4056:4060]

        ident = sb("ident", [P, P])
        ident_b = sb("ident_b", [P, P], BF16)
        ones_b = sb("ones_b", [P, P], BF16)
        causal_b = sb("causal_b", [P, P], BF16)
        before_b = sb("before_b", [P, P], BF16)
        iota_b = sb("iota_b", [P, SLOTS], BF16)
        row_no = sb("row_no", [P, 1])
        table_b = sb("table_b", [P, NDIST + 1], BF16)
        rel_parts = sb("rel_parts", [P, H], BF16)
        c_col = sb("c_col", [P, KD])
        sc_col = sb("sc_col", [P, 3, KD])
        ada_b_col = sb("ada_b_col", [P, 16])
        mod_col = sb("mod_col", [P, 16])
        bf_row = sb("bf_row", [P, H])
        ffng = sb("ffng", [P, TT, 32])
        gates = sb("gates", [P, TT, 24])
        fx = sb("fx", [P, 3, TT, H])
        pos2 = sb("pos2", [P, 2, 16])
        w2 = sb("w2", [P, 2, 2, DH])
        kc2 = sb("kc2", [P, 64])
        nmax = sb("nmax", [P, 4])
        rowsum = sb("rowsum", [P, 4])
        inv_sum = sb("inv_sum", [P, 4])
        early = sb("early", [P, 1])
        c_stat = sb("c_stat", [P, 3, 16])
        ln_stats = sb("ln_stats", [P, 12])
        ln_mv = sb("ln_mv", [P, 2])
        ln_r = sb("ln_r", [P, 2])
        e_bias_row = sb("e_bias_row", [P, E])
        slot_idx = mod_rows[:, 1, 0:UNITS].bitcast(U32)
        slot_gate = mod_rows[:, 1, 128:128 + UNITS]
        idx_gather = [sb(f"idx_gather{i}", [P, 1], U32) for i in range(2)]
        idx_scatter = [sb(f"idx_scatter{i}", [P, 1], U32) for i in range(2)]
        unit_at = area_f[0:1, 2944:3072].bitcast(I32)
        unit_expert = area_f[0:1, 2816:2944].bitcast(I32)
        expert_end = mod_rows[0:1, 1, 256:256 + E + 2].bitcast(I32)
        w_router_t = area_f[:, 2048:2560].rearrange("p (k e) -> p k e", k=KD)
        gathered = [area_e[:, i * 1024:(i + 1) * 1024] for i in range(2)]
        gatheredT = [area_f[:, i * 1024:(i + 1) * 1024].rearrange("p (k m) -> p k m", k=KD) for i in range(2)]
        ring_flat = ring[:, :, :].rearrange("p s n -> p (s n)")
        down_flat = down[:, :, :].rearrange("p s n -> p (s n)")
        y_out = [area_g[:, i * 1024:(i + 1) * 1024] for i in range(2)]
        silu_g = area_f[:, 2048:2304]
        e_act = area_f[:, 2304:2560]
        e_actT = area_f[:, 2560:2816].rearrange("p (i f) -> p i f", i=2)
        unit_hot = area_g[:, 2048:3048].bitcast(BF16).rearrange("p (b n) -> p b n", b=4)
        list_sum = area_e[:, 0:5 * UNITS]

        slot_in = [sem(f"slot_in{s}") for s in range(RING)]
        down_in = [sem(f"down_in{s}") for s in range(RING)]
        chunk_used = sem("chunk_used")
        c_in = sem("c_in")
        ada_part = sem("ada_part")
        ada_mm = sem("ada_mm")
        ada_out = sem("ada_out")
        k_padded = sem("k_padded")
        hidT_mm = sem("hidT_mm")
        hidT_ready = sem("hidT_ready")
        inv_ready = sem("inv_ready")
        diag_ready = sem("diag_ready")
        rows_ready = sem("rows_ready")
        o_act = sem("o_act")
        o_dve = sem("o_dve")
        xT_in = sem("xT_in")
        consts_in = sem("consts_in")
        table_in = sem("table_in")
        modb_in = sem("modb_in")
        masks_set = sem("masks_set")
        ident_set = sem("ident_set")
        passed = sem("passed")
        rel_set = sem("rel_set")
        bias_mm = sem("bias_mm")
        bias_out = sem("bias_out")
        c_exp = sem("c_exp")
        c_ready = sem("c_ready")
        mod_ready = sem("mod_ready")
        h1_ready = sem("h1_ready")
        job_mm = sem("job_mm")
        job_act = sem("job_act")
        job_dve = sem("job_dve")
        ffng_act = sem("ffng_act")
        fx_ready = sem("fx_ready")
        cum_mm = sem("cum_mm")
        parts_ready = sem("parts_ready")
        parts_in = sem("parts_in")
        pair_in = [sem("pair_in_k"), sem("pair_in_v")]
        xb_ready = sem("xb_ready")
        hid_mm = sem("hid_mm")
        hid_exp = sem("hid_exp")
        hid_ready = sem("hid_ready")
        kc_mm = sem("kc_mm")
        kc_ready = sem("kc_ready")
        cmp_qk = sem("cmp_qk")
        cmp_max = sem("cmp_max")
        cmp_exp = sem("cmp_exp")
        cmp_p = sem("cmp_p")
        cmp_tr = sem("cmp_tr")
        cmp_pT = sem("cmp_pT")
        qk_done = sem("qk_done")
        max_done = sem("max_done")
        exp_done = sem("exp_done")
        tr_done = sem("tr_done")
        pT_act = sem("pT_act")
        pT_dve = sem("pT_dve")
        pv_done = sem("pv_done")
        x_in = sem("x_in")
        ln_in = sem("ln_in")
        mix_mm = sem("mix_mm")
        mix_read = sem("mix_read")
        var_ready = sem("var_ready")
        rstd_ready = sem("rstd_ready")
        x1_ready = sem("x1_ready")
        h2_ready = sem("h2_ready")
        h2_stored = sem("h2_stored")
        h2T_mm = sem("h2T_mm")
        h2T_act = sem("h2T_act")
        router_mm = sem("router_mm")
        router_exp = sem("router_exp")
        router_in = sem("router_in")
        sel_ready = sem("sel_ready")
        pos_mm = sem("pos_mm")
        units_ready = sem("units_ready")
        units_row = sem("units_row")
        hot_ready = sem("hot_ready")
        list_mm = sem("list_mm")
        lists_ready = sem("lists_ready")
        tables_ready = sem("tables_ready")
        weights_ready = sem("weights_ready")
        sh_gu = sem("sh_gu")
        sh_silu = sem("sh_silu")
        sh_act_ready = sem("sh_act_ready")
        sh_tr = sem("sh_tr")
        sh_actT_ready = sem("sh_actT_ready")
        sh_down = sem("sh_down")
        sh_y_ready = sem("sh_y_ready")
        ffn_started = [sem(f"ffn_started{i}") for i in range(2)]
        cleared = sem("cleared")
        idx_set = sem("idx_set")
        idx_out = sem("idx_out")
        gather_in = [sem(f"gather_in{i}") for i in range(2)]
        xe_tr = sem("xe_tr")
        xe_act = sem("xe_act")
        xe_dve = sem("xe_dve")
        gu_done = sem("gu_done")
        silu_done = sem("silu_done")
        act_done = sem("act_done")
        at_tr = sem("at_tr")
        at_ready = sem("at_ready")
        down_done = sem("down_done")
        y_act = sem("y_act")
        y_dve = sem("y_dve")
        scattered = [sem(f"scattered{i}") for i in range(2)]
        ffn_in = [sem(f"ffn_in{t}") for t in range(TT)]
        x2_ready = sem("x2_ready")
        stored = sem("stored")
        dve_step = sem("dve_step")
        act_step = sem("act_step")
        pool_step = sem("pool_step")

        block = ctx.enter_context(nc.Block())

        NJ = 24
        owner = ["act" if j % 2 == 0 else "dve" for j in range(NJ)]

        def copied(j):
            o = owner[j]
            return (job_act if o == "act" else job_dve), sum(owner[i] == o for i in range(j + 1))

        def settle(eng):
            eng.sem_inc(passed, 1)

        def used(i):
            mine = [(kind == "ada") == (CHUNKS[i][0] == "ada") for kind, c in CHUNKS[:i + 1]]
            return (ada_part if CHUNKS[i][0] == "ada" else chunk_used), sum(mine)

        def heads_out(u):
            return (o_act, u + 1) if u < H // 2 else (o_dve, u - H // 2 + 1)

        def chunks_before(slot):
            return sum(i % RING == slot for i in range(len(CHUNKS)))

        def pT_ready(t):
            if t < FIRST_NSA:
                return pT_dve, t + 1
            return pT_act, t - FIRST_NSA + 1

        @block.sync
        def _(sp):
            def load_chunk(i):
                kind, c = CHUNKS[i]
                if i >= RING:
                    sp.wait_ge(*used(i - RING))
                if kind == "small":
                    sp.dma_start(ring[:, i % RING, 0:KD * WS_SMALL], a["w_small"]).then_inc(slot_in[i % RING], 16)
                else:
                    src = {"ada": a["w_ada"], "in": a["w_in"], "cmp": a["w_cmp1"], "out": a["w_out"],
                           "shared": a["ws_gu"]}[kind]
                    sp.dma_start(ring[:, i % RING, :], src[c]).then_inc(slot_in[i % RING], 16)

            for i in range(len(CHUNKS)):
                load_chunk(i)
            def slot_of(u):
                return (len(CHUNKS) + u) % RING

            def landed(e, i, u):
                s = slot_of(u)
                sp.wait_ge(slot_in[s], 16 * (i + chunks_before(s) + 1))
                settle(sp)
                sp.wait_ge(down_in[s], 16 * (i + (1 if s == WS_SLOT else 0) + 1))
                sp.sem_inc(weights_ready, 1)

            for u in range(RING):
                s = slot_of(u)
                sp.wait_ge(*used(len(CHUNKS) + u - RING))
                sp.dma_start(ring[:, s, :], a["w_gu"][u]).then_inc(slot_in[s], 16)
                if u == 0:
                    sp.wait_ge(pv_done, NT // 2)
                    sp.dma_start(down[:, WS_SLOT, :], a["ws_d"]).then_inc(down_in[WS_SLOT], 16)
                if s == WS_SLOT:
                    sp.wait_ge(sh_down, TT)
                sp.dma_start(down[:, s, :], a["w_d"][u]).then_inc(down_in[s], 16)
                if u >= LEAD:
                    landed(u - LEAD, 0, u - LEAD)
            sp.wait_ge(tables_ready, 1)
            with sp.Fori(1, E // RING) as i:
                for u in range(RING):
                    s = slot_of(u)
                    e = i * RING + u
                    units = sp.value_load(expert_end[0:1, bass.ds(e - RING, 1)], min_val=1, max_val=UNITS)
                    sp.wait_ge(gu_done, units)
                    settle(sp)
                    sp.dma_start(ring[:, s, :], a["w_gu"][bass.ds(e, 1)].rearrange("o p n -> p (o n)"))\
                        .then_inc(slot_in[s], 16)
                    sp.wait_ge(down_done, units)
                    settle(sp)
                    sp.dma_start(down[:, s, :], a["w_d"][bass.ds(e, 1)].rearrange("o p n -> p (o n)"))\
                        .then_inc(down_in[s], 16)
                    landed(e - LEAD, i if u >= LEAD else i - 1, (u - LEAD) % RING)
            for u in range(RING - LEAD, RING):
                landed(E - RING + u, E // RING - 1, u)

        @block.scalar
        def _(act):
            steps = [0]

            def link(ins):
                steps[0] += 1
                ins.then_inc(act_step, 1)
                act.wait_ge(act_step, steps[0])

            act.dma_start(c_col[:, :], a["c_col"]).then_inc(c_in, 16)
            act.dma_start(ada_b_col[:, :], a["ada_b_col"]).then_inc(consts_in, 16)
            act.dma_start(area_a[:, :], a["xT"]).then_inc(xT_in, 16)
            act.dma_start(bf_row[:, :], a["b_f"].to_broadcast([P, H])).then_inc(consts_in, 16)
            act.dma_start(pos2[:, :, :], a["cmp_pos"]).then_inc(consts_in, 16)
            act.dma_start(w2[:, :, :, :], a["w_cmp2"]).then_inc(consts_in, 16)
            act.dma_start(e_bias_row[:, :], a["e_bias"].to_broadcast([P, E])).then_inc(consts_in, 16)
            act.dma_start(mod_rows[:, :, :].rearrange("p i d -> p (i d)"),
                          a["ada_b_row"].to_broadcast([P, 4 * D])).then_inc(modb_in, 16)

            act.wait_ge(c_in, 16)
            nc.scalar.activation(sc_col[:, 0, :], c_col[:, :], ACT.Exp, scale=-1.0).then_inc(c_exp, 1)

            for j in range(0, 24, 2):
                act.wait_ge(job_mm, j + 1)
                if j < 16:
                    i = j % 4
                    dst = [fqT, fkT, nqT, kvT][j // 4][:, i, :]
                    nc.scalar.activation(dst, bank[j % 4][:, :], ACT.Copy,
                                         scale=SCALE if j // 4 in (0, 2) else 1.0).then_inc(job_act, 1)
                elif j < 20:
                    nc.scalar.activation(fv[:, j - 16, :], bank[j % 4][:, :], ACT.Copy).then_inc(job_act, 1)
                else:
                    t = j - 20
                    nc.scalar.activation(ffng[:, t, :], bank[j % 4][:, 256:288], ACT.Copy).then_inc(ffng_act, 1)
                    nc.scalar.activation(vsw[:, t, :], bank[j % 4][:, 0:256], ACT.Copy).then_inc(job_act, 1)

            act.wait_ge(ffng_act, TT)
            nc.scalar.activation(gates[:, :, :], ffng[:, :, H:32], ACT.Exp, scale=-1.0).then_inc(fx_ready, 1)
            act.wait_ge(fx_ready, 2)
            link(nc.scalar.activation(fx[:, 1, :, :], fx[:, 1, :, :], ACT.Exp, scale=-1.0))
            nc.scalar.activation(fx[:, 1, :, :], fx[:, 1, :, :], ACT.Ln, bias=1.0).then_inc(fx_ready, 1)

            act.wait_ge(hid_mm, 1)
            nc.scalar.activation(hid_e, bank[4][:, 0:256], ACT.Exp, scale=-1.0).then_inc(hid_exp, 1)

            for i in range(2):
                act.wait_ge(cmp_max, i + 1)
                nc.scalar.activation(p_cmp[:, i, :], p_cmp[:, i, :], ACT.Exp).then_inc(cmp_exp, 1)
            for g in range(G):
                act.wait_ge(cmp_tr, g + 1)
                nc.scalar.activation(p_cmpT[:, g, :], bank[6 + g][:, :], ACT.Copy).then_inc(cmp_pT, 1)

            def exp_task(t):
                kind, h, qt = TASKS[t]
                n = P * (qt + 1)
                act.wait_ge(max_done, t + 1)
                if t == 0:
                    act.wait_ge(kc_mm, 1)
                    act.wait_ge(cmp_tr, 2)
                if t >= 4:
                    act.wait_ge(tr_done, t - 3)
                nc.scalar.activation(p_buf[t % 4][:, 0:n], bank[t % 4][:, 0:n], ACT.Exp,
                                     bias=nmax[:, t % 4:t % 4 + 1],
                                     accum_out=rowsum[:, t % 4:t % 4 + 1]).then_inc(exp_done, 1)

            def copy_pT(t):
                n = P * (TASKS[t][2] + 1)
                act.wait_ge(tr_done, t + 1)
                if t >= 4:
                    act.wait_ge(pv_done, (t - 4) // 2 + 1)
                nc.scalar.activation(pT_buf[t % 4][:, 0:n], bank[4 + t % 2][:, 0:n], ACT.Copy).then_inc(pT_act, 1)

            for t in range(NT + 3):
                if t < NT:
                    exp_task(t)
                if t >= 3 and t - 3 >= FIRST_NSA:
                    copy_pT(t - 3)
                for u in range(H // 2):
                    if t == 2 * LAST_PAIR[u] + 6:
                        act.wait_ge(pv_done, LAST_PAIR[u] + 1)
                        nc.scalar.activation(oT[:, u, :], bank[6 + u % 2][:, :], ACT.Copy).then_inc(o_act, 1)
                if t == FIRST_NSA + 2:
                    act.wait_ge(qk_done, FIRST_NSA)
                    act.dma_start(area_d[:, :].rearrange("p (t d) -> p t d", t=TT), a["x_tok"]).then_inc(x_in, 16)

            act.wait_ge(qk_done, NT)
            act.dma_start(ln_rows[:, :, :].rearrange("p i d -> p (i d)"), a["ln_rows"].to_broadcast([P, 4 * D])).then_inc(ln_in, 16)

            act.wait_ge(pv_done, NT // 2)
            act.dma_start(w_router_t, a["w_router"]).then_inc(router_in, 16)

            def rstd(n):
                act.wait_ge(var_ready, n)
                link(nc.scalar.activation(ln_r[:, 0:1], ln_r[:, 0:1], ACT.Ln))
                nc.scalar.activation(ln_r[:, 1:2], ln_r[:, 0:1], ACT.Exp, scale=-0.5).then_inc(rstd_ready, 1)

            for t in range(TT):
                rstd(t + 1)
                for half in range(2):
                    act.wait_ge(h2T_mm, 2 * t + half + 1)
                    nc.scalar.activation(h2T[:, 4 * half:4 * half + 4, t * P:(t + 1) * P],
                                         bank[4 + half][:, :].rearrange("p (k m) -> p k m", k=4),
                                         ACT.Copy).then_inc(h2T_act, 1)
            act.wait_ge(router_mm, TT)
            act.wait_ge(h2_stored, 16 * TT)
            nc.scalar.activation(r_score, bank[6][:, 0:256].rearrange("p (t e) -> p t e", t=TT),
                                 ACT.Exp, scale=-1.0).then_inc(router_exp, 1)

            for t in range(TT):
                act.wait_ge(sh_gu, t + 1)
                if t >= 2:
                    act.wait_ge(sh_act_ready, t - 1)
                nc.scalar.activation(sh_sil[:, t % 2, :], bank[t % 2][:, 0:F], ACT.Silu).then_inc(sh_silu, 1)
            for t in range(TT):
                act.wait_ge(sh_tr, t + 1)
                if t >= 1:
                    act.wait_ge(sh_down, t)
                nc.scalar.activation(sh_actT[:, :, 0:P], bank[2][:, 0:F].rearrange("p (i f) -> p i f", i=2),
                                     ACT.Copy).then_inc(sh_actT_ready, 1)
                act.wait_ge(sh_down, t + 1)
                if t >= 2:
                    act.wait_ge(ffn_started[t % 2], 16 * (t // 2))
                nc.scalar.activation(sh_y[:, t % 2, 0:512], bank[4][:, :], ACT.Copy).then_inc(sh_y_ready, 1)
                nc.scalar.activation(sh_y[:, t % 2, 512:1024], bank[5][:, :], ACT.Copy).then_inc(sh_y_ready, 1)
                act.wait_ge(sh_y_ready, 2 * t + 2)
                act.dma_start(ffn_dram[0][t * P:(t + 1) * P, :], sh_y[:, t % 2, :]).then_inc(ffn_started[t % 2], 16)

            def silu(n):
                act.wait_ge(gu_done, n + 1)
                nc.scalar.activation(silu_g, bank[0][:, 0:F], ACT.Silu).then_inc(silu_done, 1)

            def copy_xT(n, u):
                act.wait_ge(xe_tr, n + 1)
                nc.scalar.activation(gatheredT[u % 2][:, 0:4, :], bank[1][:, :].rearrange("p (k m) -> p k m", k=4),
                                     ACT.Copy).then_inc(xe_act, 1)

            def copy_y(n, u, i):
                act.wait_ge(down_done, n + 1)
                if isinstance(i, int) and i == 0:
                    for stored_rows in ffn_started:
                        act.wait_ge(stored_rows, 8 * TT)
                else:
                    act.wait_ge(scattered[u], 16 * (i + u))
                nc.scalar.activation(y_out[u][:, 0:512], bank[4][:, :], ACT.Copy).then_inc(y_act, 1)

            copy_xT(0, 0)
            silu(0)
            copy_xT(1, 1)
            silu(1)
            copy_xT(2, 0)
            copy_y(0, 0, 0)
            act.wait_ge(tables_ready, 1)
            pairs = act.value_load(expert_end[0:1, E:E + 1], min_val=E // 2, max_val=UNITS // 2 - 1)
            with act.Fori(1, pairs) as i:
                silu(2 * i)
                copy_xT(2 * i + 1, 1)
                copy_y(2 * i - 1, 1, i - 1)
                silu(2 * i + 1)
                copy_xT(2 * i + 2, 0)
                copy_y(2 * i, 0, i)
            last = 2 * pairs - 1
            copy_y(last, 1, pairs - 1)

            for t in range(TT):
                rstd(TT + t + 1)

        @block.tensor
        def _(pe):
            pe.wait_ge(table_in, 80)
            pe.wait_ge(rel_set, 1)
            for b in range(4):
                for i in range(64):
                    j = 64 * b + i
                    first = DIST0 + P - j
                    last = nc.tensor.matmul(bank[b][:, 8 * i:8 * i + 8], table_b[0:97, first:first + P],
                                            rel_parts[0:97, :], start=True, stop=True)
                last.then_inc(bias_mm, 1)
            for t in range(TT):
                for n in range(NCMP):
                    first = DIST0 + P * t - 16 * n - 31
                    last = nc.tensor.matmul(bank[4 + t][:, 8 * n:8 * n + 8], table_b[0:97, first:first + P],
                                            rel_parts[0:97, :], start=True, stop=True)
                last.then_inc(bias_mm, 1)

            pe.wait_ge(masks_set, 1)
            pe.wait_ge(bias_out, 1)
            for i in range(4):
                pe.wait_ge(ada_part, i + 1)
                for m in range(4):
                    last = nc.tensor.matmul(bank[0][:, 4 * i + m:4 * i + m + 1], ada_sum[i % 2][:, m * P:(m + 1) * P],
                                            ones_f[:, 0:1], start=True, stop=True)
                last.then_inc(ada_mm, 1)
            pe.wait_ge(mod_ready, 1)
            pe.wait_ge(h1_ready, 1)
            pe.wait_ge(bias_out, 8)

            def arrived(i):
                pe.wait_ge(slot_in[i % RING], 16 * (i // RING + 1))

            def free_bank(j):
                if j >= 4:
                    pe.wait_ge(*copied(j - 4))

            def ada_row(c):
                pe.wait_ge(ada_part, 4 + c + 1)
                if c >= 2:
                    pe.wait_ge(ada_out, c - 1)
                nc.tensor.matmul(bank[6 + c % 2][:, :], ones_f, ada_sum[c % 2], start=True, stop=True)\
                    .then_inc(ada_mm, 1)

            for c in range(4):
                i = AT["in", c]
                arrived(i)
                w = ring[:, i % RING, :].rearrange("p (k n) -> p k n", k=KD)
                for m in range(4):
                    j = 4 * c + m
                    free_bank(j)
                    for k in range(KD):
                        last = nc.tensor.matmul(bank[j % 4][:, :], w[:, k, m * P:(m + 1) * P], h1T[:, k, :],
                                                start=(k == 0), stop=(k == KD - 1))
                    last.then_inc(job_mm, 1)
                pe.wait_ge(job_mm, 4 * c + 4)
                nc.tensor.nop().then_inc(chunk_used, 1)
                if c >= 1:
                    ada_row(c - 1)
            for c, width in ((AT["in", 4], CW), (AT["small", 0], WS_SMALL)):
                arrived(c)
                w = ring[:, c % RING, 0:KD * width].rearrange("p (k n) -> p k n", k=KD)
                for t in range(TT):
                    j = (16 if width == CW else 20) + t
                    free_bank(j)
                    for k in range(KD):
                        last = nc.tensor.matmul(bank[j % 4][:, 0:width], h1T[:, k, t * P:(t + 1) * P], w[:, k, :],
                                                start=(k == 0), stop=(k == KD - 1))
                    last.then_inc(job_mm, 1)
                    if j in (17, 18, 21, 23):
                        ada_row({17: 3, 18: 4, 21: 5, 23: 6}[j])
                pe.wait_ge(job_mm, j + 1)
                nc.tensor.nop().then_inc(chunk_used, 1)

            pe.wait_ge(xb_ready, 2)
            arrived(AT["cmp", 0])
            arrived(AT["cmp", 1])
            for jj in range(16):
                for s in range(2):
                    w = ring[:, AT["cmp", s] % RING, :].rearrange("p (k n) -> p k n", k=16)
                    last = nc.tensor.matmul(bank[4][64 * s:64 * s + 64, 0:CMPH], xb[s][:, 64 * jj:64 * jj + 64],
                                            w[:, jj, :], start=(jj == 0), stop=(jj == 15))
            last.then_inc(hid_mm, 1)
            pe.wait_ge(hid_mm, 1)
            nc.tensor.nop().then_inc(chunk_used, 2)

            pe.wait_ge(fx_ready, 4)
            pe.wait_ge(masks_set, 1)
            for kt in range(TT):
                last = nc.tensor.matmul(bank[5][0:H, kt * P:S], fx[:, 2, kt, :], tri[:, 0:S - kt * P],
                                        start=(kt == 0), stop=(kt == TT - 1))
            last.then_inc(cum_mm, 1)

            ada_row(7)
            pe.wait_ge(hid_ready, 1)
            pe.wait_ge(ident_set, 2)
            for f in range(2):
                last = nc.tensor.transpose(bank[4][:, 256 + f * P:256 + (f + 1) * P], hid[:, f * P:(f + 1) * P],
                                           ident[:, :])
            last.then_inc(hidT_mm, 1)
            pe.wait_ge(hidT_ready, 1)
            for g in range(G):
                for f in range(2):
                    nc.tensor.matmul(bank[4][g * DH:(g + 1) * DH, 0:NCMP], w2[:, 0, f, :],
                                     hidT[:, f, g * NCMP:(g + 1) * NCMP], start=(f == 0), stop=(f == 1))
            for r in range(R):
                for g in range(G):
                    for f in range(2):
                        last = nc.tensor.matmul(bank[4][32 * r:32 * r + NCMP, 64 + g * DH:64 + (g + 1) * DH],
                                                hidT[:, f, 64 + g * NCMP:64 + (g + 1) * NCMP], w2[:, 1, f, :],
                                                start=(f == 0), stop=(f == 1))
            last.then_inc(kc_mm, 1)
            pe.wait_ge(kc_ready, 1)
            pe.wait_ge(ada_out, 8)
            for qt in range(TT):
                for r in range(R):
                    dst = bank[6 + qt // 2][:, :].rearrange("p (g m n) -> p g m n", g=G, m=2 * R)
                    last = nc.tensor.matmul(dst[:, :, (qt % 2) * R + r, :], nqT[:, r, qt * P:(qt + 1) * P],
                                            kc2[:, :].rearrange("p (g n) -> p g n", g=G), start=True, stop=True)
            last.then_inc(cmp_qk, 1)

            def cmp_transposes():
                pe.wait_ge(cmp_p, 2)
                for g in range(G):
                    for qt in range(TT):
                        at = g * 256 + (qt % 2) * P
                        last = nc.tensor.transpose(bank[6 + g][:, qt * P:(qt + 1) * P],
                                                   p_cmp[:, qt // 2, at:at + P], ident[:, :])
                    last.then_inc(cmp_tr, 1)

            cmp_transposes()
            pe.wait_ge(parts_in, 48)
            pe.wait_ge(k_padded, 2)
            for j in range(20, 24):
                pe.wait_ge(*copied(j))

            def qk(t):
                kind, h, qt = TASKS[t]
                n = P * (qt + 1)
                if t >= 4:
                    pe.wait_ge(exp_done, t - 3)
                dst = bank[t % 4]
                if kind == "fox":
                    nc.tensor.matmul(dst[:, 0:n], fqT[:, h // 2, qt * P:(qt + 1) * P],
                                     (fkT, fk_odd)[h % 2][:, h // 2, 0:n], start=True, stop=False)
                    nc.tensor.matmul(dst[:, n - P:n], ident_b[:, :], causal_b[:, :], start=False, stop=False)
                    nc.tensor.matmul(dst[:, 0:n], ones_b[0:3, :], fox_parts[:, h, 0:n],
                                     start=False, stop=True).then_inc(qk_done, 1)
                else:
                    g, r = h // R, h % R
                    nc.tensor.matmul(dst[:, 0:n], nqT[:, r, qt * P:(qt + 1) * P],
                                     kvT[:, (0 if kind == "sel" else 1) + 2 * g, 0:n],
                                     start=True, stop=True).then_inc(qk_done, 1)

            def transposes(t):
                qt = TASKS[t][2]
                pe.wait_ge(exp_done, t + 1)
                pe.wait_ge(diag_ready, t + 1)
                if t >= 2:
                    pe.wait_ge(*pT_ready(t - 2))
                for kt in range(qt + 1):
                    last = nc.tensor.matmul(bank[4 + t % 2][:, kt * P:(kt + 1) * P],
                                            p_buf[t % 4][:, kt * P:(kt + 1) * P], diag[:, t % 4, :],
                                            start=True, stop=True)
                last.then_inc(tr_done, 1)

            def pv(w):
                kind, h, qt = TASKS[2 * w]
                u = h // 2 + (0 if kind == "fox" else H // 2)
                dst = bank[6 + u % 2]
                if w == 0:
                    pe.wait_ge(cmp_pT, 2)
                if w - 1 in LAST_PAIR and u >= 2:
                    pe.wait_ge(*heads_out(u - 2))
                if (w == 0 or w - 1 in LAST_PAIR) and kind != "fox":
                    for i in range(2):
                        at = DH * ((h + i) % R)
                        nc.tensor.matmul(dst[DH * i:DH * (i + 1), :], vc_diag[:, h // R, at:at + DH],
                                         p_cmpT[:, h // R, :], start=True, stop=False)
                for i in range(2):
                    pe.wait_ge(*pT_ready(2 * w + i))
                for kt in range(qt + 1):
                    for i in range(2):
                        if kind == "fox":
                            v = fv[:, kt, (h + i) * DH:(h + i + 1) * DH]
                        else:
                            at = (0 if kind == "sel" else 128) + DH * (h // R)
                            v = vsw[:, kt, at:at + DH]
                        last = nc.tensor.matmul(dst[DH * i:DH * (i + 1), qt * P:(qt + 1) * P], v,
                                                pT_buf[(2 * w + i) % 4][:, kt * P:(kt + 1) * P],
                                                start=(kind == "fox" and kt == 0),
                                                stop=(kt == qt and (kind == "fox" or w in LAST_PAIR)))
                last.then_inc(pv_done, 1)

            for t in range(NT + 4):
                if t < NT:
                    qk(t)
                if 3 <= t < NT + 3:
                    transposes(t - 3)
                if t >= 5 and t % 2 == 1:
                    pv((t - 5) // 2)
            for u in (H // 2 - 1, H - 1):
                pe.wait_ge(*heads_out(u))

            def mix(t):
                for c in range(2):
                    i = AT["out", c]
                    if t == 0:
                        arrived(i)
                    w = ring[:, i % RING, :].rearrange("p (k n) -> p k n", k=KD)
                    if t >= 2:
                        pe.wait_ge(mix_read, 2 * (t - 2) + c + 1)
                    for k in range(KD):
                        last = nc.tensor.matmul(bank[2 * (t % 2) + c][:, :], oT[:, k, t * P:(t + 1) * P], w[:, k, :],
                                                start=(k == 0), stop=(k == KD - 1))
                    last.then_inc(mix_mm, 1)

            def h2_tile(t):
                pe.wait_ge(h2_ready, t + 1)
                for half in range(2):
                    if t >= 1:
                        pe.wait_ge(h2T_act, 2 * (t - 1) + half + 1)
                    for k in range(4):
                        last = nc.tensor.transpose(bank[4 + half][:, k * P:(k + 1) * P],
                                                   h2_tok[t][:, (4 * half + k) * P:(4 * half + k + 1) * P], ident[:, :])
                    last.then_inc(h2T_mm, 1)

            def router(t):
                if t == 0:
                    pe.wait_ge(router_in, 16)
                pe.wait_ge(h2T_act, 2 * t + 2)
                for k in range(KD):
                    last = nc.tensor.matmul(bank[6][:, t * E:(t + 1) * E], h2T[:, k, t * P:(t + 1) * P],
                                            w_router_t[:, k, :], start=(k == 0), stop=(k == KD - 1))
                last.then_inc(router_mm, 1)

            mix(0)
            mix(1)
            for t in range(TT):
                h2_tile(t)
                if t + 2 < TT:
                    mix(t + 2)
                if t == TT - 3:
                    pe.wait_ge(mix_mm, 2 * TT)
                    nc.tensor.nop().then_inc(chunk_used, 2)
                router(t)

            def positions():
                pe.wait_ge(sel_ready, 1)
                pe.wait_ge(router_exp, 1)
                for t in range(TT):
                    for s in range(t):
                        nc.tensor.matmul(bank[7][:, t * E:(t + 1) * E], ones_b[:, :], r_selb[:, s, :],
                                         start=(s == 0), stop=False)
                    nc.tensor.matmul(bank[7][:, t * E:(t + 1) * E], before_b[:, :], r_selb[:, t, :],
                                     start=(t == 0), stop=True)
                for s in range(TT):
                    last = nc.tensor.matmul(bank[7][:, TT * E:(TT + 1) * E], ones_b[:, :], r_selb[:, s, :],
                                            start=(s == 0), stop=(s == TT - 1))
                last.then_inc(pos_mm, 1)

            i = AT["shared", 0]
            arrived(i)
            pe.wait_ge(mix_read, 2 * TT)
            w = ring[:, i % RING, :].rearrange("p (k n) -> p k n", k=KD)
            for t in range(TT):
                if t == 2:
                    positions()
                if t >= 2:
                    pe.wait_ge(sh_act_ready, t - 1)
                for k in range(KD):
                    last = nc.tensor.matmul(bank[t % 2][:, :], h2T[:, k, t * P:(t + 1) * P], w[:, k, :],
                                            start=(k == 0), stop=(k == KD - 1))
                last.then_inc(sh_gu, 1)
            pe.wait_ge(sh_gu, TT)
            nc.tensor.nop().then_inc(chunk_used, 1)
            pe.wait_ge(down_in[WS_SLOT], 16)
            wd = down[:, WS_SLOT, :].rearrange("p (f n) -> p f n", f=2)
            for t in range(TT):
                pe.wait_ge(sh_act_ready, t + 1)
                if t >= 1:
                    pe.wait_ge(sh_actT_ready, t)
                for f in range(2):
                    last = nc.tensor.transpose(bank[2][:, f * P:(f + 1) * P], sh_act[:, t, f * P:(f + 1) * P], ident[:, :])
                last.then_inc(sh_tr, 1)
                pe.wait_ge(sh_actT_ready, t + 1)
                if t >= 1:
                    pe.wait_ge(sh_y_ready, 2 * t)
                for c in range(2):
                    for f in range(2):
                        last = nc.tensor.matmul(bank[4 + c][:, :], sh_actT[:, f, 0:P], wd[:, f, c * 512:(c + 1) * 512],
                                                start=(f == 0), stop=(f == 1))
                last.then_inc(sh_down, 1)
                if t == 0:
                    pe.wait_ge(units_ready, 1)
                    nc.tensor.matmul(bank[7][0:1, 320:448], expert_u[:, 0:1], ident[:, :],
                                     start=True, stop=True).then_inc(units_row, 1)
                for k in range(TOP_K):
                    j = TOP_K * t + k
                    pe.wait_ge(hot_ready, j + 1)
                    nc.tensor.matmul(bank[6][:, 0:5 * UNITS], slot_hot[:, j % 4, :], unit_hot[:, j % 4, :],
                                     start=(j == 0), stop=(j == TT * TOP_K - 1)).then_inc(list_mm, 1)

            xe_banks = (bank[1], bank[2])

            def tokensT(n, u, i):
                pe.wait_ge(gather_in[u], 16 * (i + 1))
                for half in range(2):
                    for k in range(4):
                        last = nc.tensor.transpose(xe_banks[half][:, k * P:(k + 1) * P],
                                                   gathered[u][:, (4 * half + k) * P:(4 * half + k + 1) * P],
                                                   ident[:, :])
                last.then_inc(xe_tr, 1)

            def gate_up(n, u):
                expert = pe.value_load(unit_expert[0:1, bass.ds(n, 1)], min_val=0, max_val=E - 1)
                at = pe.value_load(unit_at[0:1, bass.ds(n, 1)], min_val=0, max_val=(RING - 1) * 2 * D)
                pe.wait_ge(weights_ready, expert + 1)
                pe.wait_ge(xe_act, n + 1)
                pe.wait_ge(xe_dve, n + 1)
                settle(pe)
                for k in range(KD):
                    last = nc.tensor.matmul(bank[0][:, :], gatheredT[u][:, k, :],
                                            ring_flat[:, bass.ds(at * 2 + k * 2 * F, 2 * F)],
                                            start=(k == 0), stop=(k == KD - 1))
                last.then_inc(gu_done, 1)

            def act_T(n):
                pe.wait_ge(act_done, n + 1)
                for f in range(2):
                    last = nc.tensor.transpose(bank[3][:, f * P:(f + 1) * P], e_act[:, f * P:(f + 1) * P], ident[:, :])
                last.then_inc(at_tr, 1)

            def down_mm(n, used):
                at = pe.value_load(unit_at[0:1, bass.ds(n, 1)], min_val=0, max_val=(RING - 1) * 2 * D)
                pe.wait_ge(at_ready, n + 1)
                if used:
                    pe.wait_ge(y_act, n)
                    pe.wait_ge(y_dve, n)
                settle(pe)
                for c in range(2):
                    for f in range(2):
                        last = nc.tensor.matmul(bank[4 + c][:, :], e_actT[:, f, :],
                                                down_flat[:, bass.ds(at + f * D + c * 512, 512)],
                                                start=(f == 0), stop=(f == 1))
                last.then_inc(down_done, 1)

            pe.wait_ge(tables_ready, 1)
            tokensT(0, 0, 0)
            gate_up(0, 0)
            tokensT(1, 1, 0)
            act_T(0)
            gate_up(1, 1)
            tokensT(2, 0, 1)
            pe.wait_ge(sh_y_ready, 2 * TT)
            down_mm(0, False)
            act_T(1)
            pairs = pe.value_load(expert_end[0:1, E:E + 1], min_val=E // 2, max_val=UNITS // 2 - 1)
            with pe.Fori(1, pairs) as i:
                gate_up(2 * i, 0)
                tokensT(2 * i + 1, 1, i)
                down_mm(2 * i - 1, True)
                act_T(2 * i)
                gate_up(2 * i + 1, 1)
                tokensT(2 * i + 2, 0, i + 1)
                down_mm(2 * i, True)
                act_T(2 * i + 1)
            down_mm(pe.value_load(expert_end[0:1, E + 1:E + 2], min_val=E - 1, max_val=UNITS - 1), True)

        @block.gpsimd
        def _(pool):
            steps = [0]

            def link(ins):
                steps[0] += 1
                ins.then_inc(pool_step, 1)
                pool.wait_ge(pool_step, steps[0])

            pool.dma_start(table_b[0:97, 0:NDIST], a["buckets"]).then_inc(table_in, 16)
            last_row = a["rel_bias"][NB - 1:NB, :]
            for q in range(3):
                pool.dma_start(c_stat[32 * q:32 * q + 32, 0, 0:H], a["rel_bias"]).then_inc(table_in, 16)
            pool.dma_start(c_stat[0:96, 1, 0:H], last_row.to_broadcast([96, H])).then_inc(table_in, 16)

            link(nc.gpsimd.memset(ident[:, :], 0.0))
            nc.gpsimd.affine_select(out=ident[:, :], in_=ident[:, :], compare_op=ALU.not_equal, fill=1.0, base=0,
                                    pattern=[[-1, P]], channel_multiplier=1).then_inc(ident_set, 1)
            link(nc.gpsimd.memset(ident_b[:, :], 0.0))
            nc.gpsimd.affine_select(out=ident_b[:, :], in_=ident_b[:, :], compare_op=ALU.not_equal, fill=1.0,
                                    base=0, pattern=[[-1, P]], channel_multiplier=1).then_inc(ident_set, 1)
            nc.gpsimd.memset(ones_b[:, :], 1.0)
            link(nc.gpsimd.memset(causal_b[:, :], 0.0))
            nc.gpsimd.affine_select(out=causal_b[:, :], in_=causal_b[:, :], compare_op=ALU.is_ge, fill=NEG, base=0,
                                    pattern=[[-1, P]], channel_multiplier=1)
            link(nc.gpsimd.memset(before_b[:, :], 0.0))
            nc.gpsimd.affine_select(out=before_b[:, :], in_=before_b[:, :], compare_op=ALU.is_ge, fill=1.0, base=0,
                                    pattern=[[-1, P]], channel_multiplier=1)
            nc.gpsimd.iota(row_no[:, :], pattern=[[0, 1]], base=0, channel_multiplier=1,
                           allow_small_or_imprecise_dtypes=True)
            nc.gpsimd.iota(iota_b[:, :], pattern=[[1, SLOTS]], base=0, channel_multiplier=0,
                           allow_small_or_imprecise_dtypes=True)
            link(nc.gpsimd.memset(tri, 1.0))
            link(nc.gpsimd.affine_select(out=tri, in_=tri, compare_op=ALU.is_ge, fill=0.0, base=0,
                                         pattern=[[1, S]], channel_multiplier=-1))
            nc.gpsimd.memset(down[:, 1, :], 0.0)
            nc.gpsimd.memset(p_cmp[:, :, :], 0.0).then_inc(masks_set, 1)

            for s in range(2):
                j = 14 + s
                pool.wait_ge(*copied(j))
                for half in range(2):
                    for g in range(G):
                        n = S - half
                        pool.dma_start(pair[s][half * DH:(half + 1) * DH, g, 0:n],
                                       kvT[g * DH:(g + 1) * DH, 2 + s, half:S]).then_inc(pair_in[s], 16)

            for s in range(2):
                pool.wait_ge(pair_in[s], 64)
            nc.gpsimd.memset(kvT[0:DH, 2:4, :], 0.0)
            link(nc.gpsimd.tensor_copy(kvT[DH:P, 2:4, :], kvT[DH:P, 0:2, :]))
            nc.gpsimd.memset(kvT[DH:P, 0:2, :], 0.0).then_inc(k_padded, 1)
            pool.wait_ge(xb_ready, 2)
            nc.gpsimd.memset(fk_odd[0:DH, :, :], 0.0)
            link(nc.gpsimd.tensor_copy(fk_odd[DH:P, :, :], fkT[DH:P, :, :]))
            nc.gpsimd.memset(fkT[DH:P, :, :], 0.0).then_inc(k_padded, 1)

            for i, part in enumerate((fox_split[:, 0:S], fox_split[:, S:2 * S], fox_lo)):
                pool.wait_ge(parts_ready, i + 1)
                pool.dma_start(fox_parts[i:i + 1, :, :], part).then_inc(parts_in, 16)

            for t in range(NT):
                kind, h, qt = TASKS[t]
                pool.wait_ge(inv_ready, t + 1)
                if t == 0:
                    pool.wait_ge(cmp_tr, 2)
                    pool.wait_ge(cmp_p, 2)
                if t >= 4:
                    pool.wait_ge(tr_done, t - 3)
                scale = inv_sum[:, t % 4:t % 4 + 1]
                if kind == "fox":
                    nc.gpsimd.tensor_scalar(diag[:, t % 4, :], ident[:, :], scale, None, ALU.mult)\
                        .then_inc(diag_ready, 1)
                else:
                    gi = 3 * h + (1 if kind == "sel" else 2)
                    nc.gpsimd.tensor_scalar(diag[:, t % 4, :], ident[:, :], scale, gates[:, qt, gi:gi + 1],
                                            ALU.mult, ALU.mult).then_inc(diag_ready, 1)

            pool.wait_ge(ln_in, 16)
            pool.wait_ge(ada_out, 8)
            link(nc.gpsimd.tensor_tensor(ln_tmp, ln_rows[:, 1, :], mod_rows[:, 2, :], ALU.mult))
            nc.gpsimd.tensor_tensor(mod_rows[:, 1, :], mod_rows[:, 1, :], ln_tmp, ALU.add).then_inc(rows_ready, 1)
            nc.gpsimd.tensor_tensor(mod_rows[:, 2, :], mod_rows[:, 2, :], ln_rows[:, 0, :], ALU.mult)\
                .then_inc(rows_ready, 1)
            for t in range(TT):
                pool.wait_ge(h2_ready, t + 1)
                pool.dma_start(h2_dram[t * P:(t + 1) * P, :], h2_tok[t]).then_inc(h2_stored, 16)
                link(nc.gpsimd.tensor_tensor(x_tok[:, t, :], x_tok[:, t, :], ln_rows[:, 0, :], ALU.mult))
                nc.gpsimd.tensor_tensor(x_tok[:, t, :], x_tok[:, t, :], ln_rows[:, 1, :], ALU.add).then_inc(x1_ready, 1)

            pool.wait_ge(x1_ready, TT)
            nc.gpsimd.memset(area_e[:, 0:2048], 0.0).then_inc(cleared, 1)
            pool.wait_ge(cleared, 1)
            pool.dma_start(ffn_dram[1].rearrange("(p t) d -> p t d", p=P),
                           area_e[:, 0:1024].rearrange("p (o d) -> p o d", o=1).to_broadcast([P, TT, D]))\
                .then_inc(scattered[1], 16)
            pool.wait_ge(scattered[1], 16)
            pool.wait_ge(h2_stored, 16 * TT)
            last_token = pool.to_reg(S - 1)

            def gather(n, u):
                if not (isinstance(n, int) and n < 2):
                    pool.wait_ge(xe_tr, n - 1)
                    settle(pool)
                nc.gpsimd.tensor_copy(idx_gather[u][:, :], slot_idx[:, bass.ds(n, 1)]).then_inc(idx_set, 1)
                pool.wait_ge(idx_set, n + 1)
                settle(pool)
                pool.indirect_dma_start(gathered[u], None, h2_dram[:, :],
                                        bass.IndirectOffsetOnAxis(ap=idx_gather[u][:, :], axis=0),
                                        bounds_check=last_token, oob_is_err=False).then_inc(gather_in[u], 16)

            def scatter(n, u, i):
                pool.wait_ge(y_act, n + 1)
                pool.wait_ge(y_dve, n + 1)
                if not (isinstance(i, int) and i + u == 0):
                    pool.wait_ge(scattered[u], 16 * (i + u))
                settle(pool)
                nc.gpsimd.tensor_copy(idx_scatter[u][:, :], slot_idx[:, bass.ds(n, 1)]).then_inc(idx_out, 1)
                pool.wait_ge(idx_out, n + 1)
                settle(pool)
                pool.indirect_dma_start(ffn_dram[u][:, :],
                                        bass.IndirectOffsetOnAxis(ap=idx_scatter[u][:, :], axis=0),
                                        y_out[u], None, bounds_check=last_token, oob_is_err=False,
                                        compute_op=ALU.add).then_inc(scattered[u], 16)

            pool.wait_ge(lists_ready, 1)
            gather(0, 0)
            gather(1, 1)
            gather(2, 0)
            gather(3, 1)
            for stored_rows in ffn_started:
                pool.wait_ge(stored_rows, 8 * TT)
            scatter(0, 0, 0)
            pool.wait_ge(tables_ready, 1)
            pairs = pool.value_load(expert_end[0:1, E:E + 1], min_val=E // 2, max_val=UNITS // 2 - 1)
            with pool.Fori(1, pairs) as i:
                gather(2 * i + 2, 0)
                scatter(2 * i - 1, 1, i - 1)
                gather(2 * i + 3, 1)
                scatter(2 * i, 0, i)
            scatter(2 * pairs - 1, 1, pairs - 1)
            pool.wait_ge(gather_in[0], 16 * (pairs + 1))
            pool.wait_ge(gather_in[1], 16 * (pairs + 1))
            pool.wait_ge(scattered[0], 16 * pairs)
            pool.wait_ge(scattered[1], 16 * (pairs + 1))
            settle(pool)
            for t in range(TT):
                for i in range(2):
                    pool.dma_start(ffn_tok[i][:, t, :], ffn_dram[i][t * P:(t + 1) * P, :]).then_inc(ffn_in[t], 16)
            for t in range(TT):
                pool.wait_ge(x2_ready, t + 1)
                pool.dma_start(out[t * P:(t + 1) * P, :], x_tok[:, t, :]).then_inc(stored, 16)
            pool.wait_ge(stored, 16 * TT)

        @block.vector
        def _(dve):
            steps = [0]

            def link(ins):
                steps[0] += 1
                ins.then_inc(dve_step, 1)
                dve.wait_ge(dve_step, steps[0])

            v = nc.vector
            dve.wait_ge(table_in, 80)
            d0 = c_stat[0:96, 0, 0:H]
            d1 = c_stat[0:96, 1, 0:H]
            d2 = c_stat[0:96, 2, 0:H]
            hi = rel_parts[0:96, :]
            link(v.tensor_tensor(d0, d0, d1, ALU.subtract))
            link(v.tensor_copy(hi, d0))
            link(v.tensor_tensor(d1, d0, hi, ALU.subtract))
            link(v.tensor_copy(rel_parts[32:64, :], d1[32:64, :]))
            link(v.tensor_copy(rel_parts[64:96, :], d1[64:96, :]))
            link(v.tensor_tensor(d2[64:96, :], d1[64:96, :], rel_parts[64:96, :], ALU.subtract))
            link(v.tensor_copy(rel_parts[64:96, :], d2[64:96, :]))
            v.memset(rel_parts[96:97, :], NEG).then_inc(rel_set, 1)

            dve.wait_ge(c_exp, 1)
            link(v.tensor_scalar(sc_col[:, 0, :], sc_col[:, 0, :], 1.0, None, ALU.add))
            link(v.reciprocal(sc_col[:, 1, :], sc_col[:, 0, :]))
            v.tensor_tensor(sc_col[:, 2, :], c_col[:, :], sc_col[:, 1, :], ALU.mult).then_inc(c_ready, 1)

            def ada_chunk(c):
                i = AT["ada", c]
                dve.wait_ge(slot_in[i % RING], 16 * (i // RING + 1))
                if c >= 2:
                    dve.wait_ge(ada_mm, c - 1)
                w = ring[:, i % RING, :].rearrange("p (k n) -> p k n", k=KD)
                total = ada_sum[c % 2]
                link(v.tensor_scalar(total, w[:, 0, :], sc_col[:, 2, 0:1], None, ALU.mult))
                for k in range(1, KD):
                    step = v.scalar_tensor_tensor(total, w[:, k, :], sc_col[:, 2, k:k + 1], total, ALU.mult, ALU.add)
                    if k < KD - 1:
                        link(step)
                step.then_inc(ada_part, 1)

            def bias_tables(half):
                if half == 0:
                    for b in range(4):
                        dve.wait_ge(bias_mm, b + 1)
                        v.tensor_copy(bias_w[:, :, 64 * b:64 * b + 64],
                                      bank[b][:, :].rearrange("p (j h) -> p h j", h=H)).then_inc(bias_out, 1)
                else:
                    for t in range(TT):
                        dve.wait_ge(bias_mm, 4 + t + 1)
                        v.tensor_copy(bias_c[:, t, :, 0:NCMP],
                                      bank[4 + t][:, 0:8 * NCMP].rearrange("p (n h) -> p h n", h=H))\
                            .then_inc(bias_out, 1)

            dve.wait_ge(c_ready, 1)
            ada_chunk(0)
            bias_tables(0)
            ada_chunk(1)
            bias_tables(1)
            ada_chunk(2)
            ada_chunk(3)

            dve.wait_ge(ada_mm, 4)
            dve.wait_ge(consts_in, 80)
            link(v.tensor_tensor(mod_col[:, :], bank[0][:, 0:16], ada_b_col[:, :], ALU.add))
            v.tensor_scalar(mod_col[:, 8:16], mod_col[:, 8:16], 1.0, None, ALU.add).then_inc(mod_ready, 1)
            dve.wait_ge(mod_ready, 1)
            dve.wait_ge(xT_in, 16)
            for k in range(KD):
                last = v.tensor_scalar(h1T[:, k, :], h1T[:, k, :], mod_col[:, 8 + k:9 + k], mod_col[:, k:k + 1],
                                       ALU.mult, ALU.add)
            last.then_inc(h1_ready, 1)

            def ada_rows(c):
                dve.wait_ge(ada_mm, 4 + c + 1)
                if c == 0:
                    dve.wait_ge(modb_in, 16)
                dst = mod_rows[:, c // 2, (c % 2) * 512:(c % 2) * 512 + 512]
                v.scalar_tensor_tensor(dst, bank[6 + c % 2][:, :], 1.0 if c // 2 == 2 else 0.0, dst,
                                       ALU.add, ALU.add).then_inc(ada_out, 1)

            for j in range(1, 16, 2):
                dve.wait_ge(job_mm, j + 1)
                dst = [fqT, fkT, nqT, kvT][j // 4][:, j % 4, :]
                v.tensor_scalar(dst, bank[j % 4][:, :], SCALE if j // 4 in (0, 2) else 1.0, None, ALU.mult)\
                    .then_inc(job_dve, 1)
                if j == 3:
                    ada_chunk(4)
                if j == 7:
                    ada_rows(0)
                    ada_chunk(5)
                if j == 11:
                    ada_rows(1)
                    ada_chunk(6)
                if j == 15:
                    ada_rows(2)
                    ada_chunk(7)
                    ada_chunk(8)

            def build_xb(s):
                dve.wait_ge(pair_in[s], 64)
                dve.wait_ge(masks_set, 1)
                dst = xb[s].rearrange("p (j m) -> p j m", j=16)[:, :, 0:G * NCMP].rearrange("p j (g n) -> p j g n", g=G)
                for g in range(G):
                    src = pair[s][:, g, :].rearrange("p (n j two) -> p j n two", j=8, two=2)
                    for part in range(2):
                        last = v.tensor_tensor(dst[:, 8 * part:8 * part + 8, g, :], src[:, :, part:part + NCMP, 0],
                                               pos2[:, s, 8 * part:8 * part + 8].rearrange("p (j o) -> p j o", o=1)
                                               .to_broadcast([P, 8, NCMP]), ALU.add)
                last.then_inc(xb_ready, 1)

            for j in range(17, 24, 2):
                dve.wait_ge(job_mm, j + 1)
                if j < 20:
                    v.tensor_copy(fv[:, j - 16, :], bank[j % 4][:, :]).then_inc(job_dve, 1)
                else:
                    v.tensor_copy(ffng[:, j - 20, :], bank[j % 4][:, 256:288]).then_inc(ffng_act, 1)
                    v.tensor_copy(vsw[:, j - 20, :], bank[j % 4][:, 0:256]).then_inc(job_dve, 1)
                if j == 17:
                    ada_rows(3)
                    ada_chunk(9)
                    build_xb(0)
                if j == 19:
                    ada_rows(4)
                    build_xb(1)
                    ada_chunk(10)
                if j == 21:
                    ada_rows(5)
                    ada_chunk(11)
                if j == 23:
                    ada_rows(6)

            dve.wait_ge(ffng_act, TT)
            link(v.tensor_tensor(fx[:, 0, :, :], ffng[:, :, 0:H],
                                 bf_row[:, :].rearrange("p (o h) -> p o h", o=1).to_broadcast([P, TT, H]), ALU.add))
            link(v.tensor_scalar(fx[:, 2, :, :], fx[:, 0, :, :], -1.0, 0.0, ALU.mult, ALU.max))
            v.scalar_tensor_tensor(fx[:, 1, :, :], fx[:, 2, :, :], 2.0, fx[:, 0, :, :], ALU.mult, ALU.add)\
                .then_inc(fx_ready, 1)
            dve.wait_ge(fx_ready, 3)
            v.tensor_tensor(fx[:, 2, :, :], fx[:, 2, :, :], fx[:, 1, :, :], ALU.add).then_inc(fx_ready, 1)
            link(v.tensor_scalar(gates[:, :, :], gates[:, :, :], 1.0, None, ALU.add))
            link(v.reciprocal(gates[:, :, :], gates[:, :, :]))
            g0 = gates[:, 0, :].rearrange("p (h b) -> p h b", b=3)[:, :, 0]
            dve.wait_ge(ident_set, 1)
            link(v.tensor_reduce(early[:, :], ident[:, 31:P], AX, ALU.add))
            link(v.tensor_scalar(g0, g0, early[:, :], None, ALU.mult))

            dve.wait_ge(hid_exp, 1)
            link(v.tensor_scalar(hid_e, hid_e, 1.0, None, ALU.add))
            link(v.reciprocal(hid_e, hid_e))
            v.tensor_tensor(hid, bank[4][:, 0:256], hid_e, ALU.mult).then_inc(hid_ready, 1)
            dve.wait_ge(hidT_mm, 1)
            v.tensor_copy(hidT, bank[4][:, 256:512].rearrange("p (f m) -> p f m", f=2)).then_inc(hidT_ready, 1)

            dve.wait_ge(cum_mm, 1)
            link(v.tensor_copy(fox_sum, bank[5][0:H, :]))
            link(v.tensor_copy(fox_split[:, 0:S], fox_sum))
            v.tensor_tensor(fox_rest, fox_sum, fox_split[:, 0:S], ALU.subtract).then_inc(parts_ready, 1)
            dve.wait_ge(parts_ready, 1)
            link(v.tensor_copy(fox_split[:, S:2 * S], fox_rest))
            v.tensor_tensor(fox_rest, fox_rest, fox_split[:, S:2 * S], ALU.subtract).then_inc(parts_ready, 1)
            dve.wait_ge(parts_ready, 2)
            v.tensor_copy(fox_lo, fox_rest).then_inc(parts_ready, 1)

            ada_rows(7)
            v.memset(vc_diag, 0.0)
            link(v.memset(kc2[:, :], 0.0))
            dve.wait_ge(kc_mm, 1)
            for g in range(G):
                v.tensor_copy(kc2[g * DH:(g + 1) * DH, 32 * g:32 * g + NCMP], bank[4][g * DH:(g + 1) * DH, 0:NCMP])
            for r in range(R):
                last = v.tensor_copy(vc_diag[32 * r:32 * r + NCMP, :, r * DH:(r + 1) * DH],
                                     bank[4][32 * r:32 * r + NCMP, 64:64 + 2 * DH].rearrange("p (g d) -> p g d", g=G))
            last.then_inc(kc_ready, 1)
            dve.wait_ge(cmp_qk, 1)
            s0 = c_stat[:, 0, :]
            s1 = c_stat[:, 1, :]

            def spread(st):
                return st.rearrange("p (m o) -> p m o", o=1).to_broadcast([P, 16, NCMP])

            for i in range(2):
                probs = p_cmp[:, i, :].rearrange("p (m n) -> p m n", m=16)[:, :, 0:NCMP]
                for g in range(G):
                    logits = bank[6 + i][:, 256 * g:256 * g + 256].rearrange("p (t r n) -> p t r n", t=2, r=R)
                    sums = p_cmp[:, i, 256 * g:256 * g + 256].rearrange("p (t r n) -> p t r n", t=2, r=R)
                    last = v.tensor_tensor(sums[:, :, :, 0:NCMP], logits[:, :, :, 0:NCMP],
                                           bias_c[:, 2 * i:2 * i + 2, g * R:(g + 1) * R, 0:NCMP], ALU.add)
                link(last)
                link(v.tensor_reduce(s0, probs, AX, ALU.max))
                v.tensor_tensor(probs, probs, spread(s0), ALU.subtract).then_inc(cmp_max, 1)
                dve.wait_ge(cmp_max, i + 1)
            for i in range(2):
                probs = p_cmp[:, i, :].rearrange("p (m n) -> p m n", m=16)[:, :, 0:NCMP]
                dve.wait_ge(cmp_exp, i + 1)
                link(v.tensor_reduce(s0, probs, AX, ALU.add))
                link(v.reciprocal(s1, s0))
                for g in range(G):
                    gate = gates[:, 2 * i:2 * i + 2, :].rearrange("p t (h b) -> p t h b", b=3)[:, :, g * R:(g + 1) * R, 0]
                    sg = s1[:, 8 * g:8 * g + 8].rearrange("p (t r) -> p t r", t=2)
                    last = v.tensor_tensor(sg, sg, gate, ALU.mult)
                link(last)
                v.tensor_tensor(probs, probs, spread(s1), ALU.mult).then_inc(cmp_p, 1)
                dve.wait_ge(cmp_p, i + 1)

            def max_task(t):
                kind, h, qt = TASKS[t]
                n = P * (qt + 1)
                b = bank[t % 4]
                dve.wait_ge(qk_done, t + 1)
                nm = nmax[:, t % 4:t % 4 + 1]
                if kind == "fox":
                    v.tensor_reduce(nm, b[:, 0:n], AX, ALU.max, negate=True).then_inc(max_done, 1)
                    return
                near = min(n, 256)
                link(v.tensor_tensor(b[:, n - near:n], b[:, n - near:n], bias_w[:, h, 256 - near:256], ALU.add))
                v.tensor_reduce(nm, b[:, 0:n], AX, ALU.max, negate=True).then_inc(max_done, 1)

            def copy_pT(t):
                n = P * (TASKS[t][2] + 1)
                dve.wait_ge(tr_done, t + 1)
                if t == 0:
                    dve.wait_ge(hid_mm, 1)
                if t >= 4:
                    dve.wait_ge(pv_done, (t - 4) // 2 + 1)
                v.tensor_copy(pT_buf[t % 4][:, 0:n], bank[4 + t % 2][:, 0:n]).then_inc(pT_dve, 1)

            def invert_sum(t):
                dve.wait_ge(exp_done, t + 1)
                if t >= 4:
                    dve.wait_ge(diag_ready, t - 3)
                v.reciprocal(inv_sum[:, t % 4:t % 4 + 1], rowsum[:, t % 4:t % 4 + 1]).then_inc(inv_ready, 1)

            for t in range(NT + 7):
                if t < NT:
                    max_task(t)
                if 1 <= t <= NT:
                    invert_sum(t - 1)
                if 3 <= t < NT + 3 and t - 3 < FIRST_NSA:
                    copy_pT(t - 3)
                for u in range(H // 2, H):
                    if t == 2 * LAST_PAIR[u] + 6:
                        dve.wait_ge(pv_done, LAST_PAIR[u] + 1)
                        v.tensor_copy(oT[:, u, :], bank[6 + u % 2][:, :]).then_inc(o_dve, 1)

            def normalise(t, n):
                x = x_tok[:, t, :]
                for i in range(2):
                    last = v.bn_stats(ln_stats[:, 6 * i:6 * i + 6], x[:, 512 * i:512 * i + 512])
                link(last)
                link(v.bn_aggr(ln_mv[:, :], ln_stats[:, :]))
                v.tensor_scalar(ln_r[:, 0:1], ln_mv[:, 1:2], EPS, None, ALU.add).then_inc(var_ready, 1)
                dve.wait_ge(rstd_ready, n)
                link(v.tensor_scalar(x, x, ln_mv[:, 0:1], ln_r[:, 1:2], ALU.subtract, ALU.mult))

            dve.wait_ge(x_in, 16)
            dve.wait_ge(ln_in, 16)
            dve.wait_ge(rows_ready, 1)
            for t in range(TT):
                for c in range(2):
                    dve.wait_ge(mix_mm, 2 * t + c + 1)
                    last = v.tensor_tensor(ln_tmp[:, c * 512:(c + 1) * 512], bank[2 * (t % 2) + c][:, :],
                                           mod_rows[:, 0, c * 512:(c + 1) * 512], ALU.mult)
                    last.then_inc(mix_read, 1)
                dve.wait_ge(mix_read, 2 * t + 2)
                link(v.scalar_tensor_tensor(x_tok[:, t, :], x_tok[:, t, :], ALPHA, ln_tmp, ALU.mult, ALU.add))
                normalise(t, t + 1)
                if t == 0:
                    dve.wait_ge(rows_ready, 2)
                link(v.tensor_tensor(h2_tok[t], x_tok[:, t, :], mod_rows[:, 2, :], ALU.mult))
                v.tensor_tensor(h2_tok[t], h2_tok[t], mod_rows[:, 1, :], ALU.add).then_inc(h2_ready, 1)

            def shared_act(t):
                dve.wait_ge(sh_silu, t + 1)
                v.tensor_tensor(sh_act[:, t, :], sh_sil[:, t % 2, :], bank[t % 2][:, F:2 * F], ALU.mult)\
                    .then_inc(sh_act_ready, 1)

            dve.wait_ge(h2_stored, 16 * TT)
            dve.wait_ge(h2T_mm, 2 * TT)
            dve.wait_ge(router_exp, 1)
            link(v.tensor_scalar(r_score, r_score, 1.0, None, ALU.add))
            link(v.reciprocal(r_score, r_score))
            link(v.tensor_tensor(r_bias, r_score,
                                 e_bias_row[:, :].rearrange("p (o e) -> p o e", o=1).to_broadcast([P, TT, E]), ALU.add))
            for t in range(TT):
                for g in range(EG):
                    last = v.max(r_top[:, t, g, :], r_bias[:, t, 8 * g:8 * g + 8])
            link(last)
            link(v.tensor_tensor(r_group, r_top[:, :, :, 0], r_top[:, :, :, 1], ALU.add))
            mine = r_group.rearrange("p t (g o) -> p t g o", o=1).to_broadcast([P, TT, EG, EG])
            other = r_group.rearrange("p t (o g) -> p t o g", o=1).to_broadcast([P, TT, EG, EG])
            link(v.tensor_tensor(r_gt, other, mine, ALU.is_gt))
            link(v.tensor_tensor(r_eq, other, mine, ALU.is_equal))
            for g in range(1, EG):
                last = v.tensor_tensor(r_gt[:, :, g, 0:g], r_gt[:, :, g, 0:g], r_eq[:, :, g, 0:g], ALU.add)
            link(last)
            link(v.tensor_reduce(r_rank, r_gt, AX, ALU.add))
            link(v.tensor_scalar(r_gmask, r_rank, TOPK_GROUPS - 0.5, None, ALU.is_lt))
            gm = r_gmask.rearrange("p t (g o) -> p t g o", o=1).to_broadcast([P, TT, EG, EG])
            mk = r_masked.rearrange("p t (g e) -> p t g e", g=EG)
            link(v.tensor_tensor(mk, r_bias.rearrange("p t (g e) -> p t g e", g=EG), gm, ALU.mult))
            link(v.tensor_scalar(r_rank, r_gmask, -1.0, -NEG, ALU.add, ALU.mult))
            link(v.tensor_tensor(mk, mk, r_rank.rearrange("p t (g o) -> p t g o", o=1).to_broadcast([P, TT, EG, EG]),
                                 ALU.add))
            for t in range(TT):
                last = v.max(r_best[:, t, :], r_masked[:, t, :])
            link(last)
            for t in range(TT):
                last = v.match_replace(r_sel[:, t, :], r_best[:, t, :], r_masked[:, t, :], 3e38)
            link(last)
            link(v.tensor_scalar(r_sel, r_sel, 2e38, None, ALU.is_gt))
            v.tensor_copy(r_selb, r_sel).then_inc(sel_ready, 1)
            shared_act(0)
            shared_act(1)
            link(v.tensor_tensor(r_gate, r_sel, r_score, ALU.mult))
            link(v.tensor_reduce(r_den, r_gate, AX, ALU.add))
            link(v.reciprocal(r_den, r_den))
            link(v.tensor_scalar(r_den, r_den, ROUTED_SCALE, None, ALU.mult))
            for t in range(TT):
                last = v.tensor_scalar(r_gate[:, t, :], r_gate[:, t, :], r_den[:, t:t + 1], None, ALU.mult)
            link(last)
            link(v.memset(zeros_e, 0.0))
            for t in range(TT):
                last = v.tensor_tensor_scan(r_kidx[:, t, :], r_sel[:, t, :], zeros_e, 0.0, ALU.add, ALU.add)
            link(last)
            link(v.tensor_tensor(r_kidx, r_kidx, r_sel, ALU.mult))
            shared_act(2)
            shared_act(3)
            dve.wait_ge(pos_mm, 1)
            count = bank[7][:, TT * E:(TT + 1) * E]
            link(v.tensor_scalar(n_units, count, SLOTS + 0.5, 1.0, ALU.is_gt, ALU.add))
            for i in range(2, TT):
                link(v.scalar_tensor_tensor(n_units, count, i * SLOTS + 0.5, n_units, ALU.is_gt, ALU.add))
            link(v.tensor_tensor_scan(unit_end, n_units, zeros_e, 0.0, ALU.add, ALU.add))
            link(v.tensor_tensor(n_units, unit_end, n_units, ALU.subtract))
            first = n_units.rearrange("p (o e) -> p o e", o=1).to_broadcast([P, TT, E])
            link(v.scalar_tensor_tensor(pos_m, first, float(SLOTS), bank[7][:, 0:TT * E].rearrange("p (t e) -> p t e", t=TT),
                                        ALU.mult, ALU.add))
            link(v.tensor_scalar(zeros_e, unit_end, row_no[:, :], None, ALU.is_le))
            link(v.tensor_reduce(expert_u[:, 1:2], zeros_e, AX, ALU.add))
            v.tensor_scalar(expert_u[:, 0:1], expert_u[:, 1:2], E - 1.0, None, ALU.min).then_inc(units_ready, 1)
            for k in range(TOP_K):
                v.scalar_tensor_tensor(r_pick[0], r_kidx, k + 1.0, pos_m, ALU.is_equal, ALU.mult)
                link(v.scalar_tensor_tensor(r_pick[1], r_kidx, k + 1.0, r_gate, ALU.is_equal, ALU.mult))
                v.tensor_reduce(slot_k[:, :, k], r_pick[0], AX, ALU.add)
                link(v.tensor_reduce(gate_k[:, :, k], r_pick[1], AX, ALU.add))
            link(v.tensor_copy(slot_ki, slot_k))
            link(v.tensor_scalar(unit_ki, slot_ki, SLOT_BITS, None, ALU.arith_shift_right))
            v.tensor_copy(unit_k, unit_ki)
            link(v.tensor_scalar(slot_ki, slot_ki, SLOTS - 1, None, ALU.bitwise_and))
            v.tensor_copy(slot_k, slot_ki)
            for i in range(2):
                link(v.tensor_copy(part_b, gate_k))
                link(v.tensor_copy(gate_parts[:, i, :, :], part_b))
                link(v.tensor_tensor(gate_k, gate_k, gate_parts[:, i, :, :], ALU.subtract))
            link(v.tensor_copy(gate_parts[:, 2, :, :], gate_k))
            for t in range(TT):
                for k in range(TOP_K):
                    j = TOP_K * t + k
                    b = j % 4
                    if j >= 4:
                        dve.wait_ge(list_mm, j - 3)
                    v.tensor_scalar(slot_hot[:, b, :], iota_b[:, :], slot_k[:, t, k:k + 1], None, ALU.is_equal)
                    values = [row_no[:, :], t * P - OUT_OF_RANGE] + [gate_parts[:, i, t, k:k + 1] for i in range(3)]
                    for c, value in enumerate(values):
                        last = v.tensor_scalar(unit_hot[:, b, c * UNITS:(c + 1) * UNITS], iota_b[:, 0:UNITS],
                                               unit_k[:, t, k:k + 1], value, ALU.is_equal, ALU.mult)
                    last.then_inc(hot_ready, 1)
                if t == 0:
                    dve.wait_ge(units_row, 1)
                    row = bank[7][0:1, 320:448]
                    v.tensor_copy(unit_expert, row)
                    link(v.tensor_scalar(unit_at, row, float(len(CHUNKS)), None, ALU.add))
                    v.tensor_scalar(unit_at, unit_at, RING - 1, DOWN_BITS, ALU.bitwise_and, ALU.logical_shift_left)
                    v.tensor_copy(expert_end[:, 0:E], unit_end[0:1, :])
                    link(v.tensor_scalar(expert_end[:, E:E + 1], unit_end[0:1, E - 1:E], 1.0, None, ALU.add))
                    link(v.tensor_scalar(expert_end[:, E:E + 1], expert_end[:, E:E + 1], 1, None,
                                         ALU.arith_shift_right))
                    v.tensor_scalar(expert_end[:, E + 1:E + 2], expert_end[:, E:E + 1], 2.0, -1.0,
                                    ALU.mult, ALU.add).then_inc(tables_ready, 1)
            dve.wait_ge(list_mm, TT * TOP_K)
            dve.wait_ge(scattered[1], 16)
            link(v.tensor_copy(list_sum, bank[6][:, 0:5 * UNITS]))
            part = [list_sum[:, c * UNITS:(c + 1) * UNITS] for c in range(5)]
            link(v.tensor_tensor(part[2], part[2], part[3], ALU.add))
            v.tensor_tensor(slot_gate[:, :], part[2], part[4], ALU.add)
            v.scalar_tensor_tensor(slot_idx[:, :], part[0], OUT_OF_RANGE, part[1], ALU.add, ALU.add)\
                .then_inc(lists_ready, 1)

            def copy_xT(n, u):
                dve.wait_ge(xe_tr, n + 1)
                v.tensor_copy(gatheredT[u % 2][:, 4:8, :], bank[2][:, :].rearrange("p (k m) -> p k m", k=4))\
                    .then_inc(xe_dve, 1)

            def copy_y(n, u, i):
                dve.wait_ge(down_done, n + 1)
                if isinstance(i, int) and i == 0:
                    for stored_rows in ffn_started:
                        dve.wait_ge(stored_rows, 8 * TT)
                else:
                    dve.wait_ge(scattered[u], 16 * (i + u))
                v.tensor_copy(y_out[u][:, 512:1024], bank[5][:, :]).then_inc(y_dve, 1)

            def activation(n):
                dve.wait_ge(silu_done, n + 1)
                settle(dve)
                v.scalar_tensor_tensor(e_act, bank[0][:, F:2 * F], slot_gate[:, bass.ds(n, 1)], silu_g,
                                       ALU.mult, ALU.mult).then_inc(act_done, 1)

            def copy_aT(n):
                dve.wait_ge(at_tr, n + 1)
                v.tensor_copy(e_actT, bank[3][:, 0:F].rearrange("p (i f) -> p i f", i=2)).then_inc(at_ready, 1)

            copy_xT(0, 0)
            activation(0)
            copy_xT(1, 1)
            copy_aT(0)
            activation(1)
            copy_xT(2, 0)
            copy_y(0, 0, 0)
            copy_aT(1)
            dve.wait_ge(tables_ready, 1)
            pairs = dve.value_load(expert_end[0:1, E:E + 1], min_val=E // 2, max_val=UNITS // 2 - 1)
            with dve.Fori(1, pairs) as i:
                activation(2 * i)
                copy_xT(2 * i + 1, 1)
                copy_y(2 * i - 1, 1, i - 1)
                copy_aT(2 * i)
                activation(2 * i + 1)
                copy_xT(2 * i + 2, 0)
                copy_y(2 * i, 0, i)
                copy_aT(2 * i + 1)
            copy_y(2 * pairs - 1, 1, pairs - 1)

            for t in range(TT):
                dve.wait_ge(ffn_in[t], 32)
                y = ffn_tok[0][:, t, :]
                link(v.tensor_tensor(y, y, ffn_tok[1][:, t, :], ALU.add))
                link(v.tensor_tensor(y, y, mod_rows[:, 3, :], ALU.mult))
                link(v.scalar_tensor_tensor(x_tok[:, t, :], x_tok[:, t, :], ALPHA, y, ALU.mult, ALU.add))
                normalise(t, TT + t + 1)
                x = x_tok[:, t, :]
                link(v.tensor_tensor(x, x, ln_rows[:, 2, :], ALU.mult))
                v.tensor_tensor(x, x, ln_rows[:, 3, :], ALU.add).then_inc(x2_ready, 1)


def bucket_table(np):
    dist = np.arange(NDIST) - DIST0
    n = np.maximum(dist, 0)
    exact = NB // 2
    nf = np.maximum(n, 1).astype(np.float32)
    large = exact + (np.log(nf / np.float32(exact)) / np.float32(np.log(128 / exact)) * (NB - exact)).astype(np.int32)
    bucket = np.where(n < exact, n, np.minimum(large, NB - 1))
    table = np.zeros((97, NDIST), np.float32)
    for part in range(3):
        table[NB * part + bucket[dist >= 0], np.nonzero(dist >= 0)[0]] = 1.0
    table[96, dist < 0] = 1.0
    return table


def kernel(x, c, w_ada, b_ada, w_in, b_f, cmp_pos_k, cmp_w1_k, cmp_w2_k, cmp_pos_v, cmp_w1_v, cmp_w2_v,
           rel_bias, w_out, ln1_g, ln1_b, w_router, e_bias, w_gate, w_up, w_down,
           ws_gate, ws_up, ws_down, ln2_g, ln2_b):
    import numpy as np
    import concourse.bacc as bacc
    from concourse.bass_utils import run_bass_kernel_spmd

    def rows(w):
        w = np.asarray(w)
        return np.ascontiguousarray(w.reshape(w.shape[0] // P, P, w.shape[1]).transpose(1, 0, 2))

    def chunks(w):
        w = np.asarray(w)
        n = w.shape[1] // CW
        return np.ascontiguousarray(w.reshape(KD, P, n, CW).transpose(2, 1, 0, 3)).reshape(n, P, KD * CW)

    xs = np.asarray(x)[0]
    widths = (512, 512, 512, 8, 512, 128, 128, 128, 128, 128, 128, 24)
    at = np.cumsum((0,) + widths)
    fq, fk, fv, ff, nq, kc, vc, ksl, vsl, kwn, vwn, ng = (np.asarray(w_in)[0][:, at[i]:at[i + 1]] for i in range(12))
    nq = nq.reshape(D, G, R, DH).transpose(0, 2, 1, 3).reshape(D, 512)
    wg, wu, wd = np.asarray(w_gate)[0], np.asarray(w_up)[0], np.asarray(w_down)[0]
    gu = np.empty((E, P, KD, 2, F), np.float32)
    gu[:, :, :, 0] = wg.reshape(E, KD, P, F).transpose(0, 2, 1, 3)
    gu[:, :, :, 1] = wu.reshape(E, KD, P, F).transpose(0, 2, 1, 3)
    ba = np.asarray(b_ada)[0]
    pos = np.stack([np.asarray(p)[0].reshape(16, P).T for p in (cmp_pos_k, cmp_pos_v)], axis=1)
    arrays = {
        "xT": rows(xs.T).reshape(P, KD * S),
        "x_tok": np.ascontiguousarray(xs.reshape(TT, P, D).transpose(1, 0, 2)),
        "c_col": np.ascontiguousarray(np.asarray(c)[0].reshape(KD, P).T),
        "w_ada": chunks(np.asarray(w_ada)[0]),
        "ada_b_col": np.ascontiguousarray(ba[0:2 * D].reshape(16, P).T),
        "ada_b_row": np.ascontiguousarray(ba[2 * D:].reshape(1, 4 * D)),
        "w_in": chunks(np.concatenate([fq, fk, nq, ksl, kwn, kc, vc, fv], axis=1)),
        "w_small": rows(np.concatenate([vsl, vwn, ff, ng], axis=1)).reshape(P, KD * WS_SMALL),
        "b_f": np.asarray(b_f).reshape(1, H),
        "w_cmp1": np.stack([rows(np.asarray(w)[0]).reshape(P, 16 * CMPH) for w in (cmp_w1_k, cmp_w1_v)]),
        "w_cmp2": np.stack([rows(np.asarray(w)[0]) for w in (cmp_w2_k, cmp_w2_v)], axis=1),
        "cmp_pos": np.ascontiguousarray(pos),
        "rel_bias": np.asarray(rel_bias),
        "buckets": bucket_table(np),
        "w_out": chunks(np.asarray(w_out)[0]),
        "ln_rows": np.concatenate([np.asarray(r)[0] for r in (ln1_g, ln1_b, ln2_g, ln2_b)]).reshape(1, 4 * D),
        "w_router": rows(np.asarray(w_router)[0]),
        "e_bias": np.asarray(e_bias).reshape(1, E),
        "w_gu": gu.reshape(E, P, KD * 2 * F),
        "w_d": np.ascontiguousarray(wd.reshape(E, 2, P, D).transpose(0, 2, 1, 3)).reshape(E, P, 2 * D),
        "ws_gu": chunks(np.concatenate([np.asarray(ws_gate)[0], np.asarray(ws_up)[0]], axis=1)),
        "ws_d": rows(np.asarray(ws_down)[0]).reshape(P, 2 * D),
    }
    nc = bacc.Bacc("TRN2", target_bir_lowering=False, num_devices=1)
    ins = {n: nc.dram_tensor(f"in_{n}", v.shape, F32, kind="ExternalInput").ap() for n, v in arrays.items()}
    out = nc.dram_tensor("out_x", (S, D), F32, kind="ExternalOutput").ap()
    build(nc, ins, out)
    r = run_bass_kernel_spmd(nc, [{f"in_{n}": v for n, v in arrays.items()}], core_ids=[0])
    return r.results[0]["out_x"].reshape(1, S, D)
```

```python
from contextlib import ExitStack

import concourse.bass as bass
from concourse import mybir

F32 = mybir.dt.float32
BF16 = mybir.dt.bfloat16
I32 = mybir.dt.int32
U32 = mybir.dt.uint32
ALU = mybir.AluOpType
ACT = mybir.ActivationFunctionType
AX = mybir.AxisListType.X

P = 128
S = 512
D = 1024
DH = 64
H = 8
R = 4
G = 2
TT = S // P
KD = D // P
NCMP = (S - 32) // 16 + 1
NB = 32
CMPH = 256
E = 64
EG = 8
F = 256
SCALE = DH ** -0.5
ALPHA = 2.0 ** 0.25
EPS = 1e-5
NEG = -1e30
ROUTED_SCALE = 2.5
TOPK_GROUPS = 4
SLOTS = 128
UNITS = 100
TOP_K = 8
SLOT_BITS = 7
DOWN_BITS = 11
OUT_OF_RANGE = 1024.0
DIST0 = S - 1
NDIST = DIST0 + S - NCMP
CW = 512
WS_SMALL = 288
RING = 4
WS_SLOT = 2
LEAD = 2

CHUNKS = ([("ada", c) for c in range(4)]
          + [("in", 0), ("in", 1), ("ada", 4), ("in", 2), ("ada", 5), ("ada", 6), ("in", 3), ("ada", 7), ("ada", 8),
             ("small", 0), ("ada", 9), ("cmp", 0), ("cmp", 1), ("in", 4), ("ada", 10), ("ada", 11),
             ("out", 0), ("out", 1), ("shared", 0)])
AT = {c: i for i, c in enumerate(CHUNKS)}

Q_ORDER = (0, 3, 1, 2)
TASKS = ([("fox", 2 * u + i, t) for u in range(H // 2) for t in Q_ORDER for i in range(2)]
         + [(kind, 2 * u + i, t) for u in range(H // 2) for t in Q_ORDER for kind in ("sel", "win") for i in range(2)])
NT = len(TASKS)
FIRST_NSA = H * TT
LAST_PAIR = [TT * u + TT - 1 for u in range(H // 2)] + [FIRST_NSA // 2 + 2 * TT * (u + 1) - 1 for u in range(H // 2)]


def build(nc, a, out):
    with ExitStack() as ctx:
        def sb(name, shape, dt=F32):
            return ctx.enter_context(nc.sbuf_tensor(name, shape, dt))

        def sem(name):
            return ctx.enter_context(nc.semaphore(name))

        h2_dram = nc.dram_tensor("h2_rows", [S, D], F32, kind="Internal")
        ffn_dram = [nc.dram_tensor(f"ffn_rows{i}", [S, D], F32, kind="Internal") for i in range(2)]

        bank = [ctx.enter_context(nc.psum_tensor(f"bank{i}", [P, 512], F32)) for i in range(8)]

        ring = sb("ring", [P, RING, KD * CW])
        down = sb("down", [P, RING, 2 * D])
        area_a = sb("area_a", [P, KD * S])
        area_c = sb("area_c", [P, TT * D])
        area_d = sb("area_d", [P, TT * D])
        area_e = sb("area_e", [P, 4096])
        area_f = sb("area_f", [P, 3072])
        area_g = sb("area_g", [P, 3072])
        mod_rows = sb("mod_rows", [P, 4, D])

        h1T = area_a[:, :].rearrange("p (k t) -> p k t", k=KD)
        h2T = h1T
        fqT = area_d[:, 0:2048].rearrange("p (i t) -> p i t", i=4)
        fkT = area_d[:, 2048:4096].rearrange("p (i t) -> p i t", i=4)
        x_tok = area_d[:, :].rearrange("p (t d) -> p t d", t=TT)
        nqT = area_e[:, 0:2048].rearrange("p (i t) -> p i t", i=4)
        kvT = area_e[:, 2048:4096].rearrange("p (i t) -> p i t", i=4)
        fv = area_f[:, 0:2048].rearrange("p (t d) -> p t d", t=TT)
        vsw = area_f[:, 2048:3072].rearrange("p (t d) -> p t d", t=TT)
        bias_w = area_g[:, 0:2048].rearrange("p (h j) -> p h j", h=H)
        bias_c = area_g[:, 2048:3072].rearrange("p (t h n) -> p t h n", t=TT, h=H)
        oT = area_c[:, :].rearrange("p (k t) -> p k t", k=KD)
        h2_tok = [area_f[:, 0:1024], area_f[:, 1024:2048], area_g[:, 0:1024], area_g[:, 1024:2048]]
        ffn_tok = [area_c[:, :].rearrange("p (t d) -> p t d", t=TT), area_a[:, :].rearrange("p (t d) -> p t d", t=TT)]
        ada_sum = [down[:, 2, 512 * i:512 * i + 512] for i in range(2)]
        tri = down[:, 2, 1024:1536]
        ones_f = down[:, 2, 1024 + P:1024 + 2 * P]
        hid = down[:, 2, 1536:1792]
        hid_e = down[:, 2, 1792:2048]
        hidT = hid_e.rearrange("p (f m) -> p f m", f=2)
        pair = [down[:, 0, i * 1024:(i + 1) * 1024].rearrange("p (g t) -> p g t", g=G) for i in range(2)]
        xb = [down[:, 1, i * 1024:(i + 1) * 1024] for i in range(2)]
        fox_parts = area_c[0:3, 2048:4096].bitcast(BF16).rearrange("p (h t) -> p h t", h=H)
        vc_diag = area_g[:, 2048:2560].rearrange("p (g d) -> p g d", g=G)
        fox_sum = area_c[0:H, 0:512]
        fox_rest = area_c[0:H, 512:1024]
        fox_split = area_c[0:H, 1024:1536].bitcast(BF16)
        fox_lo = area_c[0:H, 0:256].bitcast(BF16)
        p_cmp = down[:, 3, 0:1024].rearrange("p (i f) -> p i f", i=2)
        p_cmpT = down[:, 3, 1024:2048].rearrange("p (g f) -> p g f", g=G)
        pT_buf = [down[:, 1, i * 512:(i + 1) * 512] for i in range(4)]
        p_buf = [down[:, 2, i * 512:(i + 1) * 512] for i in range(4)]
        fk_odd = down[:, 0, :].rearrange("p (i t) -> p i t", i=4)
        ln_rows = area_e[:, :].rearrange("p (i d) -> p i d", i=4)
        ln_tmp = area_g[:, 2048:3072]
        sh_act = area_f[:, 0:TT * F].rearrange("p (t f) -> p t f", t=TT)
        sh_sil = area_f[:, 1024:2048].rearrange("p (t f) -> p t f", t=TT)
        sh_actT = area_f[:, 2560:2816].rearrange("p (i f) -> p i f", i=2)
        sh_y = area_g[:, 0:2048].rearrange("p (i f) -> p i f", i=2)
        r_score = area_c[:, 0:256].rearrange("p (t e) -> p t e", t=TT)
        r_bias = area_c[:, 256:512].rearrange("p (t e) -> p t e", t=TT)
        r_top = area_c[:, 512:768].rearrange("p (t g e) -> p t g e", t=TT, g=EG)
        r_gt = area_c[:, 768:1024].rearrange("p (t g e) -> p t g e", t=TT, g=EG)
        r_eq = area_c[:, 1024:1280].rearrange("p (t g e) -> p t g e", t=TT, g=EG)
        r_group = area_c[:, 1280:1312].rearrange("p (t g) -> p t g", t=TT)
        r_rank = area_c[:, 1312:1344].rearrange("p (t g) -> p t g", t=TT)
        r_gmask = area_c[:, 1344:1376].rearrange("p (t g) -> p t g", t=TT)
        r_masked = area_c[:, 1376:1632].rearrange("p (t e) -> p t e", t=TT)
        r_best = area_c[:, 1632:1664].rearrange("p (t e) -> p t e", t=TT)
        r_sel = area_c[:, 1664:1920].rearrange("p (t e) -> p t e", t=TT)
        r_gate = area_c[:, 1920:2176].rearrange("p (t e) -> p t e", t=TT)
        r_den = area_c[:, 2176:2180]
        r_selb = area_c[:, 2184:2312].bitcast(BF16).rearrange("p (t e) -> p t e", t=TT)
        pos_m = area_c[:, 2312:2568].rearrange("p (t e) -> p t e", t=TT)
        r_kidx = area_c[:, 2568:2824].rearrange("p (t e) -> p t e", t=TT)
        r_pick = [area_c[:, 2824 + 256 * i:3080 + 256 * i].rearrange("p (t e) -> p t e", t=TT) for i in range(2)]
        slot_k = area_c[:, 3336:3368].rearrange("p (t k) -> p t k", t=TT)
        gate_k = area_c[:, 3368:3400].rearrange("p (t k) -> p t k", t=TT)
        slot_ki = area_c[:, 3400:3432].bitcast(I32).rearrange("p (t k) -> p t k", t=TT)
        unit_ki = area_c[:, 3432:3464].bitcast(I32).rearrange("p (t k) -> p t k", t=TT)
        unit_k = area_c[:, 3464:3496].rearrange("p (t k) -> p t k", t=TT)
        payload = area_c[:, 512:672].rearrange("p (t k c) -> p t k c", t=TT, k=TOP_K)
        slot_hot_p = area_c[:, 872:1000].bitcast(BF16).rearrange("p (b s) -> p b s", b=2)
        unit_one_p = area_c[:, 672:722].bitcast(BF16)
        unit_hot_p = area_c[:, 1000:1500].bitcast(BF16).rearrange("p (b n) -> p b n", b=2)
        slot_hot = area_c[:, 3592:3848].bitcast(BF16).rearrange("p (b s) -> p b s", b=4)
        gate_b = area_c[:, 3848:3864].bitcast(BF16).rearrange("p (t k) -> p t k", t=TT)
        n_units = area_c[:, 3864:3928]
        unit_end = area_c[:, 3928:3992]
        zeros_e = area_c[:, 3992:4056]
        expert_u = area_c[:, 4056:4060]

        ident = sb("ident", [P, P])
        ident_b = sb("ident_b", [P, P], BF16)
        ones_b = sb("ones_b", [P, P], BF16)
        causal_b = sb("causal_b", [P, P], BF16)
        before_b = sb("before_b", [P, P], BF16)
        iota_b = sb("iota_b", [P, SLOTS], BF16)
        row_no = sb("row_no", [P, 1])
        table_b = sb("table_b", [P, NDIST + 1], BF16)
        rel_parts = sb("rel_parts", [P, H], BF16)
        c_col = sb("c_col", [P, KD])
        sc_col = sb("sc_col", [P, 3, KD])
        ada_b_col = sb("ada_b_col", [P, 16])
        mod_col = sb("mod_col", [P, 16])
        bf_row = sb("bf_row", [P, H])
        ffng = sb("ffng", [P, TT, 32])
        gates = sb("gates", [P, TT, 24])
        fx = sb("fx", [P, 3, TT, H])
        pos2 = sb("pos2", [P, 2, 16])
        w2 = sb("w2", [P, 2, 2, DH])
        kc2 = sb("kc2", [P, 64])
        nmax = sb("nmax", [P, 4])
        rowsum = sb("rowsum", [P, 4])
        inv_sum = sb("inv_sum", [P, 4])
        early = sb("early", [P, 1])
        c_stat = sb("c_stat", [P, 3, 16])
        ln_stats = sb("ln_stats", [P, 12])
        ln_mv = sb("ln_mv", [P, 4])
        ln_r = sb("ln_r", [P, 4])
        ln_b = sb("ln_b", [P, 1])
        e_bias_row = sb("e_bias_row", [P, E])
        slot_idx = mod_rows[:, 1, 0:UNITS].bitcast(U32)
        slot_gate = mod_rows[:, 1, 128:128 + UNITS]
        idx_gather = [sb(f"idx_gather{i}", [P, 1], U32) for i in range(2)]
        idx_scatter = [sb(f"idx_scatter{i}", [P, 1], U32) for i in range(2)]
        unit_at = area_f[0:1, 2944:3072].bitcast(I32)
        unit_expert = area_f[0:1, 2816:2944].bitcast(I32)
        expert_end = mod_rows[0:1, 1, 256:256 + E + 2].bitcast(I32)
        w_router_t = area_f[:, 2048:2560].rearrange("p (k e) -> p k e", k=KD)
        gathered = [area_e[:, i * 1024:(i + 1) * 1024] for i in range(2)]
        gatheredT = [area_f[:, i * 1024:(i + 1) * 1024].rearrange("p (k m) -> p k m", k=KD) for i in range(2)]
        ring_flat = ring[:, :, :].rearrange("p s n -> p (s n)")
        down_flat = down[:, :, :].rearrange("p s n -> p (s n)")
        y_out = [area_g[:, i * 1024:(i + 1) * 1024] for i in range(2)]
        silu_g = area_f[:, 2048:2304]
        e_act = area_f[:, 2304:2560]
        e_actT = area_f[:, 2560:2816].rearrange("p (i f) -> p i f", i=2)
        unit_hot = area_g[:, 2048:3048].bitcast(BF16).rearrange("p (b n) -> p b n", b=4)
        list_sum = area_e[:, 0:5 * UNITS]

        slot_in = [sem(f"slot_in{s}") for s in range(RING)]
        down_in = [sem(f"down_in{s}") for s in range(RING)]
        chunk_used = sem("chunk_used")
        c_in = sem("c_in")
        ada_part = sem("ada_part")
        ada_mm = sem("ada_mm")
        ada_out = sem("ada_out")
        k_padded = sem("k_padded")
        hidT_mm = sem("hidT_mm")
        hidT_ready = sem("hidT_ready")
        inv_ready = sem("inv_ready")
        p_scaled_act = sem("p_scaled_act")
        p_scaled = sem("p_scaled")
        rows_ready = sem("rows_ready")
        o_act = sem("o_act")
        o_dve = sem("o_dve")
        xT_in = sem("xT_in")
        consts_in = sem("consts_in")
        table_in = sem("table_in")
        buckets_in = sem("buckets_in")
        modb_in = sem("modb_in")
        masks_set = sem("masks_set")
        ident_set = sem("ident_set")
        passed = sem("passed")
        rel_set = sem("rel_set")
        bias_mm = sem("bias_mm")
        bias_out = sem("bias_out")
        c_exp = sem("c_exp")
        c_ready = sem("c_ready")
        mod_ready = sem("mod_ready")
        h1_dve = sem("h1_dve")
        h1_act = sem("h1_act")
        job_mm = sem("job_mm")
        job_act = sem("job_act")
        job_dve = sem("job_dve")
        ffng_act = sem("ffng_act")
        fx_ready = sem("fx_ready")
        cum_mm = sem("cum_mm")
        parts_ready = sem("parts_ready")
        parts_in = sem("parts_in")
        pair_in = [sem("pair_in_k"), sem("pair_in_v")]
        xb_ready = sem("xb_ready")
        hid_mm = sem("hid_mm")
        hid_exp = sem("hid_exp")
        hid_ready = sem("hid_ready")
        kc_mm = sem("kc_mm")
        kc_ready = sem("kc_ready")
        vc_ready = sem("vc_ready")
        cmp_qk = sem("cmp_qk")
        cmp_max = sem("cmp_max")
        cmp_exp = sem("cmp_exp")
        cmp_p = sem("cmp_p")
        cmp_tr = sem("cmp_tr")
        cmp_pT = sem("cmp_pT")
        qk_done = sem("qk_done")
        max_done = sem("max_done")
        exp_done = sem("exp_done")
        tr_done = sem("tr_done")
        pT_act = sem("pT_act")
        pT_dve = sem("pT_dve")
        pv_done = sem("pv_done")
        x_in = sem("x_in")
        ln_in = sem("ln_in")
        mix_mm = sem("mix_mm")
        mix_read = sem("mix_read")
        var_ready = sem("var_ready")
        rstd_ready = sem("rstd_ready")
        x1_ready = sem("x1_ready")
        h2_ready = sem("h2_ready")
        h2_stored = sem("h2_stored")
        h2T_mm = sem("h2T_mm")
        h2T_act = sem("h2T_act")
        router_mm = sem("router_mm")
        router_exp = sem("router_exp")
        router_in = sem("router_in")
        sel_ready = sem("sel_ready")
        pos_mm = sem("pos_mm")
        units_ready = sem("units_ready")
        units_row = sem("units_row")
        hot_ready = sem("hot_ready")
        hot_pool = sem("hot_pool")
        payload_ready = sem("payload_ready")
        list_mm = sem("list_mm")
        lists_ready = sem("lists_ready")
        tables_ready = sem("tables_ready")
        weights_ready = sem("weights_ready")
        sh_gu = sem("sh_gu")
        sh_silu = sem("sh_silu")
        sh_act_ready = sem("sh_act_ready")
        sh_tr = sem("sh_tr")
        sh_actT_ready = sem("sh_actT_ready")
        sh_down = sem("sh_down")
        sh_y_ready = sem("sh_y_ready")
        ffn_started = [sem(f"ffn_started{i}") for i in range(2)]
        cleared = sem("cleared")
        idx_set = sem("idx_set")
        idx_out = sem("idx_out")
        gather_in = [sem(f"gather_in{i}") for i in range(2)]
        xe_tr = sem("xe_tr")
        xe_act = sem("xe_act")
        xe_dve = sem("xe_dve")
        gu_done = sem("gu_done")
        silu_done = sem("silu_done")
        act_done = sem("act_done")
        at_tr = sem("at_tr")
        at_ready = sem("at_ready")
        down_done = sem("down_done")
        y_act = sem("y_act")
        y_dve = sem("y_dve")
        scattered = [sem(f"scattered{i}") for i in range(2)]
        ffn_in = [sem(f"ffn_in{t}") for t in range(TT)]
        sums_added = sem("sums_added")
        xn_ready = sem("xn_ready")
        xg_ready = sem("xg_ready")
        x2_ready = sem("x2_ready")
        x2_last = sem("x2_last")
        stored = sem("stored")
        dve_step = sem("dve_step")
        act_step = sem("act_step")
        pool_step = sem("pool_step")

        block = ctx.enter_context(nc.Block())

        NJ = 24
        owner = ["act" if j % 2 == 0 else "dve" for j in range(NJ)]

        def copied(j):
            o = owner[j]
            return (job_act if o == "act" else job_dve), sum(owner[i] == o for i in range(j + 1))

        def settle(eng):
            eng.sem_inc(passed, 1)

        def used(i):
            mine = [(kind == "ada") == (CHUNKS[i][0] == "ada") for kind, c in CHUNKS[:i + 1]]
            return (ada_part if CHUNKS[i][0] == "ada" else chunk_used), sum(mine)

        def row_bank(c):
            return bank[6 + c % 2] if c < 5 else bank[5]

        def by_pool(j):
            return j % 4 == 3

        def hots_before(j, pool):
            return sum(by_pool(i) == pool for i in range(j))

        def spread_payload(t, k):
            return payload[:, t, k, :].rearrange("p (c o) -> p c o", o=1).to_broadcast([P, 5, UNITS])

        def for_parts(row):
            return row.rearrange("p (o u) -> p o u", o=1).to_broadcast([P, 5, UNITS])

        def heads_out(u):
            return (o_act, u + 1) if u < H // 2 else (o_dve, u - H // 2 + 1)

        def chunks_before(slot):
            return sum(i % RING == slot for i in range(len(CHUNKS)))

        def pT_ready(t):
            if t < FIRST_NSA:
                return pT_dve, t + 1
            return pT_act, t - FIRST_NSA + 1

        def scaled(t):
            return (p_scaled_act, t + 1) if t < FIRST_NSA else (p_scaled, t - FIRST_NSA + 1)

        @block.sync
        def _(sp):
            def load_chunk(i):
                kind, c = CHUNKS[i]
                if i >= RING:
                    sp.wait_ge(*used(i - RING))
                if kind == "small":
                    sp.dma_start(ring[:, i % RING, 0:KD * WS_SMALL], a["w_small"]).then_inc(slot_in[i % RING], 16)
                else:
                    src = {"ada": a["w_ada"], "in": a["w_in"], "cmp": a["w_cmp1"], "out": a["w_out"],
                           "shared": a["ws_gu"]}[kind]
                    sp.dma_start(ring[:, i % RING, :], src[c]).then_inc(slot_in[i % RING], 16)

            sp.dma_start(c_col[:, :], a["c_col"]).then_inc(c_in, 16)
            for q in range(3):
                sp.dma_start(c_stat[32 * q:32 * q + 32, 0, 0:H], a["rel_bias"]).then_inc(table_in, 16)
            sp.dma_start(c_stat[0:96, 1, 0:H], a["rel_bias"][NB - 1:NB, :].to_broadcast([96, H])).then_inc(table_in, 16)
            for i in range(RING):
                load_chunk(i)
            sp.dma_start(area_a[:, :], a["xT"]).then_inc(xT_in, 16)
            for i in range(RING, len(CHUNKS)):
                load_chunk(i)
                if i == RING:
                    sp.dma_start(mod_rows[:, :, :].rearrange("p i d -> p (i d)"),
                                 a["ada_b_row"].to_broadcast([P, 4 * D])).then_inc(modb_in, 16)

            def slot_of(u):
                return (len(CHUNKS) + u) % RING

            def landed(e, i, u):
                s = slot_of(u)
                sp.wait_ge(slot_in[s], 16 * (i + chunks_before(s) + 1))
                settle(sp)
                sp.wait_ge(down_in[s], 16 * (i + (1 if s == WS_SLOT else 0) + 1))
                sp.sem_inc(weights_ready, 1)

            for u in range(RING):
                s = slot_of(u)
                if u >= LEAD:
                    landed(u - LEAD, 0, u - LEAD)
                sp.wait_ge(*used(len(CHUNKS) + u - RING))
                sp.dma_start(ring[:, s, :], a["w_gu"][u]).then_inc(slot_in[s], 16)
                if u == 0:
                    sp.wait_ge(pv_done, NT // 2)
                    sp.dma_start(down[:, WS_SLOT, :], a["ws_d"]).then_inc(down_in[WS_SLOT], 16)
                if s == WS_SLOT:
                    sp.wait_ge(sh_down, TT)
                sp.dma_start(down[:, s, :], a["w_d"][u]).then_inc(down_in[s], 16)
            sp.wait_ge(tables_ready, 1)
            with sp.Fori(1, E // RING) as i:
                for u in range(RING):
                    s = slot_of(u)
                    e = i * RING + u
                    landed(e - LEAD, i if u >= LEAD else i - 1, (u - LEAD) % RING)
                    units = sp.value_load(expert_end[0:1, bass.ds(e - RING, 1)], min_val=1, max_val=UNITS)
                    sp.wait_ge(gu_done, units)
                    settle(sp)
                    sp.dma_start(ring[:, s, :], a["w_gu"][bass.ds(e, 1)].rearrange("o p n -> p (o n)"))\
                        .then_inc(slot_in[s], 16)
                    sp.wait_ge(down_done, units)
                    settle(sp)
                    sp.dma_start(down[:, s, :], a["w_d"][bass.ds(e, 1)].rearrange("o p n -> p (o n)"))\
                        .then_inc(down_in[s], 16)
            for u in range(RING - LEAD, RING):
                landed(E - RING + u, E // RING - 1, u)

            pairs = sp.value_load(expert_end[0:1, E:E + 1], min_val=E // 2, max_val=UNITS // 2 - 1)
            sp.wait_ge(scattered[0], 16 * pairs)
            settle(sp)
            sp.wait_ge(scattered[1], 16 * (pairs + 1))
            settle(sp)
            for t in range(TT):
                for i in range(2):
                    sp.dma_start(ffn_tok[i][:, t, :], ffn_dram[i][t * P:(t + 1) * P, :]).then_inc(ffn_in[t], 16)
            for t in range(TT):
                if t < TT - 1:
                    sp.wait_ge(x2_ready, t + 1)
                else:
                    sp.wait_ge(x2_last, 1)
                sp.dma_start(out[t * P:(t + 1) * P, :], x_tok[:, t, :]).then_inc(stored, 16)
            sp.wait_ge(stored, 16 * TT)

        @block.scalar
        def _(act):
            steps = [0]

            def link(ins):
                steps[0] += 1
                ins.then_inc(act_step, 1)
                act.wait_ge(act_step, steps[0])

            act.dma_start(ada_b_col[:, :], a["ada_b_col"]).then_inc(consts_in, 16)
            act.dma_start(bf_row[:, :], a["b_f"].to_broadcast([P, H])).then_inc(consts_in, 16)
            act.dma_start(pos2[:, :, :], a["cmp_pos"]).then_inc(consts_in, 16)
            act.dma_start(w2[:, :, :, :], a["w_cmp2"]).then_inc(consts_in, 16)
            act.dma_start(e_bias_row[:, :], a["e_bias"].to_broadcast([P, E])).then_inc(consts_in, 16)

            act.wait_ge(c_in, 16)
            nc.scalar.activation(sc_col[:, 0, :], c_col[:, :], ACT.Exp, scale=-1.0).then_inc(c_exp, 1)

            for b in range(4):
                act.wait_ge(bias_mm, b + 1)
                nc.scalar.activation(bias_w[:, :, 64 * b:64 * b + 64],
                                     bank[b][:, :].rearrange("p (j h) -> p h j", h=H), ACT.Copy).then_inc(bias_out, 1)
            for t in range(TT):
                act.wait_ge(bias_mm, 4 + t + 1)
                nc.scalar.activation(bias_c[:, t, :, 0:NCMP],
                                     bank[4 + t][:, 0:8 * NCMP].rearrange("p (n h) -> p h n", h=H), ACT.Copy)\
                    .then_inc(bias_out, 1)

            act.wait_ge(mod_ready, 1)
            act.wait_ge(xT_in, 16)
            for k in range(1, KD, 2):
                nc.scalar.activation(h1T[:, k, :], h1T[:, k, :], ACT.Identity, bias=mod_col[:, k:k + 1],
                                     scale=mod_col[:, 8 + k:9 + k]).then_inc(h1_act, 1)

            def copy_job(j):
                act.wait_ge(job_mm, j + 1)
                if j < 16:
                    i = j % 4
                    dst = [fqT, fkT, nqT, kvT][j // 4][:, i, :]
                    nc.scalar.activation(dst, bank[j % 4][:, :], ACT.Copy,
                                         scale=SCALE if j // 4 in (0, 2) else 1.0).then_inc(job_act, 1)
                elif j < 20:
                    t = j - 16
                    nc.scalar.activation(ffng[:, t, :], bank[j % 4][:, 256:288], ACT.Copy).then_inc(ffng_act, 1)
                    nc.scalar.activation(vsw[:, t, :], bank[j % 4][:, 0:256], ACT.Copy).then_inc(job_act, 1)
                else:
                    nc.scalar.activation(fv[:, j - 20, :], bank[j % 4][:, :], ACT.Copy).then_inc(job_act, 1)

            for j in range(0, 20, 2):
                copy_job(j)

            act.wait_ge(ffng_act, TT)
            nc.scalar.activation(gates[:, :, :], ffng[:, :, H:32], ACT.Exp, scale=-1.0).then_inc(fx_ready, 1)
            act.wait_ge(fx_ready, 2)
            link(nc.scalar.activation(fx[:, 1, :, :], fx[:, 1, :, :], ACT.Exp, scale=-1.0))
            nc.scalar.activation(fx[:, 1, :, :], fx[:, 1, :, :], ACT.Ln, bias=1.0).then_inc(fx_ready, 1)

            act.wait_ge(hid_mm, 1)
            nc.scalar.activation(hid_e, bank[4][:, 0:256], ACT.Exp, scale=-1.0).then_inc(hid_exp, 1)
            copy_job(20)
            copy_job(22)

            for i in range(2):
                act.wait_ge(cmp_max, i + 1)
                nc.scalar.activation(p_cmp[:, i, :], p_cmp[:, i, :], ACT.Exp).then_inc(cmp_exp, 1)
            for g in range(G):
                act.wait_ge(cmp_tr, g + 1)
                nc.scalar.activation(p_cmpT[:, g, :], bank[6 + g][:, :], ACT.Copy).then_inc(cmp_pT, 1)

            def exp_task(t):
                kind, h, qt = TASKS[t]
                n = P * (qt + 1)
                act.wait_ge(max_done, t + 1)
                if t == 0:
                    act.wait_ge(kc_mm, 1)
                    act.wait_ge(cmp_tr, 2)
                if t >= 4:
                    act.wait_ge(tr_done, t - 3)
                nc.scalar.activation(p_buf[t % 4][:, 0:n], bank[t % 4][:, 0:n], ACT.Exp,
                                     bias=nmax[:, t % 4:t % 4 + 1],
                                     accum_out=rowsum[:, t % 4:t % 4 + 1]).then_inc(exp_done, 1)

            def copy_pT(t):
                n = P * (TASKS[t][2] + 1)
                act.wait_ge(tr_done, t + 1)
                if t >= 4:
                    act.wait_ge(pv_done, (t - 4) // 2 + 1)
                nc.scalar.activation(pT_buf[t % 4][:, 0:n], bank[4 + t % 2][:, 0:n], ACT.Copy).then_inc(pT_act, 1)

            for t in range(NT + 3):
                if t >= 3 and t - 3 >= FIRST_NSA:
                    copy_pT(t - 3)
                if t < NT:
                    exp_task(t)
                if 1 <= t <= FIRST_NSA:
                    n = P * (TASKS[t - 1][2] + 1)
                    b = (t - 1) % 4
                    act.wait_ge(inv_ready, t)
                    nc.scalar.activation(p_buf[b][:, 0:n], p_buf[b][:, 0:n], ACT.Copy,
                                         scale=inv_sum[:, b:b + 1]).then_inc(p_scaled_act, 1)
                for u in range(H // 2):
                    if t == 2 * LAST_PAIR[u] + 6:
                        act.wait_ge(pv_done, LAST_PAIR[u] + 1)
                        nc.scalar.activation(oT[:, u, :], bank[6 + u % 2][:, :], ACT.Copy).then_inc(o_act, 1)
                if t == FIRST_NSA + 2:
                    act.wait_ge(qk_done, FIRST_NSA)
                    act.dma_start(area_d[:, :].rearrange("p (t d) -> p t d", t=TT), a["x_tok"]).then_inc(x_in, 16)

            act.wait_ge(qk_done, NT)
            act.dma_start(ln_rows[:, :, :].rearrange("p i d -> p (i d)"), a["ln_rows"].to_broadcast([P, 4 * D])).then_inc(ln_in, 16)

            act.wait_ge(pv_done, NT // 2)
            act.dma_start(w_router_t, a["w_router"]).then_inc(router_in, 16)

            def rstd(n, i):
                act.wait_ge(var_ready, n)
                link(nc.scalar.activation(ln_r[:, 2 * i:2 * i + 1], ln_r[:, 2 * i:2 * i + 1], ACT.Ln))
                return nc.scalar.activation(ln_r[:, 2 * i + 1:2 * i + 2], ln_r[:, 2 * i:2 * i + 1], ACT.Exp, scale=-0.5)

            for t in range(TT):
                rstd(t + 1, 0).then_inc(rstd_ready, 1)
                act.wait_ge(h2_ready, t + 1)
                act.dma_start(h2_dram[t * P:(t + 1) * P, :], h2_tok[t]).then_inc(h2_stored, 16)
                for half in range(2):
                    act.wait_ge(h2T_mm, 2 * t + half + 1)
                    nc.scalar.activation(h2T[:, 4 * half:4 * half + 4, t * P:(t + 1) * P],
                                         bank[4 + half][:, :].rearrange("p (k m) -> p k m", k=4),
                                         ACT.Copy).then_inc(h2T_act, 1)
            act.wait_ge(router_mm, TT)
            act.wait_ge(h2_stored, 16 * TT)
            nc.scalar.activation(r_score, bank[6][:, 0:256].rearrange("p (t e) -> p t e", t=TT),
                                 ACT.Exp, scale=-1.0).then_inc(router_exp, 1)

            for t in range(TT):
                act.wait_ge(sh_gu, t + 1)
                nc.scalar.activation(sh_sil[:, t, :], bank[t][:, 0:F], ACT.Silu).then_inc(sh_silu, 1)
            for t in range(TT):
                act.wait_ge(sh_tr, t + 1)
                if t >= 1:
                    act.wait_ge(sh_down, t)
                nc.scalar.activation(sh_actT[:, :, 0:P], bank[2][:, 0:F].rearrange("p (i f) -> p i f", i=2),
                                     ACT.Copy).then_inc(sh_actT_ready, 1)
                act.wait_ge(sh_down, t + 1)
                if t >= 2:
                    act.wait_ge(ffn_started[t % 2], 16 * (t // 2))
                nc.scalar.activation(sh_y[:, t % 2, 0:512], bank[4][:, :], ACT.Copy).then_inc(sh_y_ready, 1)
                nc.scalar.activation(sh_y[:, t % 2, 512:1024], bank[5][:, :], ACT.Copy).then_inc(sh_y_ready, 1)
                act.wait_ge(sh_y_ready, 2 * t + 2)
                act.dma_start(ffn_dram[0][t * P:(t + 1) * P, :], sh_y[:, t % 2, :]).then_inc(ffn_started[t % 2], 16)

            def silu(n):
                act.wait_ge(gu_done, n + 1)
                nc.scalar.activation(silu_g, bank[0][:, 0:F], ACT.Silu).then_inc(silu_done, 1)

            def copy_xT(n, u):
                act.wait_ge(xe_tr, n + 1)
                nc.scalar.activation(gatheredT[u % 2][:, 0:4, :], bank[1][:, :].rearrange("p (k m) -> p k m", k=4),
                                     ACT.Copy).then_inc(xe_act, 1)

            def copy_y(n, u, i):
                act.wait_ge(down_done, n + 1)
                if isinstance(i, int) and i == 0:
                    for stored_rows in ffn_started:
                        act.wait_ge(stored_rows, 8 * TT)
                else:
                    act.wait_ge(scattered[u], 16 * (i + u))
                nc.scalar.activation(y_out[u][:, 0:512], bank[4][:, :], ACT.Copy).then_inc(y_act, 1)

            copy_xT(0, 0)
            silu(0)
            copy_xT(1, 1)
            silu(1)
            copy_xT(2, 0)
            copy_y(0, 0, 0)
            act.wait_ge(tables_ready, 1)
            pairs = act.value_load(expert_end[0:1, E:E + 1], min_val=E // 2, max_val=UNITS // 2 - 1)
            with act.Fori(1, pairs) as i:
                silu(2 * i)
                copy_xT(2 * i + 1, 1)
                copy_y(2 * i - 1, 1, i - 1)
                silu(2 * i + 1)
                copy_xT(2 * i + 2, 0)
                copy_y(2 * i, 0, i)
            last = 2 * pairs - 1
            copy_y(last, 1, pairs - 1)

            for t in range(TT):
                link(rstd(TT + t + 1, t % 2))
                link(nc.scalar.activation(ln_b[:, :], ln_mv[:, 2 * (t % 2):2 * (t % 2) + 1], ACT.Copy,
                                          scale=ln_r[:, 2 * (t % 2) + 1:2 * (t % 2) + 2]))
                link(nc.scalar.activation(ln_b[:, :], ln_b[:, :], ACT.Copy, scale=-1.0))
                nc.scalar.activation(x_tok[:, t, :], x_tok[:, t, :], ACT.Identity, bias=ln_b[:, :],
                                     scale=ln_r[:, 2 * (t % 2) + 1:2 * (t % 2) + 2]).then_inc(xn_ready, 1)

        @block.tensor
        def _(pe):
            pe.wait_ge(table_in, 64)
            pe.wait_ge(buckets_in, 16)
            pe.wait_ge(rel_set, 1)
            for b in range(4):
                for i in range(64):
                    j = 64 * b + i
                    first = DIST0 + P - j
                    last = nc.tensor.matmul(bank[b][:, 8 * i:8 * i + 8], table_b[0:97, first:first + P],
                                            rel_parts[0:97, :], start=True, stop=True)
                last.then_inc(bias_mm, 1)
            for t in range(TT):
                for n in range(NCMP):
                    first = DIST0 + P * t - 16 * n - 31
                    last = nc.tensor.matmul(bank[4 + t][:, 8 * n:8 * n + 8], table_b[0:97, first:first + P],
                                            rel_parts[0:97, :], start=True, stop=True)
                last.then_inc(bias_mm, 1)

            pe.wait_ge(masks_set, 1)
            pe.wait_ge(bias_out, 1)
            for i in range(4):
                pe.wait_ge(ada_part, i + 1)
                for m in range(4):
                    last = nc.tensor.matmul(bank[0][:, 4 * i + m:4 * i + m + 1], ada_sum[i % 2][:, m * P:(m + 1) * P],
                                            ones_f[:, 0:1], start=True, stop=True)
                last.then_inc(ada_mm, 1)
            pe.wait_ge(mod_ready, 1)
            pe.wait_ge(bias_out, 8)

            def arrived(i):
                pe.wait_ge(slot_in[i % RING], 16 * (i // RING + 1))

            def free_bank(j):
                if j >= 4:
                    pe.wait_ge(*copied(j - 4))

            def ada_row(c):
                pe.wait_ge(ada_part, 4 + c + 1)
                if c == 5:
                    pe.wait_ge(parts_ready, 1)
                elif c >= 2:
                    pe.wait_ge(ada_out, c if c > 5 else c - 1)
                nc.tensor.matmul(row_bank(c)[:, :], ones_f, ada_sum[c % 2], start=True, stop=True)\
                    .then_inc(ada_mm, 1)

            for c in range(4):
                i = AT["in", c]
                arrived(i)
                w = ring[:, i % RING, :].rearrange("p (k n) -> p k n", k=KD)
                for m in range(4):
                    j = 4 * c + m
                    free_bank(j)
                    for k in range(KD):
                        if j == 0:
                            pe.wait_ge(h1_act if k % 2 else h1_dve, k // 2 + 1)
                        last = nc.tensor.matmul(bank[j % 4][:, :], w[:, k, m * P:(m + 1) * P], h1T[:, k, :],
                                                start=(k == 0), stop=(k == KD - 1))
                    last.then_inc(job_mm, 1)
                pe.wait_ge(job_mm, 4 * c + 4)
                nc.tensor.nop().then_inc(chunk_used, 1)
                if c >= 1:
                    ada_row(c - 1)
            def token_major(j):
                kind, width = (("small", 0), WS_SMALL) if j < 20 else (("in", 4), CW)
                i, t = AT[kind], j % 4
                if t == 0:
                    arrived(i)
                free_bank(j)
                w = ring[:, i % RING, 0:KD * width].rearrange("p (k n) -> p k n", k=KD)
                for k in range(KD):
                    last = nc.tensor.matmul(bank[j % 4][:, 0:width], h1T[:, k, t * P:(t + 1) * P], w[:, k, :],
                                            start=(k == 0), stop=(k == KD - 1))
                last.then_inc(job_mm, 1)
                if t == 3:
                    pe.wait_ge(job_mm, j + 1)
                    nc.tensor.nop().then_inc(chunk_used, 1)

            token_major(16)
            token_major(17)
            ada_row(3)
            token_major(18)
            token_major(19)

            pe.wait_ge(xb_ready, 2)
            arrived(AT["cmp", 0])
            arrived(AT["cmp", 1])
            for jj in range(16):
                for s in range(2):
                    w = ring[:, AT["cmp", s] % RING, :].rearrange("p (k n) -> p k n", k=16)
                    last = nc.tensor.matmul(bank[4][64 * s:64 * s + 64, 0:CMPH], xb[s][:, 64 * jj:64 * jj + 64],
                                            w[:, jj, :], start=(jj == 0), stop=(jj == 15))
            last.then_inc(hid_mm, 1)
            pe.wait_ge(hid_mm, 1)
            nc.tensor.nop().then_inc(chunk_used, 2)

            pe.wait_ge(fx_ready, 4)
            pe.wait_ge(masks_set, 1)
            for kt in range(TT):
                last = nc.tensor.matmul(bank[5][0:H, kt * P:S], fx[:, 2, kt, :], tri[:, 0:S - kt * P],
                                        start=(kt == 0), stop=(kt == TT - 1))
            last.then_inc(cum_mm, 1)

            ada_row(4)
            token_major(20)

            pe.wait_ge(hid_ready, 1)
            pe.wait_ge(ident_set, 2)
            for f in range(2):
                last = nc.tensor.transpose(bank[4][:, 256 + f * P:256 + (f + 1) * P], hid[:, f * P:(f + 1) * P],
                                           ident[:, :])
            last.then_inc(hidT_mm, 1)
            token_major(21)
            pe.wait_ge(hidT_ready, 1)
            for g in range(G):
                for f in range(2):
                    nc.tensor.matmul(bank[4][g * DH:(g + 1) * DH, 0:NCMP], w2[:, 0, f, :],
                                     hidT[:, f, g * NCMP:(g + 1) * NCMP], start=(f == 0), stop=(f == 1))
            for r in range(R):
                for g in range(G):
                    for f in range(2):
                        last = nc.tensor.matmul(bank[4][32 * r:32 * r + NCMP, 64 + g * DH:64 + (g + 1) * DH],
                                                hidT[:, f, 64 + g * NCMP:64 + (g + 1) * NCMP], w2[:, 1, f, :],
                                                start=(f == 0), stop=(f == 1))
            last.then_inc(kc_mm, 1)
            ada_row(5)
            token_major(22)
            pe.wait_ge(kc_ready, 1)
            pe.wait_ge(ada_out, 5)
            for qt in range(TT):
                for r in range(R):
                    dst = bank[6 + qt // 2][:, :].rearrange("p (g m n) -> p g m n", g=G, m=2 * R)
                    last = nc.tensor.matmul(dst[:, :, (qt % 2) * R + r, :], nqT[:, r, qt * P:(qt + 1) * P],
                                            kc2[:, :].rearrange("p (g n) -> p g n", g=G), start=True, stop=True)
            last.then_inc(cmp_qk, 1)

            ada_row(6)
            token_major(23)

            def cmp_transposes():
                pe.wait_ge(cmp_p, 2)
                for g in range(G):
                    for qt in range(TT):
                        at = g * 256 + (qt % 2) * P
                        last = nc.tensor.transpose(bank[6 + g][:, qt * P:(qt + 1) * P],
                                                   p_cmp[:, qt // 2, at:at + P], ident[:, :])
                    last.then_inc(cmp_tr, 1)

            pe.wait_ge(parts_in, 48)
            pe.wait_ge(k_padded, 2)
            for j in range(20, 24):
                pe.wait_ge(*copied(j))

            def qk(t):
                kind, h, qt = TASKS[t]
                n = P * (qt + 1)
                if t >= 4:
                    pe.wait_ge(exp_done, t - 3)
                dst = bank[t % 4]
                if kind == "fox":
                    nc.tensor.matmul(dst[:, 0:n], fqT[:, h // 2, qt * P:(qt + 1) * P],
                                     (fkT, fk_odd)[h % 2][:, h // 2, 0:n], start=True, stop=False)
                    nc.tensor.matmul(dst[:, n - P:n], ident_b[:, :], causal_b[:, :], start=False, stop=False)
                    nc.tensor.matmul(dst[:, 0:n], ones_b[0:3, :], fox_parts[:, h, 0:n],
                                     start=False, stop=True).then_inc(qk_done, 1)
                else:
                    g, r = h // R, h % R
                    nc.tensor.matmul(dst[:, 0:n], nqT[:, r, qt * P:(qt + 1) * P],
                                     kvT[:, (0 if kind == "sel" else 1) + 2 * g, 0:n],
                                     start=True, stop=True).then_inc(qk_done, 1)

            def transposes(t):
                qt = TASKS[t][2]
                pe.wait_ge(*scaled(t))
                if t >= 2:
                    pe.wait_ge(*pT_ready(t - 2))
                for kt in range(qt + 1):
                    last = nc.tensor.transpose(bank[4 + t % 2][:, kt * P:(kt + 1) * P],
                                               p_buf[t % 4][:, kt * P:(kt + 1) * P], ident[:, :])
                last.then_inc(tr_done, 1)

            def pv(w):
                kind, h, qt = TASKS[2 * w]
                u = h // 2 + (0 if kind == "fox" else H // 2)
                dst = bank[6 + u % 2]
                if w == 0:
                    pe.wait_ge(cmp_pT, 2)
                if w - 1 in LAST_PAIR and u >= 2:
                    pe.wait_ge(*heads_out(u - 2))
                if (w == 0 or w - 1 in LAST_PAIR) and kind != "fox":
                    for i in range(2):
                        at = DH * ((h + i) % R)
                        nc.tensor.matmul(dst[DH * i:DH * (i + 1), :], vc_diag[:, h // R, at:at + DH],
                                         p_cmpT[:, h // R, :], start=True, stop=False)
                for i in range(2):
                    pe.wait_ge(*pT_ready(2 * w + i))
                for kt in range(qt + 1):
                    for i in range(2):
                        if kind == "fox":
                            v = fv[:, kt, (h + i) * DH:(h + i + 1) * DH]
                        else:
                            at = (0 if kind == "sel" else 128) + DH * (h // R)
                            v = vsw[:, kt, at:at + DH]
                        last = nc.tensor.matmul(dst[DH * i:DH * (i + 1), qt * P:(qt + 1) * P], v,
                                                pT_buf[(2 * w + i) % 4][:, kt * P:(kt + 1) * P],
                                                start=(kind == "fox" and kt == 0),
                                                stop=(kt == qt and (kind == "fox" or w in LAST_PAIR)))
                last.then_inc(pv_done, 1)

            for t in range(NT + 4):
                if t < NT:
                    qk(t)
                if t == 2:
                    ada_row(7)
                    cmp_transposes()
                    pe.wait_ge(vc_ready, 1)
                    pe.wait_ge(ada_out, 8)
                if 3 <= t < NT + 3:
                    transposes(t - 3)
                if t >= 5 and t % 2 == 1:
                    pv((t - 5) // 2)
            for u in (H // 2 - 1, H - 1):
                pe.wait_ge(*heads_out(u))

            def mix(t):
                for c in range(2):
                    i = AT["out", c]
                    if t == 0:
                        arrived(i)
                    w = ring[:, i % RING, :].rearrange("p (k n) -> p k n", k=KD)
                    if t >= 2:
                        pe.wait_ge(mix_read, 2 * (t - 2) + c + 1)
                    for k in range(KD):
                        last = nc.tensor.matmul(bank[2 * (t % 2) + c][:, :], oT[:, k, t * P:(t + 1) * P], w[:, k, :],
                                                start=(k == 0), stop=(k == KD - 1))
                    last.then_inc(mix_mm, 1)

            def h2_tile(t):
                pe.wait_ge(h2_ready, t + 1)
                for half in range(2):
                    if t >= 1:
                        pe.wait_ge(h2T_act, 2 * (t - 1) + half + 1)
                    for k in range(4):
                        last = nc.tensor.transpose(bank[4 + half][:, k * P:(k + 1) * P],
                                                   h2_tok[t][:, (4 * half + k) * P:(4 * half + k + 1) * P], ident[:, :])
                    last.then_inc(h2T_mm, 1)

            def router(t):
                if t == 0:
                    pe.wait_ge(router_in, 16)
                pe.wait_ge(h2T_act, 2 * t + 2)
                for k in range(KD):
                    last = nc.tensor.matmul(bank[6][:, t * E:(t + 1) * E], h2T[:, k, t * P:(t + 1) * P],
                                            w_router_t[:, k, :], start=(k == 0), stop=(k == KD - 1))
                last.then_inc(router_mm, 1)

            def shared_gu(t):
                if t == 0:
                    arrived(AT["shared", 0])
                pe.wait_ge(mix_read, (6, 6, 8, 8)[t])
                w = ring[:, AT["shared", 0] % RING, :].rearrange("p (k n) -> p k n", k=KD)
                for k in range(KD):
                    last = nc.tensor.matmul(bank[t][:, :], h2T[:, k, t * P:(t + 1) * P], w[:, k, :],
                                            start=(k == 0), stop=(k == KD - 1))
                last.then_inc(sh_gu, 1)

            mix(0)
            mix(1)
            h2_tile(0)
            mix(2)
            router(0)
            h2_tile(1)
            mix(3)
            pe.wait_ge(mix_mm, 2 * TT)
            nc.tensor.nop().then_inc(chunk_used, 2)
            router(1)
            h2_tile(2)
            shared_gu(0)
            router(2)
            shared_gu(1)
            h2_tile(3)
            router(3)
            shared_gu(2)
            shared_gu(3)
            pe.wait_ge(sh_gu, TT)
            nc.tensor.nop().then_inc(chunk_used, 1)

            def positions():
                pe.wait_ge(sel_ready, 1)
                pe.wait_ge(router_exp, 1)
                for t in range(TT):
                    for s in range(t):
                        nc.tensor.matmul(bank[7][:, t * E:(t + 1) * E], ones_b[:, :], r_selb[:, s, :],
                                         start=(s == 0), stop=False)
                    nc.tensor.matmul(bank[7][:, t * E:(t + 1) * E], before_b[:, :], r_selb[:, t, :],
                                     start=(t == 0), stop=True)
                for s in range(TT):
                    last = nc.tensor.matmul(bank[7][:, TT * E:(TT + 1) * E], ones_b[:, :], r_selb[:, s, :],
                                            start=(s == 0), stop=(s == TT - 1))
                last.then_inc(pos_mm, 1)

            positions()

            pe.wait_ge(sh_act_ready, TT)
            pe.wait_ge(down_in[WS_SLOT], 16)
            wd = down[:, WS_SLOT, :].rearrange("p (f n) -> p f n", f=2)
            def shared_down(t):
                if t >= 1:
                    pe.wait_ge(sh_actT_ready, t)
                for f in range(2):
                    last = nc.tensor.transpose(bank[2][:, f * P:(f + 1) * P], sh_act[:, t, f * P:(f + 1) * P], ident[:, :])
                last.then_inc(sh_tr, 1)
                pe.wait_ge(sh_actT_ready, t + 1)
                if t >= 1:
                    pe.wait_ge(sh_y_ready, 2 * t)
                for c in range(2):
                    for f in range(2):
                        last = nc.tensor.matmul(bank[4 + c][:, :], sh_actT[:, f, 0:P], wd[:, f, c * 512:(c + 1) * 512],
                                                start=(f == 0), stop=(f == 1))
                last.then_inc(sh_down, 1)

            for t in range(TT - 1):
                shared_down(t)
            pe.wait_ge(units_ready, 1)
            nc.tensor.matmul(bank[7][0:1, 320:448], expert_u[:, 0:1], ident[:, :],
                             start=True, stop=True).then_inc(units_row, 1)
            for t in range(TT):
                for k in range(TOP_K):
                    j = TOP_K * t + k
                    n = hots_before(j, by_pool(j))
                    if by_pool(j):
                        pe.wait_ge(hot_pool, n + 1)
                        slots, places = slot_hot_p[:, n % 2, :], unit_hot_p[:, n % 2, :]
                    else:
                        pe.wait_ge(hot_ready, n + 1)
                        slots, places = slot_hot[:, n % 4, :], unit_hot[:, n % 4, :]
                    nc.tensor.matmul(bank[6][:, 0:5 * UNITS], slots, places,
                                     start=(j == 0), stop=(j == TT * TOP_K - 1)).then_inc(list_mm, 1)
            shared_down(TT - 1)

            xe_banks = (bank[1], bank[2])

            def tokensT(n, u, i):
                pe.wait_ge(gather_in[u], 16 * (i + 1))
                for half in range(2):
                    for k in range(4):
                        last = nc.tensor.transpose(xe_banks[half][:, k * P:(k + 1) * P],
                                                   gathered[u][:, (4 * half + k) * P:(4 * half + k + 1) * P],
                                                   ident[:, :])
                last.then_inc(xe_tr, 1)

            def look_up(n):
                return (pe.value_load(unit_expert[0:1, bass.ds(n, 1)], min_val=1, max_val=E),
                        pe.value_load(unit_at[0:1, bass.ds(n, 1)], min_val=0, max_val=(RING - 1) * 2 * D))

            def gate_up(n, u, looked_up=None):
                experts, at = looked_up or look_up(n)
                pe.wait_ge(weights_ready, experts)
                pe.wait_ge(xe_act, n + 1)
                pe.wait_ge(xe_dve, n + 1)
                settle(pe)
                for k in range(KD):
                    last = nc.tensor.matmul(bank[0][:, :], gatheredT[u][:, k, :],
                                            ring_flat[:, bass.ds(at * 2 + k * 2 * F, 2 * F)],
                                            start=(k == 0), stop=(k == KD - 1))
                last.then_inc(gu_done, 1)

            def act_T(n):
                pe.wait_ge(act_done, n + 1)
                for f in range(2):
                    last = nc.tensor.transpose(bank[3][:, f * P:(f + 1) * P], e_act[:, f * P:(f + 1) * P], ident[:, :])
                last.then_inc(at_tr, 1)

            def down_mm(n, used, ahead=None):
                looked_up = None
                at = pe.value_load(unit_at[0:1, bass.ds(n, 1)], min_val=0, max_val=(RING - 1) * 2 * D)
                pe.wait_ge(at_ready, n + 1)
                if used:
                    pe.wait_ge(y_act, n)
                    pe.wait_ge(y_dve, n)
                settle(pe)
                for c in range(2):
                    for f in range(2):
                        last = nc.tensor.matmul(bank[4 + c][:, :], e_actT[:, f, :],
                                                down_flat[:, bass.ds(at + f * D + c * 512, 512)],
                                                start=(f == 0), stop=(f == 1))
                    if c == 0 and ahead is not None:
                        looked_up = look_up(ahead)
                last.then_inc(down_done, 1)
                return looked_up

            pe.wait_ge(tables_ready, 1)
            tokensT(0, 0, 0)
            gate_up(0, 0)
            tokensT(1, 1, 0)
            act_T(0)
            gate_up(1, 1)
            tokensT(2, 0, 1)
            pe.wait_ge(sh_y_ready, 2 * TT)
            down_mm(0, False)
            act_T(1)
            pairs = pe.value_load(expert_end[0:1, E:E + 1], min_val=E // 2, max_val=UNITS // 2 - 1)
            with pe.Fori(1, pairs) as i:
                gate_up(2 * i, 0)
                tokensT(2 * i + 1, 1, i)
                looked_up = down_mm(2 * i - 1, True, ahead=2 * i + 1)
                act_T(2 * i)
                gate_up(2 * i + 1, 1, looked_up)
                tokensT(2 * i + 2, 0, i + 1)
                down_mm(2 * i, True)
                act_T(2 * i + 1)
            down_mm(pe.value_load(expert_end[0:1, E + 1:E + 2], min_val=E - 1, max_val=UNITS - 1), True)

        @block.gpsimd
        def _(pool):
            steps = [0]

            def link(ins):
                steps[0] += 1
                ins.then_inc(pool_step, 1)
                pool.wait_ge(pool_step, steps[0])

            pool.dma_start(table_b[0:97, 0:NDIST], a["buckets"]).then_inc(buckets_in, 16)

            link(nc.gpsimd.memset(ident[:, :], 0.0))
            nc.gpsimd.affine_select(out=ident[:, :], in_=ident[:, :], compare_op=ALU.not_equal, fill=1.0, base=0,
                                    pattern=[[-1, P]], channel_multiplier=1).then_inc(ident_set, 1)
            link(nc.gpsimd.memset(ident_b[:, :], 0.0))
            nc.gpsimd.affine_select(out=ident_b[:, :], in_=ident_b[:, :], compare_op=ALU.not_equal, fill=1.0,
                                    base=0, pattern=[[-1, P]], channel_multiplier=1).then_inc(ident_set, 1)
            nc.gpsimd.memset(ones_b[:, :], 1.0)
            link(nc.gpsimd.memset(causal_b[:, :], 0.0))
            nc.gpsimd.affine_select(out=causal_b[:, :], in_=causal_b[:, :], compare_op=ALU.is_ge, fill=NEG, base=0,
                                    pattern=[[-1, P]], channel_multiplier=1)
            link(nc.gpsimd.memset(before_b[:, :], 0.0))
            nc.gpsimd.affine_select(out=before_b[:, :], in_=before_b[:, :], compare_op=ALU.is_ge, fill=1.0, base=0,
                                    pattern=[[-1, P]], channel_multiplier=1)
            nc.gpsimd.iota(row_no[:, :], pattern=[[0, 1]], base=0, channel_multiplier=1,
                           allow_small_or_imprecise_dtypes=True)
            nc.gpsimd.iota(iota_b[:, :], pattern=[[1, SLOTS]], base=0, channel_multiplier=0,
                           allow_small_or_imprecise_dtypes=True)
            link(nc.gpsimd.memset(tri, 1.0))
            link(nc.gpsimd.affine_select(out=tri, in_=tri, compare_op=ALU.is_ge, fill=0.0, base=0,
                                         pattern=[[1, S]], channel_multiplier=-1))
            nc.gpsimd.memset(down[:, 1, :], 0.0)
            nc.gpsimd.memset(p_cmp[:, :, :], 0.0).then_inc(masks_set, 1)

            for s in range(2):
                j = 14 + s
                pool.wait_ge(*copied(j))
                for half in range(2):
                    for g in range(G):
                        n = S - half
                        pool.dma_start(pair[s][half * DH:(half + 1) * DH, g, 0:n],
                                       kvT[g * DH:(g + 1) * DH, 2 + s, half:S]).then_inc(pair_in[s], 16)

            for s in range(2):
                pool.wait_ge(pair_in[s], 64)
            nc.gpsimd.memset(kvT[0:DH, 2:4, :], 0.0)
            link(nc.gpsimd.tensor_copy(kvT[DH:P, 2:4, :], kvT[DH:P, 0:2, :]))
            nc.gpsimd.memset(kvT[DH:P, 0:2, :], 0.0).then_inc(k_padded, 1)
            pool.wait_ge(xb_ready, 2)
            nc.gpsimd.memset(fk_odd[0:DH, :, :], 0.0)
            link(nc.gpsimd.tensor_copy(fk_odd[DH:P, :, :], fkT[DH:P, :, :]))
            nc.gpsimd.memset(fkT[DH:P, :, :], 0.0).then_inc(k_padded, 1)

            for i, part in enumerate((fox_split[:, 0:S], fox_split[:, S:2 * S], fox_lo)):
                pool.wait_ge(parts_ready, i + 1)
                pool.dma_start(fox_parts[i:i + 1, :, :], part).then_inc(parts_in, 16)

            pool.wait_ge(cmp_p, 2)
            for t in range(FIRST_NSA, NT):
                kind, h, qt = TASKS[t]
                pool.wait_ge(inv_ready, t + 1)
                probs = p_buf[t % 4][:, 0:P * (qt + 1)]
                gi = 3 * h + (1 if kind == "sel" else 2)
                nc.gpsimd.tensor_scalar(probs, probs, inv_sum[:, t % 4:t % 4 + 1], gates[:, qt, gi:gi + 1],
                                        ALU.mult, ALU.mult).then_inc(p_scaled, 1)

            pool.wait_ge(ln_in, 16)
            pool.wait_ge(ada_out, 8)
            link(nc.gpsimd.tensor_tensor(ln_tmp, ln_rows[:, 1, :], mod_rows[:, 2, :], ALU.mult))
            nc.gpsimd.tensor_tensor(mod_rows[:, 1, :], mod_rows[:, 1, :], ln_tmp, ALU.add).then_inc(rows_ready, 1)
            nc.gpsimd.tensor_tensor(mod_rows[:, 2, :], mod_rows[:, 2, :], ln_rows[:, 0, :], ALU.mult)\
                .then_inc(rows_ready, 1)
            for t in range(TT):
                pool.wait_ge(h2_ready, t + 1)
                link(nc.gpsimd.tensor_tensor(x_tok[:, t, :], x_tok[:, t, :], ln_rows[:, 0, :], ALU.mult))
                nc.gpsimd.tensor_tensor(x_tok[:, t, :], x_tok[:, t, :], ln_rows[:, 1, :], ALU.add).then_inc(x1_ready, 1)

            pool.wait_ge(x1_ready, TT)
            nc.gpsimd.memset(area_e[:, 0:2048], 0.0).then_inc(cleared, 1)
            pool.wait_ge(cleared, 1)
            pool.dma_start(ffn_dram[1].rearrange("(p t) d -> p t d", p=P),
                           area_e[:, 0:1024].rearrange("p (o d) -> p o d", o=1).to_broadcast([P, TT, D]))\
                .then_inc(scattered[1], 16)
            pool.wait_ge(scattered[1], 16)
            pool.wait_ge(h2_stored, 16 * TT)
            last_token = pool.to_reg(S - 1)

            pool.wait_ge(sel_ready, 1)
            for t in range(TT):
                nc.gpsimd.memset(payload[:, t, :, 1], t * P - OUT_OF_RANGE)
            nc.gpsimd.tensor_copy(payload[:, :, :, 0],
                                  row_no[:, :].rearrange("p (a b) -> p a b", a=1).to_broadcast([P, TT, TOP_K]))\
                .then_inc(payload_ready, 1)
            pool.wait_ge(payload_ready, 2)
            for j in range(TT * TOP_K):
                if by_pool(j):
                    n = hots_before(j, True)
                    if n >= 2:
                        pool.wait_ge(list_mm, j - 8 + 1)
                    if n >= 1:
                        pool.wait_ge(hot_pool, n)
                    t, k = j // TOP_K, j % TOP_K
                    nc.gpsimd.tensor_scalar(slot_hot_p[:, n % 2, :], iota_b[:, :], slot_k[:, t, k:k + 1], None,
                                            ALU.is_equal)
                    link(nc.gpsimd.tensor_scalar(unit_one_p, iota_b[:, 0:UNITS], unit_k[:, t, k:k + 1], None,
                                                 ALU.is_equal))
                    nc.gpsimd.tensor_tensor(unit_hot_p[:, n % 2, :].rearrange("p (c u) -> p c u", c=5),
                                            for_parts(unit_one_p), spread_payload(t, k), ALU.mult)\
                        .then_inc(hot_pool, 1)

            def gather(n, u):
                if not (isinstance(n, int) and n < 2):
                    pool.wait_ge(xe_tr, n - 1)
                    settle(pool)
                nc.gpsimd.tensor_copy(idx_gather[u][:, :], slot_idx[:, bass.ds(n, 1)]).then_inc(idx_set, 1)
                pool.wait_ge(idx_set, n + 1)
                settle(pool)
                pool.indirect_dma_start(gathered[u], None, h2_dram[:, :],
                                        bass.IndirectOffsetOnAxis(ap=idx_gather[u][:, :], axis=0),
                                        bounds_check=last_token, oob_is_err=False).then_inc(gather_in[u], 16)

            def scatter(n, u, i):
                pool.wait_ge(y_act, n + 1)
                pool.wait_ge(y_dve, n + 1)
                if not (isinstance(i, int) and i + u == 0):
                    pool.wait_ge(scattered[u], 16 * (i + u))
                settle(pool)
                nc.gpsimd.tensor_copy(idx_scatter[u][:, :], slot_idx[:, bass.ds(n, 1)]).then_inc(idx_out, 1)
                pool.wait_ge(idx_out, n + 1)
                settle(pool)
                pool.indirect_dma_start(ffn_dram[u][:, :],
                                        bass.IndirectOffsetOnAxis(ap=idx_scatter[u][:, :], axis=0),
                                        y_out[u], None, bounds_check=last_token, oob_is_err=False,
                                        compute_op=ALU.add).then_inc(scattered[u], 16)

            pool.wait_ge(lists_ready, 1)
            gather(0, 0)
            gather(1, 1)
            gather(2, 0)
            gather(3, 1)
            for stored_rows in ffn_started:
                pool.wait_ge(stored_rows, 8 * TT)
            scatter(0, 0, 0)
            pool.wait_ge(tables_ready, 1)
            pairs = pool.value_load(expert_end[0:1, E:E + 1], min_val=E // 2, max_val=UNITS // 2 - 1)
            with pool.Fori(1, pairs) as i:
                gather(2 * i + 2, 0)
                scatter(2 * i - 1, 1, i - 1)
                gather(2 * i + 3, 1)
                scatter(2 * i, 0, i)
            scatter(2 * pairs - 1, 1, pairs - 1)
            pool.wait_ge(gather_in[0], 16 * (pairs + 1))
            pool.wait_ge(gather_in[1], 16 * (pairs + 1))
            settle(pool)
            for t in range(2, TT):
                pool.wait_ge(ffn_in[t], 32)
                nc.gpsimd.tensor_tensor(ffn_tok[0][:, t, :], ffn_tok[0][:, t, :], ffn_tok[1][:, t, :], ALU.add)\
                    .then_inc(sums_added, 1)
            for t in range(TT - 1):
                pool.wait_ge(xg_ready, t + 1)
                nc.gpsimd.tensor_tensor(x_tok[:, t, :], x_tok[:, t, :], ln_rows[:, 3, :], ALU.add)\
                    .then_inc(x2_ready, 1)

        @block.vector
        def _(dve):
            steps = [0]

            def link(ins):
                steps[0] += 1
                ins.then_inc(dve_step, 1)
                dve.wait_ge(dve_step, steps[0])

            v = nc.vector
            dve.wait_ge(c_exp, 1)
            link(v.tensor_scalar(sc_col[:, 0, :], sc_col[:, 0, :], 1.0, None, ALU.add))
            link(v.reciprocal(sc_col[:, 1, :], sc_col[:, 0, :]))
            v.tensor_tensor(sc_col[:, 2, :], c_col[:, :], sc_col[:, 1, :], ALU.mult).then_inc(c_ready, 1)

            dve.wait_ge(table_in, 64)
            d0 = c_stat[0:96, 0, 0:H]
            d1 = c_stat[0:96, 1, 0:H]
            d2 = c_stat[0:96, 2, 0:H]
            hi = rel_parts[0:96, :]
            link(v.tensor_tensor(d0, d0, d1, ALU.subtract))
            link(v.tensor_copy(hi, d0))
            link(v.tensor_tensor(d1, d0, hi, ALU.subtract))
            link(v.tensor_copy(rel_parts[32:64, :], d1[32:64, :]))
            link(v.tensor_copy(rel_parts[64:96, :], d1[64:96, :]))
            link(v.tensor_tensor(d2[64:96, :], d1[64:96, :], rel_parts[64:96, :], ALU.subtract))
            link(v.tensor_copy(rel_parts[64:96, :], d2[64:96, :]))
            v.memset(rel_parts[96:97, :], NEG).then_inc(rel_set, 1)

            def ada_chunk(c):
                i = AT["ada", c]
                dve.wait_ge(slot_in[i % RING], 16 * (i // RING + 1))
                if c >= 2:
                    dve.wait_ge(ada_mm, c - 1)
                w = ring[:, i % RING, :].rearrange("p (k n) -> p k n", k=KD)
                total = ada_sum[c % 2]
                link(v.tensor_scalar(total, w[:, 0, :], sc_col[:, 2, 0:1], None, ALU.mult))
                for k in range(1, KD):
                    step = v.scalar_tensor_tensor(total, w[:, k, :], sc_col[:, 2, k:k + 1], total, ALU.mult, ALU.add)
                    if k < KD - 1:
                        link(step)
                step.then_inc(ada_part, 1)

            dve.wait_ge(c_ready, 1)
            ada_chunk(0)
            ada_chunk(1)
            ada_chunk(2)
            ada_chunk(3)

            dve.wait_ge(ada_mm, 4)
            dve.wait_ge(consts_in, 80)
            link(v.tensor_tensor(mod_col[:, :], bank[0][:, 0:16], ada_b_col[:, :], ALU.add))
            v.tensor_scalar(mod_col[:, 8:16], mod_col[:, 8:16], 1.0, None, ALU.add).then_inc(mod_ready, 1)
            dve.wait_ge(mod_ready, 1)
            dve.wait_ge(xT_in, 16)
            for k in range(0, KD, 2):
                v.tensor_scalar(h1T[:, k, :], h1T[:, k, :], mod_col[:, 8 + k:9 + k], mod_col[:, k:k + 1],
                                ALU.mult, ALU.add).then_inc(h1_dve, 1)

            def ada_rows(c):
                dve.wait_ge(ada_mm, 4 + c + 1)
                if c == 0:
                    dve.wait_ge(modb_in, 16)
                dst = mod_rows[:, c // 2, (c % 2) * 512:(c % 2) * 512 + 512]
                v.scalar_tensor_tensor(dst, row_bank(c)[:, :], 1.0 if c // 2 == 2 else 0.0, dst,
                                       ALU.add, ALU.add).then_inc(ada_out, 1)

            for j in range(1, 16, 2):
                dve.wait_ge(job_mm, j + 1)
                dst = [fqT, fkT, nqT, kvT][j // 4][:, j % 4, :]
                v.tensor_scalar(dst, bank[j % 4][:, :], SCALE if j // 4 in (0, 2) else 1.0, None, ALU.mult)\
                    .then_inc(job_dve, 1)
                if j == 3:
                    ada_chunk(4)
                if j == 7:
                    ada_rows(0)
                    ada_chunk(5)
                if j == 11:
                    ada_rows(1)
                    ada_chunk(6)
                if j == 15:
                    ada_chunk(7)
                    ada_chunk(8)

            def build_xb(s):
                dve.wait_ge(pair_in[s], 64)
                dve.wait_ge(masks_set, 1)
                dst = xb[s].rearrange("p (j m) -> p j m", j=16)[:, :, 0:G * NCMP].rearrange("p j (g n) -> p j g n", g=G)
                for g in range(G):
                    src = pair[s][:, g, :].rearrange("p (n j two) -> p j n two", j=8, two=2)
                    for part in range(2):
                        last = v.tensor_tensor(dst[:, 8 * part:8 * part + 8, g, :], src[:, :, part:part + NCMP, 0],
                                               pos2[:, s, 8 * part:8 * part + 8].rearrange("p (j o) -> p j o", o=1)
                                               .to_broadcast([P, 8, NCMP]), ALU.add)
                last.then_inc(xb_ready, 1)

            def copy_job(j):
                dve.wait_ge(job_mm, j + 1)
                if j < 20:
                    v.tensor_copy(ffng[:, j - 16, :], bank[j % 4][:, 256:288]).then_inc(ffng_act, 1)
                    v.tensor_copy(vsw[:, j - 16, :], bank[j % 4][:, 0:256]).then_inc(job_dve, 1)
                else:
                    v.tensor_copy(fv[:, j - 20, :], bank[j % 4][:, :]).then_inc(job_dve, 1)

            copy_job(17)
            build_xb(0)
            build_xb(1)
            copy_job(19)
            ada_rows(2)
            ada_rows(3)

            dve.wait_ge(ffng_act, TT)
            link(v.tensor_tensor(fx[:, 0, :, :], ffng[:, :, 0:H],
                                 bf_row[:, :].rearrange("p (o h) -> p o h", o=1).to_broadcast([P, TT, H]), ALU.add))
            link(v.tensor_scalar(fx[:, 2, :, :], fx[:, 0, :, :], -1.0, 0.0, ALU.mult, ALU.max))
            v.scalar_tensor_tensor(fx[:, 1, :, :], fx[:, 2, :, :], 2.0, fx[:, 0, :, :], ALU.mult, ALU.add)\
                .then_inc(fx_ready, 1)
            dve.wait_ge(fx_ready, 3)
            v.tensor_tensor(fx[:, 2, :, :], fx[:, 2, :, :], fx[:, 1, :, :], ALU.add).then_inc(fx_ready, 1)
            link(v.tensor_scalar(gates[:, :, :], gates[:, :, :], 1.0, None, ALU.add))
            link(v.reciprocal(gates[:, :, :], gates[:, :, :]))
            g0 = gates[:, 0, :].rearrange("p (h b) -> p h b", b=3)[:, :, 0]
            dve.wait_ge(ident_set, 1)
            link(v.tensor_reduce(early[:, :], ident[:, 31:P], AX, ALU.add))
            link(v.tensor_scalar(g0, g0, early[:, :], None, ALU.mult))

            dve.wait_ge(hid_exp, 1)
            link(v.tensor_scalar(hid_e, hid_e, 1.0, None, ALU.add))
            link(v.reciprocal(hid_e, hid_e))
            v.tensor_tensor(hid, bank[4][:, 0:256], hid_e, ALU.mult).then_inc(hid_ready, 1)

            dve.wait_ge(cum_mm, 1)
            link(v.tensor_copy(fox_sum, bank[5][0:H, :]))
            link(v.tensor_copy(fox_split[:, 0:S], fox_sum))
            v.tensor_tensor(fox_rest, fox_sum, fox_split[:, 0:S], ALU.subtract).then_inc(parts_ready, 1)
            dve.wait_ge(parts_ready, 1)
            link(v.tensor_copy(fox_split[:, S:2 * S], fox_rest))
            v.tensor_tensor(fox_rest, fox_rest, fox_split[:, S:2 * S], ALU.subtract).then_inc(parts_ready, 1)
            dve.wait_ge(parts_ready, 2)
            v.tensor_copy(fox_lo, fox_rest).then_inc(parts_ready, 1)

            ada_chunk(9)
            ada_rows(4)
            dve.wait_ge(hidT_mm, 1)
            v.tensor_copy(hidT, bank[4][:, 256:512].rearrange("p (f m) -> p f m", f=2)).then_inc(hidT_ready, 1)
            copy_job(21)
            ada_chunk(10)
            link(v.memset(kc2[:, :], 0.0))
            dve.wait_ge(kc_mm, 1)
            for g in range(G):
                last = v.tensor_copy(kc2[g * DH:(g + 1) * DH, 32 * g:32 * g + NCMP],
                                     bank[4][g * DH:(g + 1) * DH, 0:NCMP])
            last.then_inc(kc_ready, 1)
            ada_rows(5)
            ada_chunk(11)
            dve.wait_ge(cmp_qk, 1)
            s0 = c_stat[:, 0, :]
            s1 = c_stat[:, 1, :]

            def spread(st):
                return st.rearrange("p (m o) -> p m o", o=1).to_broadcast([P, 16, NCMP])

            for i in range(2):
                probs = p_cmp[:, i, :].rearrange("p (m n) -> p m n", m=16)[:, :, 0:NCMP]
                for g in range(G):
                    logits = bank[6 + i][:, 256 * g:256 * g + 256].rearrange("p (t r n) -> p t r n", t=2, r=R)
                    sums = p_cmp[:, i, 256 * g:256 * g + 256].rearrange("p (t r n) -> p t r n", t=2, r=R)
                    last = v.tensor_tensor(sums[:, :, :, 0:NCMP], logits[:, :, :, 0:NCMP],
                                           bias_c[:, 2 * i:2 * i + 2, g * R:(g + 1) * R, 0:NCMP], ALU.add)
                link(last)
                link(v.tensor_reduce(s0, probs, AX, ALU.max))
                v.tensor_tensor(probs, probs, spread(s0), ALU.subtract).then_inc(cmp_max, 1)
                dve.wait_ge(cmp_max, i + 1)
            link(v.memset(vc_diag, 0.0))
            for r in range(R):
                last = v.tensor_copy(vc_diag[32 * r:32 * r + NCMP, :, r * DH:(r + 1) * DH],
                                     bank[4][32 * r:32 * r + NCMP, 64:64 + 2 * DH].rearrange("p (g d) -> p g d", g=G))
            last.then_inc(vc_ready, 1)
            ada_rows(6)
            copy_job(23)
            for i in range(2):
                probs = p_cmp[:, i, :].rearrange("p (m n) -> p m n", m=16)[:, :, 0:NCMP]
                dve.wait_ge(cmp_exp, i + 1)
                link(v.tensor_reduce(s0, probs, AX, ALU.add))
                link(v.reciprocal(s1, s0))
                for g in range(G):
                    gate = gates[:, 2 * i:2 * i + 2, :].rearrange("p t (h b) -> p t h b", b=3)[:, :, g * R:(g + 1) * R, 0]
                    sg = s1[:, 8 * g:8 * g + 8].rearrange("p (t r) -> p t r", t=2)
                    last = v.tensor_tensor(sg, sg, gate, ALU.mult)
                link(last)
                v.tensor_tensor(probs, probs, spread(s1), ALU.mult).then_inc(cmp_p, 1)
                dve.wait_ge(cmp_p, i + 1)
            ada_rows(7)

            def max_task(t):
                kind, h, qt = TASKS[t]
                n = P * (qt + 1)
                b = bank[t % 4]
                dve.wait_ge(qk_done, t + 1)
                nm = nmax[:, t % 4:t % 4 + 1]
                if kind == "fox":
                    v.tensor_reduce(nm, b[:, 0:n], AX, ALU.max, negate=True).then_inc(max_done, 1)
                    return
                near = min(n, 256)
                link(v.tensor_tensor(b[:, n - near:n], b[:, n - near:n], bias_w[:, h, 256 - near:256], ALU.add))
                v.tensor_reduce(nm, b[:, 0:n], AX, ALU.max, negate=True).then_inc(max_done, 1)

            def copy_pT(t):
                n = P * (TASKS[t][2] + 1)
                dve.wait_ge(tr_done, t + 1)
                if t == 0:
                    dve.wait_ge(hid_mm, 1)
                if t >= 4:
                    dve.wait_ge(pv_done, (t - 4) // 2 + 1)
                v.tensor_copy(pT_buf[t % 4][:, 0:n], bank[4 + t % 2][:, 0:n]).then_inc(pT_dve, 1)

            def invert_sum(t):
                dve.wait_ge(exp_done, t + 1)
                if t >= 4:
                    dve.wait_ge(*scaled(t - 4))
                v.reciprocal(inv_sum[:, t % 4:t % 4 + 1], rowsum[:, t % 4:t % 4 + 1]).then_inc(inv_ready, 1)

            for t in range(NT + 7):
                if t < NT:
                    max_task(t)
                if 1 <= t <= NT:
                    invert_sum(t - 1)
                if 3 <= t < NT + 3 and t - 3 < FIRST_NSA:
                    copy_pT(t - 3)
                for u in range(H // 2, H):
                    if t == 2 * LAST_PAIR[u] + 6:
                        dve.wait_ge(pv_done, LAST_PAIR[u] + 1)
                        v.tensor_copy(oT[:, u, :], bank[6 + u % 2][:, :]).then_inc(o_dve, 1)

            def statistics(t, i):
                x = x_tok[:, t, :]
                for half in range(2):
                    last = v.bn_stats(ln_stats[:, 6 * half:6 * half + 6], x[:, 512 * half:512 * half + 512])
                link(last)
                link(v.bn_aggr(ln_mv[:, 2 * i:2 * i + 2], ln_stats[:, :]))
                v.tensor_scalar(ln_r[:, 2 * i:2 * i + 1], ln_mv[:, 2 * i + 1:2 * i + 2], EPS, None, ALU.add)\
                    .then_inc(var_ready, 1)

            dve.wait_ge(x_in, 16)
            dve.wait_ge(ln_in, 16)
            dve.wait_ge(rows_ready, 1)
            for t in range(TT):
                for c in range(2):
                    dve.wait_ge(mix_mm, 2 * t + c + 1)
                    last = v.tensor_tensor(ln_tmp[:, c * 512:(c + 1) * 512], bank[2 * (t % 2) + c][:, :],
                                           mod_rows[:, 0, c * 512:(c + 1) * 512], ALU.mult)
                    last.then_inc(mix_read, 1)
                dve.wait_ge(mix_read, 2 * t + 2)
                link(v.scalar_tensor_tensor(x_tok[:, t, :], x_tok[:, t, :], ALPHA, ln_tmp, ALU.mult, ALU.add))
                statistics(t, 0)
                dve.wait_ge(rstd_ready, t + 1)
                link(v.tensor_scalar(x_tok[:, t, :], x_tok[:, t, :], ln_mv[:, 0:1], ln_r[:, 1:2],
                                     ALU.subtract, ALU.mult))
                if t == 0:
                    dve.wait_ge(rows_ready, 2)
                link(v.tensor_tensor(h2_tok[t], x_tok[:, t, :], mod_rows[:, 2, :], ALU.mult))
                v.tensor_tensor(h2_tok[t], h2_tok[t], mod_rows[:, 1, :], ALU.add).then_inc(h2_ready, 1)

            def shared_act(t):
                dve.wait_ge(sh_silu, t + 1)
                v.tensor_tensor(sh_act[:, t, :], sh_sil[:, t, :], bank[t][:, F:2 * F], ALU.mult)\
                    .then_inc(sh_act_ready, 1)

            dve.wait_ge(h2_stored, 16 * TT)
            dve.wait_ge(h2T_mm, 2 * TT)
            dve.wait_ge(router_exp, 1)
            link(v.tensor_scalar(r_score, r_score, 1.0, None, ALU.add))
            link(v.reciprocal(r_score, r_score))
            link(v.tensor_tensor(r_bias, r_score,
                                 e_bias_row[:, :].rearrange("p (o e) -> p o e", o=1).to_broadcast([P, TT, E]), ALU.add))
            for t in range(TT):
                for g in range(EG):
                    last = v.max(r_top[:, t, g, :], r_bias[:, t, 8 * g:8 * g + 8])
            link(last)
            link(v.tensor_tensor(r_group, r_top[:, :, :, 0], r_top[:, :, :, 1], ALU.add))
            mine = r_group.rearrange("p t (g o) -> p t g o", o=1).to_broadcast([P, TT, EG, EG])
            other = r_group.rearrange("p t (o g) -> p t o g", o=1).to_broadcast([P, TT, EG, EG])
            link(v.tensor_tensor(r_gt, other, mine, ALU.is_gt))
            link(v.tensor_tensor(r_eq, other, mine, ALU.is_equal))
            for g in range(1, EG):
                last = v.tensor_tensor(r_gt[:, :, g, 0:g], r_gt[:, :, g, 0:g], r_eq[:, :, g, 0:g], ALU.add)
            link(last)
            link(v.tensor_reduce(r_rank, r_gt, AX, ALU.add))
            link(v.tensor_scalar(r_gmask, r_rank, TOPK_GROUPS - 0.5, None, ALU.is_lt))
            gm = r_gmask.rearrange("p t (g o) -> p t g o", o=1).to_broadcast([P, TT, EG, EG])
            mk = r_masked.rearrange("p t (g e) -> p t g e", g=EG)
            link(v.tensor_tensor(mk, r_bias.rearrange("p t (g e) -> p t g e", g=EG), gm, ALU.mult))
            link(v.tensor_scalar(r_rank, r_gmask, -1.0, -NEG, ALU.add, ALU.mult))
            link(v.tensor_tensor(mk, mk, r_rank.rearrange("p t (g o) -> p t g o", o=1).to_broadcast([P, TT, EG, EG]),
                                 ALU.add))
            for t in range(TT):
                last = v.max(r_best[:, t, :], r_masked[:, t, :])
            link(last)
            for t in range(TT):
                last = v.match_replace(r_sel[:, t, :], r_best[:, t, :], r_masked[:, t, :], 3e38)
            link(last)
            link(v.tensor_scalar(r_sel, r_sel, 2e38, None, ALU.is_gt))
            v.tensor_copy(r_selb, r_sel).then_inc(sel_ready, 1)
            link(v.tensor_tensor(r_gate, r_sel, r_score, ALU.mult))
            link(v.tensor_reduce(r_den, r_gate, AX, ALU.add))
            link(v.reciprocal(r_den, r_den))
            link(v.tensor_scalar(r_den, r_den, ROUTED_SCALE, None, ALU.mult))
            for t in range(TT):
                last = v.tensor_scalar(r_gate[:, t, :], r_gate[:, t, :], r_den[:, t:t + 1], None, ALU.mult)
            link(last)
            link(v.memset(zeros_e, 0.0))
            for t in range(TT):
                last = v.tensor_tensor_scan(r_kidx[:, t, :], r_sel[:, t, :], zeros_e, 0.0, ALU.add, ALU.add)
            link(last)
            link(v.tensor_tensor(r_kidx, r_kidx, r_sel, ALU.mult))
            for t in range(TT):
                shared_act(t)
            dve.wait_ge(pos_mm, 1)
            count = bank[7][:, TT * E:(TT + 1) * E]
            link(v.tensor_scalar(n_units, count, SLOTS + 0.5, 1.0, ALU.is_gt, ALU.add))
            for i in range(2, TT):
                link(v.scalar_tensor_tensor(n_units, count, i * SLOTS + 0.5, n_units, ALU.is_gt, ALU.add))
            link(v.tensor_tensor_scan(unit_end, n_units, zeros_e, 0.0, ALU.add, ALU.add))
            link(v.tensor_tensor(n_units, unit_end, n_units, ALU.subtract))
            first = n_units.rearrange("p (o e) -> p o e", o=1).to_broadcast([P, TT, E])
            link(v.scalar_tensor_tensor(pos_m, first, float(SLOTS), bank[7][:, 0:TT * E].rearrange("p (t e) -> p t e", t=TT),
                                        ALU.mult, ALU.add))
            link(v.tensor_scalar(zeros_e, unit_end, row_no[:, :], None, ALU.is_le))
            link(v.tensor_reduce(expert_u[:, 1:2], zeros_e, AX, ALU.add))
            v.tensor_scalar(expert_u[:, 0:1], expert_u[:, 1:2], E - 1.0, None, ALU.min).then_inc(units_ready, 1)
            for k in range(TOP_K):
                v.scalar_tensor_tensor(r_pick[0], r_kidx, k + 1.0, pos_m, ALU.is_equal, ALU.mult)
                link(v.scalar_tensor_tensor(r_pick[1], r_kidx, k + 1.0, r_gate, ALU.is_equal, ALU.mult))
                v.tensor_reduce(slot_k[:, :, k], r_pick[0], AX, ALU.add)
                link(v.tensor_reduce(gate_k[:, :, k], r_pick[1], AX, ALU.add))
            link(v.tensor_copy(slot_ki, slot_k))
            link(v.tensor_scalar(unit_ki, slot_ki, SLOT_BITS, None, ALU.arith_shift_right))
            v.tensor_copy(unit_k, unit_ki)
            link(v.tensor_scalar(slot_ki, slot_ki, SLOTS - 1, None, ALU.bitwise_and))
            v.tensor_copy(slot_k, slot_ki)
            for i in range(2):
                link(v.tensor_copy(gate_b, gate_k))
                link(v.tensor_copy(payload[:, :, :, 2 + i], gate_b))
                link(v.tensor_tensor(gate_k, gate_k, payload[:, :, :, 2 + i], ALU.subtract))
            v.tensor_copy(payload[:, :, :, 4], gate_k).then_inc(payload_ready, 1)
            dve.wait_ge(payload_ready, 2)
            for t in range(TT):
                for k in range(TOP_K):
                    j = TOP_K * t + k
                    if by_pool(j):
                        continue
                    n = hots_before(j, False)
                    if n >= 4:
                        dve.wait_ge(list_mm, next(i for i in range(j) if not by_pool(i) and
                                                  hots_before(i, False) == n - 4) + 1)
                    v.tensor_scalar(slot_hot[:, n % 4, :], iota_b[:, :], slot_k[:, t, k:k + 1], None, ALU.is_equal)
                    v.scalar_tensor_tensor(unit_hot[:, n % 4, :].rearrange("p (c u) -> p c u", c=5),
                                           for_parts(iota_b[:, 0:UNITS]), unit_k[:, t, k:k + 1], spread_payload(t, k),
                                           ALU.is_equal, ALU.mult).then_inc(hot_ready, 1)
                if t == 0:
                    dve.wait_ge(units_row, 1)
                    row = bank[7][0:1, 320:448]
                    v.tensor_scalar(unit_expert, row, 1.0, None, ALU.add)
                    link(v.tensor_scalar(unit_at, row, float(len(CHUNKS)), None, ALU.add))
                    v.tensor_scalar(unit_at, unit_at, RING - 1, DOWN_BITS, ALU.bitwise_and, ALU.logical_shift_left)
                    v.tensor_copy(expert_end[:, 0:E], unit_end[0:1, :])
                    link(v.tensor_scalar(expert_end[:, E:E + 1], unit_end[0:1, E - 1:E], 1.0, None, ALU.add))
                    link(v.tensor_scalar(expert_end[:, E:E + 1], expert_end[:, E:E + 1], 1, None,
                                         ALU.arith_shift_right))
                    v.tensor_scalar(expert_end[:, E + 1:E + 2], expert_end[:, E:E + 1], 2.0, -1.0,
                                    ALU.mult, ALU.add).then_inc(tables_ready, 1)
            dve.wait_ge(list_mm, TT * TOP_K)
            dve.wait_ge(scattered[1], 16)
            link(v.tensor_copy(list_sum, bank[6][:, 0:5 * UNITS]))
            sums = [list_sum[:, c * UNITS:(c + 1) * UNITS] for c in range(5)]
            link(v.tensor_tensor(sums[2], sums[2], sums[3], ALU.add))
            v.tensor_tensor(slot_gate[:, :], sums[2], sums[4], ALU.add)
            v.scalar_tensor_tensor(slot_idx[:, :], sums[0], OUT_OF_RANGE, sums[1], ALU.add, ALU.add)\
                .then_inc(lists_ready, 1)

            def copy_xT(n, u):
                dve.wait_ge(xe_tr, n + 1)
                v.tensor_copy(gatheredT[u % 2][:, 4:8, :], bank[2][:, :].rearrange("p (k m) -> p k m", k=4))\
                    .then_inc(xe_dve, 1)

            def copy_y(n, u, i):
                dve.wait_ge(down_done, n + 1)
                if isinstance(i, int) and i == 0:
                    for stored_rows in ffn_started:
                        dve.wait_ge(stored_rows, 8 * TT)
                else:
                    dve.wait_ge(scattered[u], 16 * (i + u))
                v.tensor_copy(y_out[u][:, 512:1024], bank[5][:, :]).then_inc(y_dve, 1)

            def activation(n):
                dve.wait_ge(silu_done, n + 1)
                settle(dve)
                v.scalar_tensor_tensor(e_act, bank[0][:, F:2 * F], slot_gate[:, bass.ds(n, 1)], silu_g,
                                       ALU.mult, ALU.mult).then_inc(act_done, 1)

            def copy_aT(n):
                dve.wait_ge(at_tr, n + 1)
                v.tensor_copy(e_actT, bank[3][:, 0:F].rearrange("p (i f) -> p i f", i=2)).then_inc(at_ready, 1)

            copy_xT(0, 0)
            activation(0)
            copy_xT(1, 1)
            copy_aT(0)
            activation(1)
            copy_xT(2, 0)
            copy_y(0, 0, 0)
            copy_aT(1)
            dve.wait_ge(tables_ready, 1)
            pairs = dve.value_load(expert_end[0:1, E:E + 1], min_val=E // 2, max_val=UNITS // 2 - 1)
            with dve.Fori(1, pairs) as i:
                activation(2 * i)
                copy_xT(2 * i + 1, 1)
                copy_y(2 * i - 1, 1, i - 1)
                copy_aT(2 * i)
                activation(2 * i + 1)
                copy_xT(2 * i + 2, 0)
                copy_y(2 * i, 0, i)
                copy_aT(2 * i + 1)
            copy_y(2 * pairs - 1, 1, pairs - 1)

            def scale_rows(t):
                dve.wait_ge(xn_ready, t + 1)
                step = v.tensor_tensor(x_tok[:, t, :], x_tok[:, t, :], ln_rows[:, 2, :], ALU.mult)
                if t < TT - 1:
                    step.then_inc(xg_ready, 1)
                else:
                    link(step)
                    v.tensor_tensor(x_tok[:, t, :], x_tok[:, t, :], ln_rows[:, 3, :], ALU.add).then_inc(x2_last, 1)

            for t in range(TT):
                dve.wait_ge(ffn_in[t], 32)
                y = ffn_tok[0][:, t, :]
                if t < 2:
                    link(v.tensor_tensor(y, y, ffn_tok[1][:, t, :], ALU.add))
                else:
                    dve.wait_ge(sums_added, t - 1)
                link(v.tensor_tensor(y, y, mod_rows[:, 3, :], ALU.mult))
                link(v.scalar_tensor_tensor(x_tok[:, t, :], x_tok[:, t, :], ALPHA, y, ALU.mult, ALU.add))
                statistics(t, t % 2)
                if t >= 1:
                    scale_rows(t - 1)
            scale_rows(TT - 1)


def bucket_table(np):
    dist = np.arange(NDIST) - DIST0
    n = np.maximum(dist, 0)
    exact = NB // 2
    nf = np.maximum(n, 1).astype(np.float32)
    large = exact + (np.log(nf / np.float32(exact)) / np.float32(np.log(128 / exact)) * (NB - exact)).astype(np.int32)
    bucket = np.where(n < exact, n, np.minimum(large, NB - 1))
    table = np.zeros((97, NDIST), np.float32)
    for part in range(3):
        table[NB * part + bucket[dist >= 0], np.nonzero(dist >= 0)[0]] = 1.0
    table[96, dist < 0] = 1.0
    return table


def kernel(x, c, w_ada, b_ada, w_in, b_f, cmp_pos_k, cmp_w1_k, cmp_w2_k, cmp_pos_v, cmp_w1_v, cmp_w2_v,
           rel_bias, w_out, ln1_g, ln1_b, w_router, e_bias, w_gate, w_up, w_down,
           ws_gate, ws_up, ws_down, ln2_g, ln2_b):
    import numpy as np
    import concourse.bacc as bacc
    from concourse.bass_utils import run_bass_kernel_spmd

    def rows(w):
        w = np.asarray(w)
        return np.ascontiguousarray(w.reshape(w.shape[0] // P, P, w.shape[1]).transpose(1, 0, 2))

    def chunks(w):
        w = np.asarray(w)
        n = w.shape[1] // CW
        return np.ascontiguousarray(w.reshape(KD, P, n, CW).transpose(2, 1, 0, 3)).reshape(n, P, KD * CW)

    xs = np.asarray(x)[0]
    widths = (512, 512, 512, 8, 512, 128, 128, 128, 128, 128, 128, 24)
    at = np.cumsum((0,) + widths)
    fq, fk, fv, ff, nq, kc, vc, ksl, vsl, kwn, vwn, ng = (np.asarray(w_in)[0][:, at[i]:at[i + 1]] for i in range(12))
    nq = nq.reshape(D, G, R, DH).transpose(0, 2, 1, 3).reshape(D, 512)
    wg, wu, wd = np.asarray(w_gate)[0], np.asarray(w_up)[0], np.asarray(w_down)[0]
    gu = np.empty((E, P, KD, 2, F), np.float32)
    gu[:, :, :, 0] = wg.reshape(E, KD, P, F).transpose(0, 2, 1, 3)
    gu[:, :, :, 1] = wu.reshape(E, KD, P, F).transpose(0, 2, 1, 3)
    ba = np.asarray(b_ada)[0]
    pos = np.stack([np.asarray(p)[0].reshape(16, P).T for p in (cmp_pos_k, cmp_pos_v)], axis=1)
    arrays = {
        "xT": rows(xs.T).reshape(P, KD * S),
        "x_tok": np.ascontiguousarray(xs.reshape(TT, P, D).transpose(1, 0, 2)),
        "c_col": np.ascontiguousarray(np.asarray(c)[0].reshape(KD, P).T),
        "w_ada": chunks(np.asarray(w_ada)[0]),
        "ada_b_col": np.ascontiguousarray(ba[0:2 * D].reshape(16, P).T),
        "ada_b_row": np.ascontiguousarray(ba[2 * D:].reshape(1, 4 * D)),
        "w_in": chunks(np.concatenate([fq, fk, nq, ksl, kwn, kc, vc, fv], axis=1)),
        "w_small": rows(np.concatenate([vsl, vwn, ff, ng], axis=1)).reshape(P, KD * WS_SMALL),
        "b_f": np.asarray(b_f).reshape(1, H),
        "w_cmp1": np.stack([rows(np.asarray(w)[0]).reshape(P, 16 * CMPH) for w in (cmp_w1_k, cmp_w1_v)]),
        "w_cmp2": np.stack([rows(np.asarray(w)[0]) for w in (cmp_w2_k, cmp_w2_v)], axis=1),
        "cmp_pos": np.ascontiguousarray(pos),
        "rel_bias": np.asarray(rel_bias),
        "buckets": bucket_table(np),
        "w_out": chunks(np.asarray(w_out)[0]),
        "ln_rows": np.concatenate([np.asarray(r)[0] for r in (ln1_g, ln1_b, ln2_g, ln2_b)]).reshape(1, 4 * D),
        "w_router": rows(np.asarray(w_router)[0]),
        "e_bias": np.asarray(e_bias).reshape(1, E),
        "w_gu": gu.reshape(E, P, KD * 2 * F),
        "w_d": np.ascontiguousarray(wd.reshape(E, 2, P, D).transpose(0, 2, 1, 3)).reshape(E, P, 2 * D),
        "ws_gu": chunks(np.concatenate([np.asarray(ws_gate)[0], np.asarray(ws_up)[0]], axis=1)),
        "ws_d": rows(np.asarray(ws_down)[0]).reshape(P, 2 * D),
    }
    nc = bacc.Bacc("TRN2", target_bir_lowering=False, num_devices=1)
    ins = {n: nc.dram_tensor(f"in_{n}", v.shape, F32, kind="ExternalInput").ap() for n, v in arrays.items()}
    out = nc.dram_tensor("out_x", (S, D), F32, kind="ExternalOutput").ap()
    build(nc, ins, out)
    r = run_bass_kernel_spmd(nc, [{f"in_{n}": v for n, v in arrays.items()}], core_ids=[0])
    return r.results[0]["out_x"].reshape(1, S, D)
```
